# Optimizing a Trainium2 kernel written in Bass

```python
import math
import jax, jax.numpy as jnp
from jax import lax
import numpy as np

D_MODEL = 1024
BATCH = 1
SEQ = 512
DEPTH = 1
DEC_BATCH = 8
DEC_SEQ = 4
PAST_LEN = 4096
PAGE_SIZE = 128

MIX_WIDTH = D_MODEL
HGRN_WIDTH = MIX_WIDTH // 2
HGRN_HEADS = 4
HGRN_HEAD_DIM = HGRN_WIDTH // HGRN_HEADS
HGRN_KEY_DIM = 128
HGRN_KEY_WIDTH = HGRN_HEADS * HGRN_KEY_DIM
CONV_DIM = MIX_WIDTH - HGRN_WIDTH
CONV_GROUPS = 8
CONV_K = 3
IN_SIZES = [HGRN_KEY_WIDTH, HGRN_KEY_WIDTH, HGRN_WIDTH, HGRN_WIDTH,
            CONV_DIM, CONV_DIM, CONV_DIM]
N_IN = sum(IN_SIZES)
N_EXPERTS = 16
N_EXPERT_GROUPS = 4
EXPERTS_PER_GROUP = N_EXPERTS // N_EXPERT_GROUPS
TOP_K = 2
EXPERT_FF = 512
CHUNK = 64
ALPHA = (2 * DEPTH) ** 0.25
BETA = (8 * DEPTH) ** -0.25
LN_EPS = 1e-5
RMS_EPS = 1e-6

kernel_name = "hgrn2_shortconv_parallel_moe_decoder_step"

def layer_norm(x, g, b):
    xf = x.astype(jnp.float32)
    mu = jnp.mean(xf, axis=-1, keepdims=True)
    xc = xf - mu
    var = jnp.mean(xc * xc, axis=-1, keepdims=True)
    y = xc * lax.rsqrt(var + LN_EPS) * g.astype(jnp.float32) + b.astype(jnp.float32)
    return y.astype(x.dtype)

def group_rms(x, g, n_groups):
    shp = x.shape
    xf = x.astype(jnp.float32).reshape(shp[:-1] + (n_groups, shp[-1] // n_groups))
    xf = xf * lax.rsqrt(jnp.mean(xf * xf, axis=-1, keepdims=True) + RMS_EPS)
    return (xf.reshape(shp) * g.astype(jnp.float32)).astype(x.dtype)

def forget_lower_bounds(lower_bounds):
    lb = jnp.cumsum(jax.nn.softmax(lower_bounds.astype(jnp.float32), axis=0), axis=0)
    return lb - lb[0:1]

def hgrn_recurrence(q, k, v, logf, S0):
    B, T, H, dk = q.shape
    dv = v.shape[-1]
    C = math.gcd(T, CHUNK)
    n = T // C

    def to_chunks(a):
        return a.reshape(B, n, C, H, a.shape[-1]).transpose(1, 0, 3, 2, 4)

    causal = jnp.tril(jnp.ones((C, C), dtype=bool))[:, :, None]

    def step(S, inp):
        qc, kc, vc, gc = inp
        b = jnp.cumsum(gc, axis=2)
        o_inter = jnp.einsum('bhtk,bhkv->bhtv', qc * jnp.exp(b), S)
        diff = b[:, :, :, None, :] - b[:, :, None, :, :]
        decay = jnp.exp(jnp.where(causal, diff, -jnp.inf))
        att = jnp.einsum('bhtk,bhtsk,bhsk->bhts', qc, decay, kc)
        o = o_inter + jnp.einsum('bhts,bhsv->bhtv', att, vc)
        b_last = b[:, :, -1:, :]
        S_new = jnp.exp(b_last[:, :, 0, :])[..., None] * S + jnp.einsum(
            'bhsk,bhsv->bhkv', kc * jnp.exp(b_last - b), vc)
        return S_new, o

    S_fin, o = lax.scan(step, S0, (to_chunks(q), to_chunks(k), to_chunks(v), to_chunks(logf)))
    o = o.transpose(1, 0, 3, 2, 4).reshape(B, T, H, dv)
    return o, S_fin

def token_mixer(x, w_in, w_out, lb, hgrn_norm_g, conv_w, conv_norm_g, S0, conv_buf):
    B, T, _ = x.shape
    proj = x @ w_in
    q, fz, i, g, gb, gc, cx = jnp.split(proj, list(np.cumsum(IN_SIZES[:-1])), axis=-1)

    f32 = jnp.float32
    qh = jax.nn.silu(q.astype(f32)).reshape(B, T, HGRN_HEADS, HGRN_KEY_DIM)
    logf = jnp.logaddexp(jnp.log(lb), jnp.log1p(-lb) + jax.nn.log_sigmoid(fz.astype(f32)))
    logf = logf.reshape(B, T, HGRN_HEADS, HGRN_KEY_DIM)
    kh = -jnp.expm1(logf)
    vh = i.astype(f32).reshape(B, T, HGRN_HEADS, HGRN_HEAD_DIM)
    o, S_new = hgrn_recurrence(qh, kh, vh, logf, S0.astype(f32))
    o = group_rms(o.reshape(B, T, HGRN_WIDTH).astype(x.dtype), hgrn_norm_g, HGRN_HEADS)
    o = o * jax.nn.silu(g)

    u = gc * cx
    up = jnp.concatenate([conv_buf.astype(u.dtype), u], axis=1)
    y = sum(conv_w[j] * up[:, j:j + T] for j in range(CONV_K))
    yc = group_rms(gb * y, conv_norm_g, CONV_GROUPS)
    new_buf = up[:, T:]

    out = jnp.concatenate([o, yc.astype(o.dtype)], axis=-1) @ w_out
    return out, S_new, new_buf

def grouped_moe(x, w_router, router_bias, w_gate, w_up, w_down):
    B, T, D = x.shape
    xt = x.reshape(B * T, D)
    logits = (xt @ w_router).astype(jnp.float32) + router_bias.astype(jnp.float32)
    probs = jax.nn.softmax(logits, axis=-1)
    grp = probs.reshape(-1, N_EXPERT_GROUPS, EXPERTS_PER_GROUP)
    grp_score = lax.top_k(grp, TOP_K)[0].sum(-1)
    g_idx = lax.top_k(grp_score, 1)[1][:, 0]
    emask = jnp.repeat(jax.nn.one_hot(g_idx, N_EXPERT_GROUPS, dtype=jnp.bool_),
                       EXPERTS_PER_GROUP, axis=1)
    top_w, top_i = lax.top_k(jnp.where(emask, probs, -1.0), TOP_K)
    top_w = top_w / jnp.sum(top_w, axis=-1, keepdims=True)
    gates = jnp.sum(jax.nn.one_hot(top_i, N_EXPERTS, dtype=jnp.float32) * top_w[..., None], axis=1)
    gates = gates.astype(x.dtype)
    y = jnp.zeros_like(xt)
    for e in range(N_EXPERTS):
        h = jax.nn.silu(xt @ w_gate[e]) * (xt @ w_up[e])
        y = y + gates[:, e:e + 1] * (h @ w_down[e])
    return y.reshape(B, T, D)

def trunk(x, S_all, buf_all, w_in, w_out, lbs, hgrn_norm_g, conv_w, conv_norm_g,
          ln1_g, ln1_b, ln2_g, ln2_b, w_router, router_bias, w_gate, w_up, w_down):
    new_S, new_buf = [], []
    for l in range(DEPTH):
        m, S_l, b_l = token_mixer(x, w_in[l], w_out[l], lbs[l], hgrn_norm_g[l], conv_w[l],
                                  conv_norm_g[l], S_all[l], buf_all[l])
        x = layer_norm(ALPHA * x + m, ln1_g[l], ln1_b[l])
        x = layer_norm(ALPHA * x + grouped_moe(x, w_router, router_bias, w_gate[l], w_up[l], w_down[l]),
                       ln2_g[l], ln2_b[l])
        new_S.append(S_l)
        new_buf.append(b_l)
    return x, jnp.stack(new_S), jnp.stack(new_buf)

def setup_inputs(seed: int = 0) -> dict:
    key = jax.random.key(seed)
    ks = jax.random.split(key, 20)
    nrm = jax.random.normal
    f32 = jnp.float32
    return {
        "x_prompt": nrm(ks[0], (BATCH, SEQ, D_MODEL), f32),
        "x_sample": nrm(ks[1], (DEC_BATCH, DEC_SEQ, D_MODEL), f32),
        "state_hgrn": 0.5 * nrm(ks[2], (DEPTH, DEC_BATCH, HGRN_HEADS, HGRN_KEY_DIM, HGRN_HEAD_DIM), f32),
        "state_conv": nrm(ks[3], (DEPTH, DEC_BATCH, CONV_K - 1, CONV_DIM), f32),
        "w_in": nrm(ks[4], (DEPTH, D_MODEL, N_IN), f32) * D_MODEL ** -0.5,
        "w_out": nrm(ks[5], (DEPTH, MIX_WIDTH, D_MODEL), f32) * (MIX_WIDTH ** -0.5 * BETA),
        "lower_bounds": nrm(ks[6], (DEPTH, HGRN_KEY_WIDTH), f32),
        "hgrn_norm_g": 1.0 + 0.02 * nrm(ks[7], (DEPTH, HGRN_WIDTH), f32),
        "conv_w": nrm(ks[8], (DEPTH, CONV_K, CONV_DIM), f32) * CONV_K ** -0.5,
        "conv_norm_g": 1.0 + 0.02 * nrm(ks[9], (DEPTH, CONV_DIM), f32),
        "ln1_g": 1.0 + 0.02 * nrm(ks[10], (DEPTH, D_MODEL), f32),
        "ln1_b": 0.02 * nrm(ks[11], (DEPTH, D_MODEL), f32),
        "ln2_g": 1.0 + 0.02 * nrm(ks[12], (DEPTH, D_MODEL), f32),
        "ln2_b": 0.02 * nrm(ks[13], (DEPTH, D_MODEL), f32),
        "w_router": nrm(ks[14], (D_MODEL, N_EXPERTS), f32) * D_MODEL ** -0.5,
        "router_bias": 0.01 * nrm(ks[15], (N_EXPERTS,), f32),
        "w_gate": nrm(ks[16], (DEPTH, N_EXPERTS, D_MODEL, EXPERT_FF), f32) * D_MODEL ** -0.5,
        "w_up": nrm(ks[17], (DEPTH, N_EXPERTS, D_MODEL, EXPERT_FF), f32) * D_MODEL ** -0.5,
        "w_down": nrm(ks[18], (DEPTH, N_EXPERTS, EXPERT_FF, D_MODEL), f32) * (EXPERT_FF ** -0.5 * BETA),
    }

def reference(x_prompt, x_sample, state_hgrn, state_conv, w_in, w_out, lower_bounds, hgrn_norm_g,
              conv_w, conv_norm_g, ln1_g, ln1_b, ln2_g, ln2_b, w_router, router_bias,
              w_gate, w_up, w_down):
    lbs = forget_lower_bounds(lower_bounds)
    bp = x_prompt.shape[0]
    S0_prompt = jnp.zeros((DEPTH, bp, HGRN_HEADS, HGRN_KEY_DIM, HGRN_HEAD_DIM), jnp.float32)
    buf0_prompt = jnp.zeros((DEPTH, bp, CONV_K - 1, CONV_DIM), x_prompt.dtype)
    y_prompt, S_prompt, buf_prompt = trunk(
        x_prompt, S0_prompt, buf0_prompt, w_in, w_out, lbs, hgrn_norm_g, conv_w, conv_norm_g,
        ln1_g, ln1_b, ln2_g, ln2_b, w_router, router_bias, w_gate, w_up, w_down)
    y_sample, S_sample, buf_sample = trunk(
        x_sample, state_hgrn, state_conv, w_in, w_out, lbs, hgrn_norm_g, conv_w, conv_norm_g,
        ln1_g, ln1_b, ln2_g, ln2_b, w_router, router_bias, w_gate, w_up, w_down)
    return (y_prompt, y_sample, S_prompt, buf_prompt, S_sample, buf_sample)


_drawn_inputs = setup_inputs


def setup_inputs(seed=0):
    import zlib

    import numpy as np

    out = dict(_drawn_inputs(seed))
    spreads = {}
    factors = {'ln2_g': 8.329, 'ln2_b': 7.927, 'router_bias': 3.388, 'hgrn_norm_g': 4.1}
    for name, (base, spread) in spreads.items():
        noise = np.random.default_rng([zlib.crc32(name.encode()), seed]).standard_normal(out[name].shape)
        drawn = base * np.exp(spread * noise) if base else spread * noise
        out[name] = __import__('jax').numpy.asarray(drawn.astype(out[name].dtype))
    for name, factor in factors.items():
        out[name] = (out[name] * factor).astype(out[name].dtype)
    return out
```

```python
from contextlib import ExitStack

import numpy as np

import concourse.bass as bass
from concourse import mybir

F32 = mybir.dt.float32
F32R = mybir.dt.float32r
U8 = mybir.dt.uint8
I32 = mybir.dt.int32
U32 = mybir.dt.uint32
ALU = mybir.AluOpType
ACT = mybir.ActivationFunctionType
AX = mybir.AxisListType.X

P = 128
D = 1024
KT = D // P
SEQ, DB, DS = 512, 8, 4
NS = DB * DS
T = SEQ + NS
NTT = (T + P - 1) // P
H = 4
NC = SEQ // P
LEVELS = 7
SLEVELS = 2
CW = 256
N_IN = 3584
NCH = N_IN // CW
NWO = D // CW
UW = 2 + SEQ + DB * (2 + DS)
E, TOPG, FF = 16, 4, 512
NOV = 8
NBLK = E + NOV
ALPHA = float(2 ** 0.25)
LN_EPS, RMS_EPS = 1e-5, 1e-6

ORDER = [("f", 2), ("f", 3), ("q", 0), ("q", 1), ("v", 4), ("v", 5), ("gc", 10), ("gc", 11),
         ("cx", 12), ("cx", 13), ("gb", 8), ("gb", 9), ("g", 6), ("g", 7)]


def out_tiles():
    out = []
    for o, (kind, _) in enumerate(ORDER):
        out += [(kind, o, j) for j in range(NTT if kind == "v" else CW // P)]
    return out


TILES = out_tiles()
BY_DVE = ("cx", "gb")
FIRST_LEVEL_STEP = 6

C_ID, C_TRI, C_BLK, C_ONE, C_RST, C_SM = 0, 128, 256, 384, 512, 512 + T
C_N = C_SM + 80
SM_E16, SM_E128, SM_G4, SM_VAL, SM_SEQ, SM_IOTA = 0, 16, 32, 36, 41, 49


def constants():
    p = np.arange(P)
    c = np.zeros((P, C_N), np.float32)
    c[:, C_ID:C_ID + P] = np.eye(P)
    c[:, C_TRI:C_TRI + P] = p[:, None] < p[None, :]
    c[:, C_BLK:C_BLK + P] = (p[:, None] // 64) == (p[None, :] // 64)
    c[:, C_ONE:C_ONE + P] = 1.0
    t = np.arange(T)
    c[:, C_RST:C_RST + T] = np.where(t < SEQ, t % P != 0, (t - SEQ) % DS != 0)
    s = c[:, C_SM:]
    s[:, SM_E16:SM_E16 + E] = E - np.arange(E)
    s[:, SM_E128:SM_E128 + E] = P * np.arange(E)
    s[:, SM_G4:SM_G4 + TOPG] = TOPG - np.arange(TOPG)
    s[:, SM_VAL:SM_VAL + NTT] = (np.arange(NTT)[None, :] * P + p[:, None]) < T
    s[:, SM_SEQ:SM_SEQ + DB] = (p[:, None] // DS) == np.arange(DB)[None, :]
    s[:, SM_IOTA:SM_IOTA + NOV] = np.arange(NOV)
    m = np.zeros((P, LEVELS, P), np.float32)
    for l in range(LEVELS):
        L = 1 << l
        m[:, l, :] = ((p[:, None] // (2 * L) == p[None, :] // (2 * L)) & (p[:, None] % (2 * L) < L)
                      & (p[None, :] % (2 * L) >= L))
    return c, m.reshape(P, LEVELS * P)


def build(nc, a):
    ctx = ExitStack()

    def sem(name):
        return ctx.enter_context(nc.semaphore(name))

    with ctx:
        xg_dram = nc.dram_tensor("x_by_slot", (NBLK * P, D), F32, kind="Internal").ap()
        yg_dram = nc.dram_tensor("y_by_slot", (NBLK * P, D), F32, kind="Internal").ap()

        FW = 35472
        FA = ctx.enter_context(nc.sbuf_tensor("FA", [P, FW], F32))
        RA = ctx.enter_context(nc.sbuf_tensor("RA", [P, 68 * 256], F32R))
        masks = ctx.enter_context(nc.sbuf_tensor("masks", [P, LEVELS * P], U8))
        itab = ctx.enter_context(nc.sbuf_tensor("itab", [P, 16], I32))
        slot_i = ctx.enter_context(nc.sbuf_tensor("slot_i", [P, 2 * NTT], I32))
        bank = [ctx.enter_context(nc.psum_tensor(f"bank{i}", [P, 512], F32)) for i in range(8)]

        def fa(off, n):
            return FA[:, off:off + n]

        const = fa(0, C_N)
        ident, tri = const[:, C_ID:C_ID + P], const[:, C_TRI:C_TRI + P]
        blk_ones, ones = const[:, C_BLK:C_BLK + P], const[:, C_ONE:C_ONE + P]
        reset = const[:, C_RST:C_RST + T]
        small = const[:, C_SM:C_SM + 80]
        o_small = C_N
        params = fa(o_small, 88)
        ebl = fa(o_small + 88, H * 12)
        rt = fa(o_small + 136, 464)
        assert o_small + 600 <= 2048
        K = 256
        raw = [fa(8 * K + 2048 * i, 2048) for i in range(6)]
        s0 = fa(32 * K, 4096).rearrange("p (b h v) -> p b h v", b=DB, h=H)
        A0 = 48 * K
        xn = fa(A0, NTT * D).rearrange("p (t n) -> p t n", t=NTT)
        v_tok = fa(A0, NTT * 512).rearrange("p (t n) -> p t n", t=NTT)
        sg = fa(A0 + NTT * 512, H * T).rearrange("p (h t) -> p h t", h=H)
        Q0 = 68 * K
        heads = lambda off: fa(off, H * T).rearrange("p (h t) -> p h t", h=H)
        q, k, b = heads(Q0), heads(Q0 + H * T), heads(Q0 + 2 * H * T)
        Z0 = Q0 + 3 * H * T
        z = heads(Z0)
        yc = heads(Z0)
        E0 = Z0 + H * T
        ex = [heads(E0), heads(E0 + H * T)]
        AT0 = E0 + 2 * H * T
        att = fa(AT0, H * NC * P).rearrange("p (h c t) -> p h c t", h=H, c=NC)
        att_s = fa(AT0 + H * NC * P, H * NS).rearrange("p (h t) -> p h t", h=H)
        U0 = AT0 + H * NC * P + H * NS
        u = fa(U0, 4 * UW).rearrange("p (j t) -> p j t", j=4)
        sq = heads(U0)
        SQ0 = U0 + 4 * UW
        cb = fa(SQ0, 4 * 18).rearrange("p (j t) -> p j t", j=4)
        cb_out = fa(SQ0 + 72, 512)
        assert SQ0 + 72 + 512 <= FW, (SQ0 + 584, FW)
        k_tok = fa(E0 + H * T, H * NC * P).rearrange("p (h c k) -> p h c k", h=H, c=NC)
        state = fa(E0, NC * H * P).rearrange("p (c h v) -> p c h v", c=NC, h=H)
        k_tok_s = fa(Q0 + H * T, 512).rearrange("p (h k) -> p h k", h=H)
        v_msk = fa(Q0 + H * T + 512, DB * P).rearrange("p (b v) -> p b v", b=DB)
        mix = heads(Q0 + 2 * H * T)
        xr = fa(E0, NTT * D).rearrange("p (t n) -> p t n", t=NTT)
        ln = fa(Q0, 4 * D).rearrange("p (i n) -> p i n", i=4)
        x1T = [fa(U0, D).rearrange("p (k t) -> p k t", k=KT),
               fa(U0 + D, D).rearrange("p (k t) -> p k t", k=KT)]
        xg = [fa(56 * K, D), fa(60 * K, D)]
        wr = fa(Z0, KT * E).rearrange("p (k e) -> p k e", k=KT)
        silu_g, hbuf = fa(64 * K, 512), fa(66 * K, 512)
        ysb = [fa(U0, D), fa(U0 + D, D)]
        y_a, y_b = fa(8 * K, NTT * D).rearrange("p (t n) -> p t n", t=NTT), \
            fa(28 * K, NTT * D).rearrange("p (t n) -> p t n", t=NTT)

        split = [[RA[:, (8 * (2 * s + w)) * K:(8 * (2 * s + w) + 8) * K] for w in range(2)] for s in range(3)]
        xT = [RA[:, 32 * K + w * KT * T:32 * K + (w + 1) * KT * T].rearrange("p (k t) -> p k t", k=KT)
              for w in range(2)]
        xgT = [[RA[:, (48 + 8 * par + 4 * w) * K:(52 + 8 * par + 4 * w) * K].rearrange("p (k t) -> p k t", k=KT)
                for w in range(2)] for par in range(2)]
        hT = [RA[:, (64 + 2 * w) * K:(66 + 2 * w) * K].rearrange("p (k t) -> p k t", k=4) for w in range(2)]

        s_const, s_x, s_par, s_s0 = sem("const_in"), sem("x_in"), sem("param_in"), sem("s0_in")
        s_raw = [sem(f"raw_in{i}") for i in range(3)]
        s_hi, s_lo, s_tile = sem("hi_done"), sem("lo_done"), sem("tile_made")
        s_eva, s_evd = sem("evacuated_by_act"), sem("evacuated_by_dve")
        s_xt, s_xh, s_xl = sem("x_transposed"), sem("xT_hi"), sem("xT_lo")
        s_pt, s_pp = sem("param_transposed"), sem("param_ready")
        s_zero, s_fill, s_upad = sem("zero_tile"), sem("slots_filled"), sem("u_pads")
        s_abs, s_lnf, s_b = sem("abs_z"), sem("ln1p"), sem("b_ready")
        s_d, s_e, s_z, s_p, s_pc = sem("exponent"), sem("decay"), sem("decayed_qk"), sem("pairs"), sem("pairs_used")
        s_ps = sem("sample_pairs_used")
        s_qx, s_kx = sem("q_decayed"), sem("k_decayed")
        s_cb, s_cbt, s_cbo, s_cbs = sem("conv_tail"), sem("conv_tail_t"), sem("conv_tail_out"), sem("conv_state_stored")
        s_kt, s_ktc = sem("k_transposed"), sem("k_token_major")
        s_su, s_st, s_o, s_oc = sem("state_update"), sem("state_ready"), sem("o_made"), sem("o_copied")
        s_vm, s_sus, s_s0n, s_sto = sem("v_masked"), sem("sample_update"), sem("sample_state"), sem("sample_states_stored")
        s_stp = sem("prompt_state_stored")
        s_sq, s_ms, s_rt_, s_cat_f, s_cat_h, s_cat_l = (sem("squares"), sem("mean_square"), sem("root"),
                                                        sem("mix_f32"), sem("mix_hi"), sem("mix_lo"))
        s_xr, s_lnp, s_wr = sem("residual_in"), sem("ln_params_in"), sem("router_in")
        s_xr0 = sem("residual_zeroed")
        s_w, s_wc = sem("mix_out"), sem("mix_added")
        s_var, s_std, s_x1 = sem("ln_var"), sem("ln_std"), sem("ln_out")
        s_1t, s_1c, s_lg, s_lgc = sem("x1_transposed"), sem("x1T_copied"), sem("logits"), sem("logits_used")
        s_rl, s_re = sem("logit_shifted"), sem("logit_exp")
        s_oh, s_rk, s_slot, s_sc = sem("choice"), sem("rank"), sem("slots"), sem("rows_scattered")
        s_dv, s_ac = sem("dve_chain"), sem("act_chain")
        m_raw = [sem(f"moe_raw_in{i}") for i in range(6)]
        m_xg = [sem(f"moe_x_in{i}") for i in range(2)]
        m_t, m_th, m_tl = sem("moe_x_transposed"), sem("moe_xT_hi"), sem("moe_xT_lo")
        m_hi, m_lo, m_use = sem("moe_hi"), sem("moe_lo"), sem("moe_chunk_used")
        m_sg, m_h, m_ht, m_hh, m_hl = sem("moe_silu"), sem("moe_h"), sem("moe_h_transposed"), sem("moe_hT_hi"), sem("moe_hT_lo")
        m_ya, m_yd = sem("moe_y_act"), sem("moe_y_dve")
        m_st = [sem(f"moe_y_stored{i}") for i in range(2)]
        s_ga, s_fin, s_fvar, s_fstd, s_out = sem("rows_gathered"), sem("final_sum"), sem("final_var"), sem("final_std"), sem("out_stored")
        s_y1 = sem("final_out")

        block = ctx.enter_context(nc.Block())

        act_tiles = [n for n, (kind, _, _) in enumerate(TILES) if kind not in BY_DVE]
        dve_tiles = [n for n, (kind, _, _) in enumerate(TILES) if kind in BY_DVE]

        def wait_evacuated(eng, n):
            if n in act_tiles:
                eng.wait_ge(s_eva, act_tiles.index(n) + 1)
            else:
                eng.wait_ge(s_evd, dve_tiles.index(n) + 1)

        def tiles_of(o):
            return [n for n, t in enumerate(TILES) if t[1] == o]

        def halves(view, L, n):
            w = view[:, :, 0:n].rearrange("p h (n s l) -> p h n s l", s=2, l=L)
            return w[:, :, :, 0, :], w[:, :, :, 1, :], w[:, :, :, 0, L - 1:L]

        def chunk_weights(s, w):
            return split[s][w].rearrange("p (k n) -> p k n", k=KT)

        def tok(tt):
            return slice(tt * P, min((tt + 1) * P, T))

        NP_LEVELS = (LEVELS + 1) * H

        OV_ORDER = (0, 1, 4, 5, 2, 3)
        mv1 = rt[:, 8:8 + 2 * NTT].rearrange("p (t s) -> p t s", s=2)
        eps_rms, eps_ln = rt[:, 20:21], rt[:, 21:22]
        stats = rt[:, 24:24 + 12 * NTT].rearrange("p (t s) -> p t s", t=NTT)
        NE = NTT * E
        ra = lambda i: rt[:, 88 + i * NE:88 + (i + 1) * NE]
        t3 = lambda v: v.rearrange("p (t e) -> p t e", t=NTT)
        t4 = lambda v: v.rearrange("p (x e) -> p x e", e=TOPG)
        r_l, r_p, r_o1, r_o2 = ra(0), ra(1), ra(2), ra(3)
        R0 = Z0 + KT * E
        rb = lambda i, n: fa(R0 + i, n)

        gw = rt[:, 408:418]
        choice = fa(R0 + 640, NE)

        def norm_bank(m):
            return bank[[4, 5, 6, 0, 1][m]]

        def raw_use(bi, j):
            return bi if j in (2, 3) else bi + 1

        def gate_count(bi):
            return 2 if isinstance(bi, int) and bi == 0 else 6 * bi + 0

        def up_count(bi):
            return 4 if isinstance(bi, int) and bi == 0 else 6 * bi + 4

        def down_count(bi):
            if isinstance(bi, int) and bi == E - 1:
                return 6 * E
            return 6 * (bi + 1) + 2

        def store_count(bi, par):
            return 8 * (bi - par)

        def count_of(bi, j):
            if isinstance(bi, int) and bi == 0:
                return j + 1 if j < 2 else j - 1
            if isinstance(bi, int) and bi == E:
                return 6 * E - 2 + j - 1
            return 6 * bi + j - 1

        def slot_free_count(bi, j):
            first = isinstance(bi, int) and bi == 0
            if first:
                return count_of(0, 1) if j == 4 else None
            if isinstance(bi, int) and bi == E and j == 3:
                return count_of(E - 1, 3)
            if j >= 3:
                return count_of(bi, j - 3)
            if isinstance(bi, int) and bi == 1 and j == 0:
                return count_of(0, 1)
            return count_of(bi - 1, j + 3)

        @block.sync
        def _(sp):
            sp.dma_start(xn[:, 0:4, :], a["x_prompt"][0].rearrange("(t p) n -> p t n", p=P)).then_inc(s_x, 16)
            sp.dma_start(xn[0:NS, 4, :], a["x_sample"].rearrange("b t n -> (b t) n")).then_inc(s_x, 16)
            sp.dma_start(const, a["const_f32"]).then_inc(s_const, 16)
            pr = sq[:, 0, 0:P]
            sp.dma_start(fa(E0, LEVELS * P), a["const_mask"]).then_inc(s_const, 16)
            sp.dma_start(pr[0:4, :], a["hgrn_norm_g"].rearrange("a (t p) -> (a t) p", p=P)).then_inc(s_par, 16)
            sp.dma_start(pr[4:16, :], a["conv_w"].rearrange("a j (t p) -> (a j t) p", p=P)).then_inc(s_par, 16)
            sp.dma_start(pr[16:20, :], a["conv_norm_g"].rearrange("a (t p) -> (a t) p", p=P)).then_inc(s_par, 16)
            sp.dma_start(pr[20:84, :], a["state_conv"].rearrange("a b j (t p) -> (a b j t) p", p=P)).then_inc(s_par, 16)
            w_in = a["w_in"][0].rearrange("(k p) n -> p k n", p=P)
            w_out = a["w_out"][0].rearrange("(k p) n -> p k n", p=P)
            for c in range(NCH + NWO):
                if c >= 3:
                    sp.wait_ge(s_lo, c - 2)
                src = w_in[:, :, ORDER[c][1] * CW:(ORDER[c][1] + 1) * CW] if c < NCH \
                    else w_out[:, :, (c - NCH) * CW:(c - NCH + 1) * CW]
                sp.dma_start(raw[c % 3].rearrange("p (k n) -> p k n", k=KT), src).then_inc(s_raw[c % 3], 16)
                if c == 3:
                    sp.dma_start(s0, a["state_hgrn"][0].rearrange("b h k v -> k b h v")).then_inc(s_s0, 16)
            sp.wait_ge(s_cbo, 1)
            sp.dma_start(a["out_conv_prompt"][0, 0, :, :], cb_out[0:2, :]).then_inc(s_cbs, 16)
            sp.dma_start(a["out_conv_sample"][0].rearrange("b j n -> (b j) n"), cb_out[2:18, :]).then_inc(s_cbs, 16)
            sp.wait_ge(s_st, NC)
            sp.dma_start(a["out_hgrn_prompt"][0, 0].rearrange("h k v -> k h v"), state[:, NC - 1, :, :]).then_inc(s_stp, 16)
            sp.wait_ge(s_s0n, DB * H)
            sp.dma_start(a["out_hgrn_sample"][0].rearrange("b h k v -> k b h v"), s0).then_inc(s_sto, 16)
            sp.wait_ge(s_stp, 16)
            sp.wait_ge(s_oc, H + 1)
            sp.wait_ge(s_xr0, 1)
            sp.dma_start(xr[:, 0:4, :], a["x_prompt"][0].rearrange("(t p) n -> p t n", p=P)).then_inc(s_xr, 16)
            sp.dma_start(xr[0:NS, 4, :], a["x_sample"].rearrange("b t n -> (b t) n")).then_inc(s_xr, 16)
            sp.wait_ge(s_s0n, DB * H)
            for i, name in enumerate(("ln1_g", "ln1_b", "ln2_g", "ln2_b")):
                sp.dma_start(ln[:, i, :], a[name].broadcast_to([P, D])).then_inc(s_lnp, 16)
            sp.wait_ge(s_cat_l, 8)
            sp.dma_start(wr, a["w_router"].rearrange("(k p) e -> p k e", p=P)).then_inc(s_wr, 16)
            sp.dma_start(rt[:, 448:464], a["router_bias"].unsqueeze(0).broadcast_to([P, E])).then_inc(s_wr, 16)

            w_gu = [a["w_gate"][0], a["w_up"][0]]

            def gu_src(which, e, c):
                w = w_gu[which][e] if isinstance(e, int) else w_gu[which][bass.ds(e, 1)].squeeze(0)
                return w[c * 512:(c + 1) * 512, :].rearrange("(p t) n -> p (t n)", t=4)

            def d_src(e, c):
                w = a["w_down"][0][e] if isinstance(e, int) else a["w_down"][0][bass.ds(e, 1)].squeeze(0)
                return w[c * 256:(c + 1) * 256, :].rearrange("(p t) n -> p (t n)", t=2)

            def load(slot, src):
                sp.dma_start(raw[slot], src).then_inc(m_raw[slot], 16)

            def moe_loads(bi, e, ep):
                last = isinstance(bi, int) and bi == E
                for j in (2, 3) if last else range(6):
                    sp.wait_ge(m_lo, count_of(bi - 1, j))
                    load(j, gu_src(0, e, j) if j < 2 else d_src(ep, j - 2) if j < 4 else gu_src(1, e, j - 4))

            sp.wait_ge(s_sto, 16)
            load(4, gu_src(1, 0, 0))
            load(5, gu_src(1, 0, 1))
            load(3, d_src(0, 1))
            sp.wait_ge(s_lo, NCH + NWO - 2)
            load(0, gu_src(0, 0, 0))
            sp.wait_ge(s_lo, NCH + NWO - 1)
            load(1, gu_src(0, 0, 1))
            sp.wait_ge(s_lo, NCH + NWO)
            load(2, d_src(0, 0))
            sp.wait_ge(s_cat_f, 12)
            x_slot = xg_dram.rearrange("(b p) n -> b p n", p=P)

            def load_x(bi, par):
                src = x_slot[bi] if isinstance(bi, int) else x_slot[bass.ds(bi, 1)].squeeze(0)
                sp.dma_start(xg[par], src).then_inc(m_xg[par], 16)

            sp.wait_ge(s_sc, 16 * 2 * NTT)
            load_x(0, 0)
            load_x(1, 1)
            for j in (0, 1, 4, 5):
                sp.wait_ge(m_lo, count_of(0, j))
                load(j, gu_src(j // 4, 1, j % 4))
            sp.wait_ge(m_t, 1)
            load_x(2, 0)
            def load_step(bi, par):
                sp.wait_ge(m_t, bi)
                if not (isinstance(bi, int) and bi == E - 1):
                    load_x(bi + 1, 1 - par)
                moe_loads(bi, bi, bi - 1)

            with sp.Fori(0, (E - 4) // 2) as i:
                load_step(2 * i + 2, 0)
                load_step(2 * i + 3, 1)
            load_step(E - 2, 0)
            load_step(E - 1, 1)
            moe_loads(E, None, E - 1)
            sp.wait_ge(s_slot, 3)
            n_over = sp.value_load(itab[0:1, 0:1], min_val=0, max_val=NOV)
            with sp.Fori(0, NOV // 2) as i:
                for r in range(2):
                    v = 2 * i + r
                    with sp.If(v < n_over):
                        e = sp.value_load(itab[0:1, bass.ds(v + 1, 1)], min_val=0, max_val=E - 1)
                        sp.wait_ge(m_t, E + v)
                        load_x(E + v, r)
                        sp.wait_ge(m_lo, 6 * E + 6 * v)
                        for j in range(2):
                            load(j, gu_src(0, e, j))
                        for j in range(2):
                            load(4 + j, gu_src(1, e, j))
                        for j in range(2):
                            load(2 + j, d_src(e, j))

        @block.gpsimd
        def _(pool):
            nc.gpsimd.memset(fa(U0 + 1024, D), 0.0).then_inc(s_zero, 1)
            pool.wait_ge(s_zero, 1)
            pool.wait_ge(s_xl, 2 * NTT)
            fill_src = fa(U0 + 1024, D).unsqueeze(1).broadcast_to([P, NBLK, D])
            pool.dma_start(xg_dram.rearrange("(b p) n -> p b n", p=P), fill_src).then_inc(s_fill, 16)
            pool.dma_start(yg_dram[E * P:NBLK * P, :].rearrange("(b p) n -> p b n", p=P), fill_src[:, 0:NOV, :]).then_inc(s_fill, 16)
            pool.wait_ge(s_fill, 32)
            pool.wait_ge(s_pt, 1)
            for j in range(4):
                last = nc.gpsimd.memset(u[:, j, 0:2], 0.0)
            last.then_inc(s_upad, 1)
            for n in range(2):
                for tt in range(NTT):
                    rows = NS if tt == NTT - 1 else P
                    if n == 0 and tt == 0:
                        pool.wait_ge(s_slot, 1)
                        pool.wait_ge(s_x1, NTT)
                    pool.indirect_dma_start(
                        out=xg_dram, out_offset=bass.IndirectOffsetOnAxis(ap=slot_i[0:rows, 5 * n + tt:5 * n + tt + 1].bitcast(U32), axis=0),
                        in_=xr[0:rows, tt, :], in_offset=None).then_inc(s_sc, 16)
            y_slot = yg_dram.rearrange("(b p) n -> b p n", p=P)

            def store(bi, par):
                pool.wait_ge(m_ya, bi + 1)
                pool.wait_ge(m_yd, bi + 1)
                dst = y_slot[bi] if isinstance(bi, int) else y_slot[bass.ds(bi, 1)].squeeze(0)
                pool.dma_start(dst, ysb[par]).then_inc(m_st[par], 16)

            with pool.Fori(0, E // 2) as i:
                for par in range(2):
                    store(2 * i + par, par)
            for par in range(2):
                pool.wait_ge(m_st[par], 16 * (E // 2))
            pool.wait_ge(s_slot, 3)
            n_over = pool.value_load(itab[0:1, 0:1], min_val=0, max_val=NOV)
            with pool.Fori(0, NOV // 2) as i:
                for par in range(2):
                    with pool.If(2 * i + par < n_over):
                        store(E + 2 * i + par, par)
                        pool.wait_ge(m_st[par], 16 * (E // 2) + 16 * (i + 1))
            for tt in range(NTT):
                rows = NS if tt == NTT - 1 else P
                for n, dst in enumerate((y_a, y_b)):
                    pool.indirect_dma_start(
                        out=dst[0:rows, tt, :], out_offset=None, in_=yg_dram,
                        in_offset=bass.IndirectOffsetOnAxis(ap=slot_i[0:rows, 5 * n + tt:5 * n + tt + 1].bitcast(U32), axis=0)).then_inc(s_ga, 16)
            for tt in range(NTT):
                pool.wait_ge(s_y1, tt + 1)
                if tt < 4:
                    pool.dma_start(a["out_prompt"][0, tt * P:(tt + 1) * P, :], y_a[:, tt, :]).then_inc(s_out, 16)
                else:
                    pool.dma_start(a["out_sample"].rearrange("b t n -> (b t) n"), y_a[0:NS, tt, :]).then_inc(s_out, 16)
            pool.wait_ge(s_out, 16 * NTT)
            pool.wait_ge(s_cbs, 32)
            pool.wait_ge(s_sto, 16)
            pool.wait_ge(s_stp, 16)

        @block.scalar
        def _(act):
            chain = [0]

            def link(ins):
                chain[0] += 1
                ins.then_inc(s_ac, 1)
                act.wait_ge(s_ac, chain[0])

            for m in range(2 * NTT):
                tt, hf = m // 2, m % 2
                n = P if tt < 4 else NS
                act.wait_ge(s_xt, m + 1)
                src = bank[4 + m % 2][:, 0:4 * n].rearrange("p (k t) -> p k t", k=4)
                nc.scalar.activation(xT[0][:, 4 * hf:4 * hf + 4, tok(tt)], src, ACT.Copy).then_inc(s_xh, 1)
            act.wait_ge(s_pt, 1)
            nc.scalar.activation(params[:, 0:84], bank[7][:, 0:84], ACT.Copy).then_inc(s_pp, 1)

            def hi(o):
                act.wait_ge(s_raw[o % 3], 16 * (o // 3 + 1))
                if 2 <= o < NCH + 2:
                    act.wait_ge(s_tile, tiles_of(o - 2)[-1] + 1)
                elif o >= NCH + 2:
                    act.wait_ge(s_w, NTT * (o - 1 - NCH))
                nc.scalar.activation(split[o % 2][0], raw[o % 3], ACT.Copy).then_inc(s_hi, 1)

            def evacuate(o):
                for n in tiles_of(o):
                    kind, _, j = TILES[n]
                    if kind in BY_DVE:
                        continue
                    act.wait_ge(s_tile, n + 1)
                    pb, ps = bank[n % 2], bank[2 + n % 2]
                    if kind == "v":
                        rows = P if j < 4 else NS
                        half = ORDER[o][1] - 4
                        nc.scalar.activation(v_tok[0:rows, j, half * CW:(half + 1) * CW], pb[0:rows, 0:CW],
                                             ACT.Copy).then_inc(s_eva, 1)
                        continue
                    h = 2 * (o % 2) + j
                    cols = [(pb[:, :], slice(0, SEQ)), (ps[:, 0:NS], slice(SEQ, T))]
                    if kind == "f":
                        for src, c in cols:
                            nc.scalar.activation(z[:, h, c], src, ACT.Copy)
                        nc.scalar.activation(k[:, h, 0:SEQ], pb[:, :], ACT.Sigmoid, scale=-1.0)
                        nc.scalar.activation(k[:, h, SEQ:T], ps[:, 0:NS], ACT.Sigmoid, scale=-1.0).then_inc(s_eva, 1)
                    elif kind == "gc":
                        if o == 6 and j == 0:
                            act.wait_ge(s_upad, 1)
                        nc.scalar.activation(u[:, h, 2:2 + SEQ], pb[:, :], ACT.Copy)
                        nc.scalar.activation(u[:, h, 2 + SEQ:UW].rearrange("p (b t) -> p b t", b=DB)[:, :, 2:2 + DS],
                                             ps[:, 0:NS].rearrange("p (b t) -> p b t", b=DB), ACT.Copy).then_inc(s_eva, 1)
                    else:
                        dst = q if kind == "q" else sg
                        nc.scalar.activation(dst[:, h, 0:SEQ], pb[:, :], ACT.Silu)
                        nc.scalar.activation(dst[:, h, SEQ:T], ps[:, 0:NS], ACT.Silu).then_inc(s_eva, 1)

            for o in range(NCH + 2):
                if o >= 2:
                    evacuate(o - 2)
                hi(o)
                if o == 5:
                    act.wait_ge(s_abs, 1)
                    link(nc.scalar.activation(ex[0][:, :, :], ex[0][:, :, :], ACT.Exp, scale=-1.0))
                    nc.scalar.activation(ex[0][:, :, :], ex[0][:, :, :], ACT.Ln, bias=1.0).then_inc(s_lnf, 1)
                l = o - FIRST_LEVEL_STEP
                if 0 <= l < LEVELS:
                    act.wait_ge(s_d, l + 1)
                    n = T if l < SLEVELS else SEQ
                    nc.scalar.activation(ex[l % 2][:, :, 0:n], ex[l % 2][:, :, 0:n], ACT.Exp).then_inc(s_e, 1)
            act.wait_ge(s_p, H * LEVELS)
            nc.scalar.activation(ex[1][:, :, :], b[:, :, :], ACT.Exp).then_inc(s_e, 1)
            act.wait_ge(s_d, LEVELS + 1)
            nc.scalar.activation(ex[0][:, :, :], ex[0][:, :, :], ACT.Exp).then_inc(s_e, 1)

            act.wait_ge(s_cbt, 1)
            nc.scalar.activation(cb_out[0:18, :], bank[7][0:18, :], ACT.Copy).then_inc(s_cbo, 1)

            for g in range(2):
                for m in range(H + 1):
                    act.wait_ge(s_ms, (H + 1) * g + m + 1)
                    pb = norm_bank(m)
                    scale = 1.0 / 64 if g == 0 else 1.0 / P
                    dst, src = (sq[:, m, 0:SEQ], pb[:, :]) if m < H else \
                        (sq[:, :, SEQ:T], pb[:, 0:H * NS].rearrange("p (h t) -> p h t", h=H))
                    nc.scalar.activation(dst, src, ACT.Sqrt, bias=eps_rms, scale=scale).then_inc(s_rt_, 1)
                act.wait_ge(s_tile, len(TILES))
                for j in range(4):
                    act.wait_ge(s_cat_f, 8 * g + j + 1)
                    src, row = (yc, 4 + j) if g == 0 else (mix, j)
                    nc.scalar.activation(xT[0][:, row, :], src[:, j, :], ACT.Copy).then_inc(s_cat_h, 1)
            hi(NCH + 2)
            hi(NCH + 3)
            act.wait_ge(s_var, 1)
            nc.scalar.activation(rt[:, 0:NTT], mv1[:, :, 1], ACT.Sqrt, bias=eps_ln).then_inc(s_std, 1)
            act.wait_ge(s_rl, 1)
            nc.scalar.activation(r_p, r_l, ACT.Exp).then_inc(s_re, 1)

            def mhi(bi, j, slot=None):
                act.wait_ge(m_raw[j], 16 * raw_use(bi, j))
                f = slot_free_count(bi, j)
                if f is not None:
                    act.wait_ge(m_use, f)
                nc.scalar.activation(split[j % 3][0], raw[j], ACT.Copy).then_inc(m_hi, 1)

            def x_hi(bi, par):
                for c in range(2):
                    act.wait_ge(m_t, bi + 1)
                    nc.scalar.activation(xgT[par][0][:, 4 * c:4 * c + 4, :], bank[c][:, :].rearrange("p (k t) -> p k t", k=4),
                                         ACT.Copy).then_inc(m_th, 1)

            def h_hi(bi):
                act.wait_ge(m_ht, bi + 1)
                nc.scalar.activation(hT[0][:, :, :], bank[4][:, :].rearrange("p (k t) -> p k t", k=4),
                                     ACT.Copy).then_inc(m_hh, 1)

            def silu(bi):
                act.wait_ge(m_use, gate_count(bi))
                if not (isinstance(bi, int) and bi == 0):
                    act.wait_ge(m_h, bi)
                nc.scalar.activation(silu_g, bank[2][:, :], ACT.Silu).then_inc(m_sg, 1)

            def y_half(bi, par):
                act.wait_ge(m_use, down_count(bi))
                if not (isinstance(bi, int) and bi < 2):
                    act.wait_ge(m_st[par], store_count(bi, par))
                nc.scalar.activation(ysb[par][:, 0:512], bank[5][:, :], ACT.Copy).then_inc(m_ya, 1)

            def step(bi, par):
                first, last = isinstance(bi, int) and bi == 0, isinstance(bi, int) and bi == E - 1
                if not first:
                    mhi(bi, 2)
                    h_hi(bi - 1)
                    mhi(bi, 3)
                mhi(bi, 4)
                silu(bi)
                mhi(bi, 5)
                if not last:
                    mhi(bi + 1, 0)
                if not first:
                    y_half(bi - 1, 1 - par)
                if not last:
                    x_hi(bi + 1, 1 - par)
                    mhi(bi + 1, 1)

            mhi(0, 0)
            mhi(0, 1)
            x_hi(0, 0)
            step(0, 0)
            step(1, 1)
            step(2, 0)
            with act.Fori(0, (E - 4) // 2) as i:
                step(2 * i + 3, 1)
                step(2 * i + 4, 0)
            step(E - 1, 1)
            mhi(E, 2)
            h_hi(E - 1)
            mhi(E, 3)
            y_half(E - 1, 1)
            act.wait_ge(s_slot, 3)
            n_over = act.value_load(itab[0:1, 0:1], min_val=0, max_val=NOV)
            with act.Fori(0, NOV // 2) as i:
                for par in range(2):
                    v = 2 * i + par
                    with act.If(v < n_over):
                        x_hi(E + v, par)
                        for s, j in enumerate(OV_ORDER):
                            if s == 4:
                                h_hi(E + v)
                            act.wait_ge(m_raw[j], 16 * (E + v + 1))
                            act.wait_ge(m_use, 6 * E + 6 * v if s < 3 else 6 * E + 6 * v + s - 2)
                            nc.scalar.activation(split[s % 3][0], raw[j], ACT.Copy).then_inc(m_hi, 1)
                            if s == 3:
                                act.wait_ge(m_use, 6 * E + 6 * v + 2)
                                act.wait_ge(m_h, E + v)
                                nc.scalar.activation(silu_g, bank[2][:, :], ACT.Silu).then_inc(m_sg, 1)
                        act.wait_ge(m_use, 6 * E + 6 * v + 6)
                        act.wait_ge(m_st[par], 16 * (E // 2) + 16 * i)
                        nc.scalar.activation(ysb[par][:, 0:512], bank[5][:, :], ACT.Copy).then_inc(m_ya, 1)
            act.wait_ge(s_fvar, 1)
            nc.scalar.activation(rt[:, 0:NTT], mv1[:, :, 1], ACT.Sqrt, bias=eps_ln).then_inc(s_fstd, 1)

        @block.vector
        def _(dve):
            tt_, ts_, stt = nc.vector.tensor_tensor, nc.vector.tensor_scalar, nc.vector.scalar_tensor_tensor
            chain = [0]

            def link(ins):
                chain[0] += 1
                ins.then_inc(s_dv, 1)
                dve.wait_ge(s_dv, chain[0])

            f = lambda r: r.bitcast(F32)
            nc.vector.memset(eps_rms, RMS_EPS)
            link(nc.vector.memset(eps_ln, LN_EPS))
            dve.wait_ge(s_const, 32)
            link(nc.vector.tensor_copy(masks[:, :], fa(E0, LEVELS * P)))
            for m in range(2 * NTT):
                tt, hf = m // 2, m % 2
                n = P if tt < 4 else NS
                dve.wait_ge(s_xh, m + 1)
                src = bank[4 + m % 2][:, 0:4 * n].rearrange("p (k t) -> p k t", k=4)
                tt_(xT[1][:, 4 * hf:4 * hf + 4, tok(tt)], src, f(xT[0][:, 4 * hf:4 * hf + 4, tok(tt)]),
                    ALU.subtract).then_inc(s_xl, 1)

            def lo(o):
                dve.wait_ge(s_hi, o + 1)
                tt_(split[o % 2][1], raw[o % 3], f(split[o % 2][0]), ALU.subtract).then_inc(s_lo, 1)

            par_g = lambda base, j: params[:, base + j:base + j + 1]

            def evacuate(o):
                for n in tiles_of(o):
                    kind, _, j = TILES[n]
                    if kind not in BY_DVE:
                        continue
                    dve.wait_ge(s_tile, n + 1)
                    pb, ps = bank[n % 2], bank[2 + n % 2]
                    h = 2 * (o % 2) + j
                    if kind == "cx":
                        if o == 8 and j == 0:
                            dve.wait_ge(s_eva, act_tiles.index(tiles_of(7)[1]) + 1)
                            dve.wait_ge(s_pp, 1)
                        us = u[:, h, 2 + SEQ:UW].rearrange("p (b t) -> p b t", b=DB)
                        up = u[:, h, 2:2 + SEQ]
                        tt_(up, up, pb[:, :], ALU.mult)
                        tt_(us[:, :, 2:2 + DS], us[:, :, 2:2 + DS], ps[:, 0:NS].rearrange("p (b t) -> p b t", b=DB),
                            ALU.mult).then_inc(s_evd, 1)
                        link(nc.vector.tensor_copy(us[:, :, 0:2],
                                                   params[:, 20:84].rearrange("p (b j t) -> p b j t", b=DB, j=2)[:, :, :, h]))
                        dve.wait_ge(s_evd, dve_tiles.index(n) + 1)
                        yp, ys = yc[:, h, 0:SEQ], yc[:, h, SEQ:T].rearrange("p (b t) -> p b t", b=DB)
                        ts_(yp, u[:, h, 0:SEQ], par_g(4, h), None, ALU.mult)
                        link(ts_(ys, us[:, :, 0:DS], par_g(4, h), None, ALU.mult))
                        for jj in (1, 2):
                            stt(yp, u[:, h, jj:jj + SEQ], par_g(4 + 4 * jj, h), yp, ALU.mult, ALU.add)
                            link(stt(ys, us[:, :, jj:jj + DS], par_g(4 + 4 * jj, h), ys, ALU.mult, ALU.add))
                        nc.vector.tensor_copy(cb[:, h, 0:2], u[:, h, SEQ:SEQ + 2])
                        nc.vector.tensor_copy(cb[:, h, 2:18].rearrange("p (b t) -> p b t", b=DB),
                                              us[:, :, DS:DS + 2]).then_inc(s_cb, 1)
                    else:
                        tt_(yc[:, h, 0:SEQ], yc[:, h, 0:SEQ], pb[:, :], ALU.mult)
                        tt_(yc[:, h, SEQ:T], yc[:, h, SEQ:T], ps[:, 0:NS], ALU.mult).then_inc(s_evd, 1)

            def exponents(l):
                L, n = 1 << l, T if l < SLEVELS else SEQ
                if l >= 2:
                    dve.wait_ge(s_p, H * l)
                bl, br, mid = halves(b, L, n)
                dl, dr, _ = halves(ex[l % 2], L, n)
                mb = mid.broadcast_to(list(bl.shape))
                tt_(dr, br, mb, ALU.subtract)
                tt_(dl, mb, bl, ALU.subtract).then_inc(s_d, 1)

            def decayed(l):
                L, n = 1 << l, T if l < SLEVELS else SEQ
                dve.wait_ge(s_e, l + 1)
                dl, dr, _ = halves(ex[l % 2], L, n)
                _, qr, _ = halves(q, L, n)
                kl, _, _ = halves(k, L, n)
                tt_(dr, dr, qr, ALU.mult)
                tt_(dl, dl, kl, ALU.mult).then_inc(s_z, 1)

            def take_pairs(li):
                for h in range(H):
                    p = li * H + h
                    dve.wait_ge(s_p, p + 1)
                    src = bank[4 + p % 3][:, :].rearrange("p (c t) -> p c t", c=NC)
                    if li == 0:
                        tt_(att[:, h, :, :], src, ident.unsqueeze(1).broadcast_to([P, NC, P]), ALU.mult).then_inc(s_pc, 1)
                    else:
                        m = masks[:, (li - 1) * P:li * P].unsqueeze(1).broadcast_to([P, NC, P])
                        nc.vector.copy_predicated(att[:, h, :, :], m, src).then_inc(s_pc, 1)
                if li <= SLEVELS:
                    src = bank[7][0:NS, 0:H * NS].rearrange("p (h t) -> p h t", h=H)
                    if li == 0:
                        tt_(att_s[0:NS], src, ident[0:NS, 0:NS].unsqueeze(1).broadcast_to([NS, H, NS]), ALU.mult).then_inc(s_ps, 1)
                    else:
                        m = masks[0:NS, (li - 1) * P:(li - 1) * P + NS].unsqueeze(1).broadcast_to([NS, H, NS])
                        nc.vector.copy_predicated(att_s[0:NS], m, src).then_inc(s_ps, 1)
                    dve.wait_ge(s_ps, li + 1)
                dve.wait_ge(s_pc, H * (li + 1))

            for o_ in range(NCH + 2):
                if o_ >= 2:
                    evacuate(o_ - 2)
                lo(o_)
                if o_ == 4:
                    dve.wait_ge(s_eva, 4)
                    stt(ex[0][:, :, :], z[:, :, :], -1.0, z[:, :, :], ALU.mult, ALU.max).then_inc(s_abs, 1)
                if o_ == 5:
                    dve.wait_ge(s_lnf, 1)
                    link(stt(z[:, :, :], z[:, :, :], 0.0, ex[0][:, :, :], ALU.min, ALU.subtract))
                    for h in range(H):
                        nc.vector.tensor_tensor_scan(b[:, h, :], reset, z[:, h, :], 0.0, ALU.mult, ALU.add).then_inc(s_b, 1)
                    dve.wait_ge(s_b, H)
                l = o_ - FIRST_LEVEL_STEP
                if 0 <= l - 1 < LEVELS:
                    if l == 1:
                        dve.wait_ge(s_eva, 8)
                    decayed(l - 1)
                if 0 <= l - 1 <= LEVELS:
                    take_pairs(l - 1)
                if 0 <= l < LEVELS:
                    exponents(l)
            dve.wait_ge(s_e, LEVELS + 1)
            tt_(q[:, :, :], q[:, :, :], ex[1][:, :, :], ALU.mult).then_inc(s_qx, 1)
            eb = ebl.rearrange("p (h c) -> p h c", h=H)
            nc.vector.tensor_copy(eb[:, :, 0:NC], ex[1][:, :, P - 1:SEQ:P])
            link(nc.vector.tensor_copy(eb[:, :, NC:12], ex[1][:, :, SEQ + DS - 1:T:DS]))
            for (c0, c1, w) in ((0, SEQ, P), (SEQ, T, DS)):
                bv = b[:, :, c0:c1].rearrange("p h (c t) -> p h c t", t=w)
                dv = ex[0][:, :, c0:c1].rearrange("p h (c t) -> p h c t", t=w)
                last = tt_(dv, bv[:, :, :, w - 1:w].broadcast_to(list(bv.shape)), bv, ALU.subtract)
            last.then_inc(s_d, 1)
            dve.wait_ge(s_e, LEVELS + 2)
            tt_(k[:, :, :], k[:, :, :], ex[0][:, :, :], ALU.mult).then_inc(s_kx, 1)
            for h in range(H):
                dve.wait_ge(s_kt, h + 1)
                nc.vector.tensor_copy(k_tok[:, h, :, :], bank[4 + (NP_LEVELS + h) % 3][:, :].rearrange("p (c k) -> p c k", c=NC)).then_inc(s_ktc, 1)
            dve.wait_ge(s_kt, H + 1)
            nc.vector.tensor_copy(k_tok_s[0:NS], bank[4 + (NP_LEVELS + H) % 3][0:NS, :].rearrange("p (h k) -> p h k", h=H)).then_inc(s_ktc, 1)
            for c in range(NC):
                dve.wait_ge(s_su, c + 1)
                pb = bank[4 + c % 2]
                if c == 0:
                    nc.vector.tensor_copy(state[:, 0, :, :], pb[:, :].rearrange("p (h v) -> p h v", h=H)).then_inc(s_st, 1)
                else:
                    for h in range(H):
                        last = stt(state[:, c, h, :], state[:, c - 1, h, :], eb[:, h, c:c + 1], pb[:, h * P:(h + 1) * P],
                                   ALU.mult, ALU.add)
                    last.then_inc(s_st, 1)
                dve.wait_ge(s_st, c + 1)
            seq_mask = small[0:NS, SM_SEQ:SM_SEQ + DB].unsqueeze(2).broadcast_to([NS, DB, P])
            for h in range(H):
                if h:
                    dve.wait_ge(s_sus, 2 * h)
                tt_(v_msk[0:NS], v_tok[0:NS, 4, h * P:(h + 1) * P].unsqueeze(1).broadcast_to([NS, DB, P]), seq_mask,
                    ALU.mult).then_inc(s_vm, 1)
                for g in range(2):
                    dve.wait_ge(s_sus, 2 * h + g + 1)
                    if h == 0 and g == 0:
                        dve.wait_ge(s_s0, 16)
                    pb = bank[4 + (2 * h + g) % 2]
                    for bb in range(4):
                        bi = 4 * g + bb
                        stt(s0[:, bi, h, :], s0[:, bi, h, :], eb[:, h, NC + bi:NC + bi + 1], pb[:, bb * P:(bb + 1) * P],
                            ALU.mult, ALU.add).then_inc(s_s0n, 1)
            for h in range(H):
                dve.wait_ge(s_o, h + 1)
                nc.vector.tensor_copy(mix[:, h, 0:SEQ], bank[h][:, :]).then_inc(s_oc, 1)
            dve.wait_ge(s_o, H + 1)
            nc.vector.tensor_copy(mix[:, :, SEQ:T], bank[7][:, 0:H * NS].rearrange("p (h t) -> p h t", h=H)).then_inc(s_oc, 1)
            dve.wait_ge(s_oc, H + 1)
            dve.wait_ge(s_stp, 16)
            nc.vector.memset(xr[:, 4, :], 0.0).then_inc(s_xr0, 1)
            for g, src in enumerate((yc, mix)):
                if g == 0:
                    dve.wait_ge(s_cb, 4)
                tt_(sq[:, :, :], src[:, :, :], src[:, :, :], ALU.mult).then_inc(s_sq, 1)
                dve.wait_ge(s_rt_, (H + 1) * (g + 1))
                link(nc.vector.reciprocal(sq[:, :, :], sq[:, :, :]))
                for j in range(4):
                    gain = params[:, 16 + j:17 + j] if g == 0 else params[:, j:j + 1]
                    stt(src[:, j, :], src[:, j, :], gain, sq[:, j, :], ALU.mult, ALU.mult).then_inc(s_cat_f, 1)
                if g:
                    dve.wait_ge(s_cat_f, 8)
                    dve.wait_ge(s_eva, len(act_tiles))
                    for j in range(4):
                        tt_(src[:, j, :], src[:, j, :], sg[:, j, :], ALU.mult).then_inc(s_cat_f, 1)
                for j in range(4):
                    dve.wait_ge(s_cat_h, 4 * g + j + 1)
                    row = 4 + j if g == 0 else j
                    tt_(xT[1][:, row, :], src[:, j, :], f(xT[0][:, row, :]), ALU.subtract).then_inc(s_cat_l, 1)
            dve.wait_ge(s_xr, 32)
            for c in range(NWO):
                for tt in range(NTT):
                    n = c * NTT + tt
                    rows = P if tt < 4 else NS
                    dve.wait_ge(s_w, n + 1)
                    dst = xr[0:rows, tt, c * CW:(c + 1) * CW]
                    stt(dst, dst, ALPHA, bank[n % 4][0:rows, 0:CW], ALU.mult, ALU.add).then_inc(s_wc, 1)
                    if c < 2 and tt == NTT - 1:
                        lo(NCH + 2 + c)
            dve.wait_ge(s_wc, NWO * NTT)

            def norm_stats(x, out_sem):
                for tt in range(NTT):
                    for g in range(2):
                        nc.vector.bn_stats(stats[:, tt, 6 * g:6 * g + 6], x[:, tt, 512 * g:512 * g + 512]).then_inc(s_dv, 1)
                chain[0] += 2 * NTT
                dve.wait_ge(s_dv, chain[0])
                for tt in range(NTT):
                    last = nc.vector.bn_aggr(mv1[:, tt, :], stats[:, tt, :])
                last.then_inc(out_sem, 1)

            def normalise(x, in_sem, g, out_sem):
                dve.wait_ge(in_sem, 1)
                link(nc.vector.reciprocal(rt[:, 0:NTT], rt[:, 0:NTT]))
                for tt in range(NTT):
                    link(ts_(x[:, tt, :], x[:, tt, :], mv1[:, tt, 0:1], rt[:, tt:tt + 1], ALU.subtract, ALU.mult))
                    link(tt_(x[:, tt, :], x[:, tt, :], ln[:, g, :], ALU.mult))
                    tt_(x[:, tt, :], x[:, tt, :], ln[:, g + 1, :], ALU.add).then_inc(out_sem, 1)

            norm_stats(xr, s_var)
            dve.wait_ge(s_lnp, 64)
            normalise(xr, s_std, 0, s_x1)
            for m in range(2 * NTT):
                tt, hf = m // 2, m % 2
                dve.wait_ge(s_1t, m + 1)
                if tt >= 2 and hf == 0:
                    dve.wait_ge(s_lg, tt - 1)
                nc.vector.tensor_copy(x1T[tt % 2][:, 4 * hf:4 * hf + 4, :],
                                      bank[4 + m % 2][:, :].rearrange("p (k t) -> p k t", k=4)).then_inc(s_1c, 1)

            bias_b = rt[:, 448:464].unsqueeze(1).broadcast_to([P, NTT, E])
            mx, s5 = rb(0, NTT), rb(8, NTT)
            pair, gs, gm, g1 = rb(16, 6 * 20), rb(136, 20), rb(156, NTT), rb(164, 20)
            pm, tmp, m1, m2 = rb(184, NE), rb(264, NE), rb(344, NTT), rb(352, NTT)
            rank, cnt, nb, ob, on_, big = rb(360, NE), rb(440, E), rb(456, E), rb(472, E), rb(488, E), rb(504, NE)
            slot_f, tf = rb(584, 2 * NTT), rb(600, 16)
            bc = lambda v, n: v.unsqueeze(2).broadcast_to([P, v.shape[1], n])
            dve.wait_ge(s_lg, NTT)
            dve.wait_ge(s_wr, 32)
            link(tt_(t3(r_l), bank[3][:, 0:NE].rearrange("p (t e) -> p t e", t=NTT), bias_b, ALU.add))
            link(nc.vector.tensor_reduce(mx, t3(r_l), AX, ALU.max))
            tt_(t3(r_l), t3(r_l), bc(mx, E), ALU.subtract).then_inc(s_rl, 1)
            dve.wait_ge(s_re, 1)
            link(nc.vector.tensor_reduce(s5, t3(r_p), AX, ALU.add))
            link(nc.vector.reciprocal(s5, s5))
            link(tt_(t3(r_p), t3(r_p), bc(s5, E), ALU.mult))
            pv, p4 = pair.rearrange("p (g s) -> p g s", s=6), t4(r_p)
            n6 = 0
            for i in range(TOPG):
                for j in range(i + 1, TOPG):
                    last = tt_(pv[:, :, n6:n6 + 1], p4[:, :, i:i + 1], p4[:, :, j:j + 1], ALU.add)
                    n6 += 1
            link(last)
            g3 = lambda v: v.rearrange("p (t g) -> p t g", t=NTT)
            link(nc.vector.tensor_reduce(gs, pv, AX, ALU.max))
            link(nc.vector.tensor_reduce(gm, g3(gs), AX, ALU.max))

            def first_max(out, vals, mxv, order, n):
                link(tt_(out, vals, bc(mxv, n), ALU.is_equal))
                link(tt_(out, out, order.unsqueeze(1).broadcast_to([P, NTT, n]), ALU.mult))
                link(nc.vector.tensor_reduce(tf[:, 0:NTT], out, AX, ALU.max))
                link(tt_(out, out, bc(tf[:, 0:NTT], n), ALU.is_equal))

            first_max(g3(g1), g3(gs), gm, small[:, SM_G4:SM_G4 + TOPG], TOPG)
            gmask = g1.unsqueeze(2).broadcast_to([P, NTT * TOPG, TOPG])
            eo = small[:, SM_E16:SM_E16 + E]
            tt_(t4(tmp), p4, gmask, ALU.mult)
            link(ts_(t4(pm), gmask, 1.0, None, ALU.subtract))
            link(tt_(pm, pm, tmp, ALU.add))
            link(nc.vector.tensor_reduce(m1, t3(pm), AX, ALU.max))
            first_max(t3(r_o1), t3(pm), m1, eo, E)
            link(stt(pm, r_o1, -4.0, pm, ALU.mult, ALU.add))
            link(nc.vector.tensor_reduce(m2, t3(pm), AX, ALU.max))
            first_max(t3(r_o2), t3(pm), m2, eo, E)
            link(tt_(tf[:, 8:8 + NTT], m1, m2, ALU.add))
            link(nc.vector.reciprocal(tf[:, 8:8 + NTT], tf[:, 8:8 + NTT]))
            tt_(gw[:, 0:NTT], m1, tf[:, 8:8 + NTT], ALU.mult)
            link(tt_(gw[:, NTT:2 * NTT], m2, tf[:, 8:8 + NTT], ALU.mult))
            val = small[:, SM_VAL:SM_VAL + NTT].unsqueeze(2).broadcast_to([P, NTT, E])
            link(tt_(tmp, r_o1, r_o2, ALU.add))
            tt_(t3(choice), t3(tmp), val, ALU.mult).then_inc(s_oh, 1)
            dve.wait_ge(s_rk, 1)
            nc.vector.tensor_copy(rank, bank[4][:, 0:NE])
            link(nc.vector.tensor_copy(cnt, bank[4][:, NE:NE + E]))
            link(ts_(nb, cnt, float(P), None, ALU.is_gt))
            for j in range(2, NTT):
                link(stt(nb, cnt, float(P * j), nb, ALU.is_gt, ALU.add))
            link(nc.vector.tensor_tensor_scan(ob, ones[:, 0:E], nb, 0.0, ALU.mult, ALU.add))
            link(tt_(on_, ob, nb, ALU.subtract))
            link(ts_(on_, on_, float(P), float(E * P - P), ALU.mult, ALU.add))
            link(tt_(on_, on_, small[:, SM_E128:SM_E128 + E], ALU.subtract))
            link(ts_(big, rank, float(P), None, ALU.is_ge))
            link(tt_(t3(big), t3(big), on_.unsqueeze(1).broadcast_to([P, NTT, E]), ALU.mult))
            link(tt_(rank, rank, big, ALU.add))
            link(tt_(t3(rank), t3(rank), small[:, SM_E128:SM_E128 + E].unsqueeze(1).broadcast_to([P, NTT, E]), ALU.add))
            for n, oh in enumerate((r_o1, r_o2)):
                link(tt_(tmp, rank, oh, ALU.mult))
                link(nc.vector.tensor_reduce(slot_f[:, n * NTT:(n + 1) * NTT], t3(tmp), AX, ALU.add))
            nc.vector.tensor_copy(slot_i[:, :], slot_f).then_inc(s_slot, 1)
            link(nc.vector.tensor_copy(tf[:, 0:1], ob[:, E - 1:E]))
            for v in range(NOV):
                link(ts_(tmp[:, 0:E], ob, float(v), None, ALU.is_le))
                link(nc.vector.tensor_reduce(tf[:, 1 + v:2 + v], tmp[:, 0:E], AX, ALU.add))
            link(ts_(tf[:, 1:1 + NOV], tf[:, 1:1 + NOV], float(E - 1), None, ALU.min))
            nc.vector.tensor_copy(itab[:, 0:1 + NOV], tf[:, 0:1 + NOV]).then_inc(s_slot, 2)
            dve.wait_ge(s_slot, 3)

            def mlo(bi, j):
                dve.wait_ge(m_hi, count_of(bi, j))
                tt_(split[j % 3][1], raw[j], f(split[j % 3][0]), ALU.subtract).then_inc(m_lo, 1)

            def x_lo(bi, par):
                for c in range(2):
                    dve.wait_ge(m_th, 2 * bi + c + 1)
                    tt_(xgT[par][1][:, 4 * c:4 * c + 4, :], bank[c][:, :].rearrange("p (k t) -> p k t", k=4),
                        f(xgT[par][0][:, 4 * c:4 * c + 4, :]), ALU.subtract).then_inc(m_tl, 1)

            def h_lo(bi):
                dve.wait_ge(m_hh, bi + 1)
                tt_(hT[1][:, :, :], bank[4][:, :].rearrange("p (k t) -> p k t", k=4), f(hT[0][:, :, :]),
                    ALU.subtract).then_inc(m_hl, 1)

            def y_half(bi, par):
                dve.wait_ge(m_use, down_count(bi))
                if not (isinstance(bi, int) and bi < 2):
                    dve.wait_ge(m_st[par], store_count(bi, par))
                nc.vector.tensor_copy(ysb[par][:, 512:D], bank[6][:, :]).then_inc(m_yd, 1)

            def hidden(bi):
                dve.wait_ge(m_use, up_count(bi))
                dve.wait_ge(m_sg, bi + 1)
                if not (isinstance(bi, int) and bi == 0):
                    dve.wait_ge(m_ht, bi)
                tt_(hbuf, silu_g, bank[3][:, :], ALU.mult).then_inc(m_h, 1)

            def step(bi, par):
                first, last = isinstance(bi, int) and bi == 0, isinstance(bi, int) and bi == E - 1
                if not first:
                    mlo(bi, 2)
                    h_lo(bi - 1)
                    mlo(bi, 3)
                mlo(bi, 4)
                mlo(bi, 5)
                if not last:
                    mlo(bi + 1, 0)
                if not first:
                    y_half(bi - 1, 1 - par)
                if not last:
                    x_lo(bi + 1, 1 - par)
                    mlo(bi + 1, 1)
                hidden(bi)

            mlo(0, 0)
            mlo(0, 1)
            x_lo(0, 0)
            step(0, 0)
            step(1, 1)
            step(2, 0)
            with dve.Fori(0, (E - 4) // 2) as i:
                step(2 * i + 3, 1)
                step(2 * i + 4, 0)
            step(E - 1, 1)
            mlo(E, 2)
            h_lo(E - 1)
            mlo(E, 3)
            y_half(E - 1, 1)
            dve.wait_ge(s_slot, 3)
            n_over = dve.value_load(itab[0:1, 0:1], min_val=0, max_val=NOV)
            with dve.Fori(0, NOV // 2) as i:
                for par in range(2):
                    v = 2 * i + par
                    with dve.If(v < n_over):
                        x_lo(E + v, par)
                        for s, j in enumerate(OV_ORDER):
                            if s == 4:
                                h_lo(E + v)
                            dve.wait_ge(m_hi, 6 * E + 6 * v + s + 1)
                            tt_(split[s % 3][1], raw[j], f(split[s % 3][0]), ALU.subtract).then_inc(m_lo, 1)
                            if s == 3:
                                dve.wait_ge(m_ht, E + v)
                                dve.wait_ge(m_use, 6 * E + 6 * v + 4)
                                dve.wait_ge(m_sg, E + v + 1)
                                tt_(hbuf, silu_g, bank[3][:, :], ALU.mult).then_inc(m_h, 1)
                        dve.wait_ge(m_use, 6 * E + 6 * v + 6)
                        dve.wait_ge(m_st[par], 16 * (E // 2) + 16 * i)
                        nc.vector.tensor_copy(ysb[par][:, 512:D], bank[6][:, :]).then_inc(m_yd, 1)
            dve.wait_ge(s_ga, 32 * NTT)
            for n, y in enumerate((y_a, y_b)):
                for tt in range(NTT):
                    rows = P if tt < 4 else NS
                    g = gw[0:rows, n * NTT + tt:n * NTT + tt + 1]
                    if n == 0:
                        link(ts_(xr[0:rows, tt, :], xr[0:rows, tt, :], ALPHA, None, ALU.mult))
                    link(stt(xr[0:rows, tt, :], y[0:rows, tt, :], g, xr[0:rows, tt, :], ALU.mult, ALU.add))
            norm_stats(xr, s_fvar)
            dve.wait_ge(s_fstd, 1)
            link(nc.vector.reciprocal(rt[:, 0:NTT], rt[:, 0:NTT]))
            for tt in range(NTT):
                link(ts_(xr[:, tt, :], xr[:, tt, :], mv1[:, tt, 0:1], rt[:, tt:tt + 1], ALU.subtract, ALU.mult))
                link(tt_(xr[:, tt, :], xr[:, tt, :], ln[:, 2, :], ALU.mult))
                tt_(y_a[:, tt, :], xr[:, tt, :], ln[:, 3, :], ALU.add).then_inc(s_y1, 1)

        @block.tensor
        def _(pe):
            mm, tr = nc.tensor.matmul, nc.tensor.transpose
            pe.wait_ge(s_const, 32)
            pe.wait_ge(s_x, 32)
            for m in range(2 * NTT):
                tt, hf = m // 2, m % 2
                rows = P if tt < 4 else NS
                if m >= 2:
                    pe.wait_ge(s_xl, m - 1)
                for j in range(4):
                    kt = 4 * hf + j
                    last = tr(bank[4 + m % 2][:, j * rows:(j + 1) * rows], xn[0:rows, tt, kt * P:(kt + 1) * P],
                              ident[0:rows, 0:rows])
                last.then_inc(s_xt, 1)
            pe.wait_ge(s_par, 64)
            tr(bank[7][:, 0:84], sq[0:84, 0, 0:P], ident[0:84, 0:84]).then_inc(s_pt, 1)
            pe.wait_ge(s_xl, 2 * NTT)
            pe.wait_ge(s_pp, 1)

            def project(o):
                pe.wait_ge(s_lo, o + 1)
                wh, wl = chunk_weights(o % 2, 0), chunk_weights(o % 2, 1)
                for n in tiles_of(o):
                    kind, _, j = TILES[n]
                    if n >= 2:
                        wait_evacuated(pe, n - 2)
                    pb, ps = bank[n % 2], bank[2 + n % 2]
                    if kind == "v":
                        rows = P if j < 4 else NS
                        for kt in range(KT):
                            for i, (x_, w_) in enumerate(((0, wh), (0, wl), (1, wh))):
                                last = mm(pb[0:rows, 0:CW], xT[x_][:, kt, tok(j)], w_[:, kt, :],
                                          start=(kt == 0 and i == 0), stop=(kt == KT - 1 and i == 2))
                    else:
                        for kt in range(KT):
                            for i, (w_, x_) in enumerate(((wh, 0), (wh, 1), (wl, 0))):
                                first, end = kt == 0 and i == 0, kt == KT - 1 and i == 2
                                lhs = w_[:, kt, j * P:(j + 1) * P]
                                mm(pb[:, :], lhs, xT[x_][:, kt, 0:SEQ], start=first, stop=end)
                                last = mm(ps[:, 0:NS], lhs, xT[x_][:, kt, SEQ:T], start=first, stop=end)
                    last.then_inc(s_tile, 1)

            def pairs(li):
                if li == 0:
                    pe.wait_ge(s_eva, 8)
                else:
                    pe.wait_ge(s_z, li)
                lf, rf = (k, q) if li == 0 else (ex[(li - 1) % 2], ex[(li - 1) % 2])
                if li <= SLEVELS:
                    if li:
                        pe.wait_ge(s_ps, li)
                    for h in range(H):
                        last = mm(bank[7][0:NS, h * NS:(h + 1) * NS], lf[:, h, SEQ:T], rf[:, h, SEQ:T], start=True, stop=True)
                for h in range(H):
                    p = li * H + h
                    if p >= 3:
                        pe.wait_ge(s_pc, p - 2)
                    for c in range(NC):
                        cols = slice(c * P, (c + 1) * P)
                        last = mm(bank[4 + p % 3][:, cols], lf[:, h, cols], rf[:, h, cols], start=True, stop=True)
                    last.then_inc(s_p, 1)

            for o_ in range(NCH):
                project(o_)
                if 0 <= o_ - 5 <= LEVELS:
                    pairs(o_ - 5)

            pe.wait_ge(s_cb, 4)
            pe.wait_ge(s_ps, SLEVELS + 1)
            for j in range(4):
                last = tr(bank[7][0:18, j * P:(j + 1) * P], cb[:, j, :], ident)
            last.then_inc(s_cbt, 1)
            pe.wait_ge(s_kx, 1)
            for m in range(H + 1):
                pe.wait_ge(s_pc, NP_LEVELS)
                if m >= 3:
                    pe.wait_ge(s_ktc, m - 2)
                pb = bank[4 + (NP_LEVELS + m) % 3]
                if m < H:
                    for c in range(NC):
                        last = tr(pb[:, c * P:(c + 1) * P], k[:, m, c * P:(c + 1) * P], ident)
                else:
                    for h in range(H):
                        last = tr(pb[0:NS, h * P:(h + 1) * P], k[:, h, SEQ:T], ident)
                last.then_inc(s_kt, 1)
            for n in (len(TILES) - 2, len(TILES) - 1):
                wait_evacuated(pe, n)
            pe.wait_ge(s_ktc, H + 1)
            pe.wait_ge(s_qx, 1)
            for c in range(NC):
                cols = slice(c * P, (c + 1) * P)
                if c >= 2:
                    pe.wait_ge(s_st, c - 1)
                for h in range(H):
                    last = mm(bank[4 + c % 2][:, h * P:(h + 1) * P], k_tok[:, h, c, :], v_tok[:, c, h * P:(h + 1) * P],
                              start=True, stop=True)
                last.then_inc(s_su, 1)
                if c:
                    pe.wait_ge(s_st, c)
                for h in range(H):
                    last = mm(bank[h][:, cols], v_tok[:, c, h * P:(h + 1) * P], att[:, h, c, :], start=True, stop=(c == 0))
                    if c:
                        last = mm(bank[h][:, cols], state[:, c - 1, h, :], q[:, h, cols], start=False, stop=True)
                    if c == NC - 1:
                        last.then_inc(s_o, 1)
            pe.wait_ge(s_cbo, 1)
            pe.wait_ge(s_s0, 16)
            for h in range(H):
                mm(bank[7][:, h * NS:(h + 1) * NS], v_tok[0:NS, 4, h * P:(h + 1) * P], att_s[0:NS, h, :],
                   start=True, stop=False, skip_group_check=True)
                for bi in range(DB):
                    t0 = DS * bi
                    last = mm(bank[7][:, h * NS + t0:h * NS + t0 + DS], s0[:, bi, h, :], q[:, h, SEQ + t0:SEQ + t0 + DS],
                              start=False, stop=(bi == DB - 1), skip_group_check=True)
            last.then_inc(s_o, 1)
            pe.wait_ge(s_st, NC)
            for h in range(H):
                pe.wait_ge(s_vm, h + 1)
                for g in range(2):
                    n = 2 * h + g
                    if n >= 2:
                        pe.wait_ge(s_s0n, 4 * (n - 1))
                    mm(bank[4 + n % 2][:, :], k_tok_s[0:NS, h, :], v_msk[0:NS, 4 * g:4 * g + 4, :],
                       start=True, stop=True).then_inc(s_sus, 1)
            for g in range(2):
                pe.wait_ge(s_sq, g + 1)
                for m in range(H + 1):
                    if g:
                        pe.wait_ge(s_rt_, m + 1)
                    w = blk_ones if g == 0 else ones
                    if m < H:
                        mm(norm_bank(m)[:, :], w, sq[:, m, 0:SEQ], start=True, stop=True).then_inc(s_ms, 1)
                    else:
                        mm(norm_bank(m)[:, 0:H * NS], w, sq[:, :, SEQ:T], start=True, stop=True).then_inc(s_ms, 1)
            pe.wait_ge(s_cat_l, 8)
            pe.wait_ge(s_rt_, 2 * (H + 1))
            for c in range(NWO):
                pe.wait_ge(s_lo, NCH + c + 1)
                wh, wl = chunk_weights((NCH + c) % 2, 0), chunk_weights((NCH + c) % 2, 1)
                for tt in range(NTT):
                    n = c * NTT + tt
                    rows = P if tt < 4 else NS
                    if n >= 4:
                        pe.wait_ge(s_wc, n - 3)
                    for kt in range(KT):
                        for i, (x_, w_) in enumerate(((0, wh), (0, wl), (1, wh))):
                            last = mm(bank[n % 4][0:rows, 0:CW], xT[x_][:, kt, tok(tt)], w_[:, kt, :],
                                      start=(kt == 0 and i == 0), stop=(kt == KT - 1 and i == 2))
                    last.then_inc(s_w, 1)
            pe.wait_ge(s_wc, NWO * NTT)
            pe.wait_ge(s_wr, 32)
            for tt in range(NTT):
                pe.wait_ge(s_x1, tt + 1)
                for hf in range(2):
                    m = 2 * tt + hf
                    if m >= 2:
                        pe.wait_ge(s_1c, m - 1)
                    for j in range(4):
                        kt = 4 * hf + j
                        last = tr(bank[4 + m % 2][:, j * P:(j + 1) * P], xr[:, tt, kt * P:(kt + 1) * P], ident)
                    last.then_inc(s_1t, 1)
                pe.wait_ge(s_1c, 2 * tt + 2)
                for kt in range(KT):
                    last = mm(bank[3][:, tt * E:(tt + 1) * E], x1T[tt % 2][:, kt, :], wr[:, kt, :],
                              start=(kt == 0), stop=(kt == KT - 1))
                last.then_inc(s_lg, 1)
            pe.wait_ge(s_oh, 1)
            for tt in range(NTT):
                for j in range(tt + 1):
                    mm(bank[4][:, tt * E:(tt + 1) * E], tri if j == tt else ones, choice[:, j * E:(j + 1) * E],
                       start=(j == 0), stop=(j == tt))
            for j in range(NTT):
                last = mm(bank[4][:, NE:NE + E], ones, choice[:, j * E:(j + 1) * E], start=(j == 0), stop=(j == NTT - 1))
            last.then_inc(s_rk, 1)

            def x_turn(bi, par):
                pe.wait_ge(m_xg[par], 8 * (bi - par) + 16)
                if not (isinstance(bi, int) and bi == 0):
                    pe.wait_ge(m_tl, 2 * bi)
                for c in range(2):
                    for t in range(4):
                        last = tr(bank[c][:, t * P:(t + 1) * P], xg[par][:, c * 512 + t:(c + 1) * 512:4], ident)
                last.then_inc(m_t, 1)

            def gate_up(out, par, slot, c, wait):
                pe.wait_ge(m_lo, wait)
                w = [split[slot][i].rearrange("p (t n) -> p t n", t=4) for i in range(2)]
                for t in range(4):
                    kt = 4 * c + t
                    for i, (x_, w_) in enumerate(((0, 0), (0, 1), (1, 0))):
                        last = mm(out[:, :], xgT[par][x_][:, kt, :], w[w_][:, t, :],
                                  start=(kt == 0 and i == 0), stop=(kt == KT - 1 and i == 2))
                last.then_inc(m_use, 1)

            def down(slot, c, wait):
                pe.wait_ge(m_lo, wait)
                w = [split[slot][i].rearrange("p (t n) -> p t n", t=2) for i in range(2)]
                for t in range(2):
                    kt = 2 * c + t
                    for i, (x_, w_) in enumerate(((0, 0), (0, 1), (1, 0))):
                        for g in range(2):
                            last = mm(bank[5 + g][:, :], hT[x_][:, kt, :], w[w_][:, t, 512 * g:512 * g + 512],
                                      start=(kt == 0 and i == 0), stop=(kt == 3 and i == 2))
                last.then_inc(m_use, 1)

            def h_turn(bi):
                pe.wait_ge(m_h, bi + 1)
                if not (isinstance(bi, int) and bi == 0):
                    pe.wait_ge(m_hl, bi)
                for kt in range(4):
                    c, t = kt // 2, kt % 2
                    last = tr(bank[4][:, kt * P:(kt + 1) * P], hbuf[:, c * 256 + t:(c + 1) * 256:2], ident)
                last.then_inc(m_ht, 1)

            def down_ready(bi):
                pe.wait_ge(m_hl, bi + 1)
                if not (isinstance(bi, int) and bi == 0):
                    pe.wait_ge(m_ya, bi)
                    pe.wait_ge(m_yd, bi)

            def step(bi, par):
                first, last = isinstance(bi, int) and bi == 0, isinstance(bi, int) and bi == E - 1
                pe.wait_ge(m_tl, 2 * bi + 2)
                if not first:
                    pe.wait_ge(m_sg, bi)
                gate_up(bank[2], par, 0, 0, count_of(bi, 0))
                if not first:
                    h_turn(bi - 1)
                gate_up(bank[2], par, 1, 1, count_of(bi, 1))
                if not first:
                    down_ready(bi - 1)
                    down(2, 0, count_of(bi, 2))
                    down(0, 1, count_of(bi, 3))
                if not last:
                    x_turn(bi + 1, 1 - par)
                gate_up(bank[3], par, 1, 0, count_of(bi, 4))
                gate_up(bank[3], par, 2, 1, count_of(bi, 5))

            x_turn(0, 0)
            step(0, 0)
            step(1, 1)
            step(2, 0)
            with pe.Fori(0, (E - 4) // 2) as i:
                step(2 * i + 3, 1)
                step(2 * i + 4, 0)
            step(E - 1, 1)
            h_turn(E - 1)
            down_ready(E - 1)
            down(2, 0, count_of(E, 2))
            down(0, 1, count_of(E, 3))
            pe.wait_ge(s_slot, 3)
            n_over = pe.value_load(itab[0:1, 0:1], min_val=0, max_val=NOV)
            with pe.Fori(0, NOV // 2) as i:
                for par in range(2):
                    v = 2 * i + par
                    with pe.If(v < n_over):
                        base = 6 * E + 6 * v
                        x_turn(E + v, par)
                        pe.wait_ge(m_tl, 2 * (E + v) + 2)
                        pe.wait_ge(m_sg, E + v)
                        gate_up(bank[2], par, 0, 0, base + 1)
                        gate_up(bank[2], par, 1, 1, base + 2)
                        gate_up(bank[3], par, 2, 0, base + 3)
                        gate_up(bank[3], par, 0, 1, base + 4)
                        h_turn(E + v)
                        down_ready(E + v)
                        down(1, 0, base + 5)
                        down(2, 1, base + 6)


_INS = ["x_prompt", "x_sample", "state_hgrn", "state_conv", "w_in", "w_out", "hgrn_norm_g", "conv_w", "conv_norm_g",
        "ln1_g", "ln1_b", "ln2_g", "ln2_b", "w_router", "router_bias", "w_gate", "w_up", "w_down"]
_OUTS = [("out_prompt", (1, SEQ, D)), ("out_sample", (DB, DS, D)), ("out_hgrn_prompt", (1, 1, H, P, P)),
         ("out_conv_prompt", (1, 1, 2, 512)), ("out_hgrn_sample", (1, DB, H, P, P)), ("out_conv_sample", (1, DB, 2, 512))]


def kernel(**inputs):
    import concourse.bacc as bacc
    from concourse.bass_utils import run_bass_kernel_spmd

    nc = bacc.Bacc("TRN2", target_bir_lowering=False, num_devices=1)
    const_f32, const_mask = constants()
    arrays = {name: np.ascontiguousarray(inputs[name]) for name in _INS}
    arrays["const_f32"], arrays["const_mask"] = const_f32, const_mask
    aps = {name: nc.dram_tensor(name, x.shape, mybir.dt.from_np(x.dtype), kind="ExternalInput").ap()
           for name, x in arrays.items()}
    for name, shape in _OUTS:
        aps[name] = nc.dram_tensor(name, shape, F32, kind="ExternalOutput").ap()
    build(nc, aps)
    r = run_bass_kernel_spmd(nc, [arrays], core_ids=[0])
    return tuple(r.results[0][name] for name, _ in _OUTS)
```

```python
from contextlib import ExitStack

import numpy as np

import concourse.bass as bass
from concourse import mybir

F32 = mybir.dt.float32
F32R = mybir.dt.float32r
U8 = mybir.dt.uint8
I32 = mybir.dt.int32
U32 = mybir.dt.uint32
ALU = mybir.AluOpType
ACT = mybir.ActivationFunctionType
AX = mybir.AxisListType.X

P = 128
D = 1024
KT = D // P
SEQ, DB, DS = 512, 8, 4
NS = DB * DS
T = SEQ + NS
HT = T // 2
NTT = (T + P - 1) // P
H = 4
NC = SEQ // P
LEVELS = 7
SLEVELS = 2
CW = 256
N_IN = 3584
NCH = N_IN // CW
NWO = D // CW
UW = 2 + SEQ + DB * (2 + DS)
E, TOPG, FF = 16, 4, 512
NOV = 8
NBLK = E + NOV
ALPHA = float(2 ** 0.25)
LN_EPS, RMS_EPS = 1e-5, 1e-6

ORDER = [("f", 2), ("f", 3), ("q", 0), ("q", 1), ("v", 4), ("v", 5), ("gc", 10), ("gc", 11),
         ("cx", 12), ("cx", 13), ("gb", 8), ("gb", 9), ("g", 6), ("g", 7)]


TOKEN_MAJOR = ("v", "g")


def out_tiles():
    out = []
    for o, (kind, _) in enumerate(ORDER):
        out += [(kind, o, j) for j in range(NTT if kind in TOKEN_MAJOR else CW // P)]
    return out


TILES = out_tiles()
POOL_LN = 3
BY_DVE = ("cx", "gb")
FIRST_LEVEL_STEP = 5

C_ID, C_TRI, C_ONE, C_SEL, C_RST, C_SM = 0, 128, 256, 384, 416, 416 + T
C_QM = C_SM + 80
C_N = C_QM + DB * NS
SM_E16, SM_E128, SM_G4, SM_VAL, SM_SEQ, SM_IOTA = 0, 16, 32, 36, 41, 49


def constants():
    p = np.arange(P)
    c = np.zeros((P, C_N), np.float32)
    c[:, C_ID:C_ID + P] = np.eye(P)
    c[:, C_TRI:C_TRI + P] = p[:, None] < p[None, :]
    for j in range(4):
        c[:, C_SEL + 8 * j:C_SEL + 8 * j + 8] = 2 * j + p[:, None] // 64 == np.arange(8)[None, :]
    c[:, C_ONE:C_ONE + P] = 1.0
    t = np.arange(T)
    c[:, C_RST:C_RST + T] = np.where(t < SEQ, t % P != 0, (t - SEQ) % DS != 0)
    s = c[:, C_SM:]
    s[:, SM_E16:SM_E16 + E] = E - np.arange(E)
    s[:, SM_E128:SM_E128 + E] = P * np.arange(E)
    s[:, SM_G4:SM_G4 + TOPG] = TOPG - np.arange(TOPG)
    s[:, SM_VAL:SM_VAL + NTT] = (np.arange(NTT)[None, :] * P + p[:, None]) < T
    s[:, SM_SEQ:SM_SEQ + DB] = (p[:, None] // DS) == np.arange(DB)[None, :]
    s[:, SM_IOTA:SM_IOTA + NOV] = np.arange(NOV)
    c[:, C_QM:] = (np.arange(NS)[None, :] // DS == np.arange(DB)[:, None]).reshape(1, -1)
    m = np.zeros((P, LEVELS, P), np.float32)
    for l in range(LEVELS):
        L = 1 << l
        m[:, l, :] = ((p[:, None] // (2 * L) == p[None, :] // (2 * L)) & (p[:, None] % (2 * L) < L)
                      & (p[None, :] % (2 * L) >= L))
    return c, m.reshape(P, LEVELS * P)


def build(nc, a):
    ctx = ExitStack()

    def sem(name):
        return ctx.enter_context(nc.semaphore(name))

    with ctx:
        xg_dram = nc.dram_tensor("x_by_slot", (NBLK * P, D), F32, kind="Internal").ap()
        yg_dram = nc.dram_tensor("y_by_slot", (NBLK * P, D), F32, kind="Internal").ap()

        FW = 35472
        FA = ctx.enter_context(nc.sbuf_tensor("FA", [P, FW], F32))
        RA = ctx.enter_context(nc.sbuf_tensor("RA", [P, 68 * 256], F32R))
        masks = ctx.enter_context(nc.sbuf_tensor("masks", [P, LEVELS * P], U8))
        itab = ctx.enter_context(nc.sbuf_tensor("itab", [P, 16], I32))
        slot_i = ctx.enter_context(nc.sbuf_tensor("slot_i", [P, 2 * NTT], I32))
        bank = [ctx.enter_context(nc.psum_tensor(f"bank{i}", [P, 512], F32)) for i in range(8)]

        def fa(off, n):
            return FA[:, off:off + n]

        const = fa(0, C_N)
        ident, tri = const[:, C_ID:C_ID + P], const[:, C_TRI:C_TRI + P]
        ones = const[:, C_ONE:C_ONE + P]
        groups = const[:, C_SEL:C_SEL + 32].rearrange("p (j g) -> p j g", j=4)
        reset = const[:, C_RST:C_RST + T]
        groups_t = const[0:8, C_RST:C_RST + 4 * P].rearrange("p (j c) -> p j c", j=4)
        small = const[:, C_SM:C_SM + 80]
        o_small = C_N
        params = fa(o_small, 88)
        p_decay = fa(o_small + 88, H * NC).rearrange("p (h c) -> p h c", h=H)
        s0_decay = fa(o_small + 88 + H * NC, DB * H)
        rt = fa(o_small + 136, 464)
        assert o_small + 600 <= 2048
        K = 256
        raw = [fa(8 * K + 2048 * i, 2048) for i in range(6)]
        s0 = fa(32 * K, 4096).rearrange("p (b h v) -> p b h v", b=DB, h=H)
        A0 = 48 * K
        xn = fa(A0, NTT * D).rearrange("p (t n) -> p t n", t=NTT)
        v_tok = fa(A0, NTT * 512).rearrange("p (t n) -> p t n", t=NTT)
        sg = fa(A0 + NTT * 512, NTT * 512).rearrange("p (t n) -> p t n", t=NTT)
        Q0 = 68 * K
        heads = lambda off: fa(off, H * T).rearrange("p (h t) -> p h t", h=H)
        q, k, b = heads(Q0), heads(Q0 + H * T), heads(Q0 + 2 * H * T)
        Z0 = Q0 + 3 * H * T
        z = heads(Z0)
        yc = heads(Z0)
        E0 = Z0 + H * T
        ex = [heads(E0), heads(E0 + H * T)]
        AT0 = E0 + 2 * H * T
        att = fa(AT0, H * NC * P).rearrange("p (h c t) -> p h c t", h=H, c=NC)
        att_s = fa(AT0 + H * NC * P, H * NS).rearrange("p (h t) -> p h t", h=H)
        U0 = AT0 + H * NC * P + H * NS
        u = fa(U0, 4 * UW).rearrange("p (j t) -> p j t", j=4)
        sq = heads(U0)
        SQ0 = U0 + 4 * UW
        cb = fa(SQ0, 4 * 18).rearrange("p (j t) -> p j t", j=4)
        cb_out = fa(SQ0 + 72, 512)
        assert SQ0 + 72 + 512 <= FW, (SQ0 + 584, FW)
        k_tok = fa(E0 + H * T, H * NC * P).rearrange("p (h c k) -> p h c k", h=H, c=NC)
        state = fa(E0, NC * H * P).rearrange("p (c h v) -> p c h v", c=NC, h=H)
        k_tok_s = fa(Q0 + H * T, 512).rearrange("p (h k) -> p h k", h=H)
        v_msk = fa(Q0 + H * T + 512, DB * P).rearrange("p (b v) -> p b v", b=DB)
        h_gain = fa(Q0 + H * T + 1536, 512)
        B0 = Q0 + 2 * H * T
        o_sq = [fa(B0, 512), fa(B0 + 512, 512)]
        o_n = [fa(B0 + 1024, 512), fa(B0 + 1536, 512)]
        q_msk = fa(U0, H * DB * NS).rearrange("p (h b t) -> p h b t", h=H, b=DB)
        r_conv = fa(B0 + 1024, T)[0:8, :]
        xr = fa(E0, NTT * D).rearrange("p (t n) -> p t n", t=NTT)
        ln = fa(Q0, 4 * D).rearrange("p (i n) -> p i n", i=4)
        x1T = [fa(U0, 2 * D).rearrange("p (k t) -> p k t", k=KT),
               fa(B0, 2 * D).rearrange("p (k t) -> p k t", k=KT),
               fa(Z0 + 1024, KT * NS).rearrange("p (k t) -> p k t", k=KT)]
        lg = fa(Z0 + 1024 + KT * NS, T)[0:E, :]
        xg = [fa(56 * K, D), fa(60 * K, D)]
        wr = fa(Z0, KT * E).rearrange("p (k e) -> p k e", k=KT)
        silu_g, hbuf = fa(64 * K, 512), fa(66 * K, 512)
        ysb = [fa(U0, D), fa(U0 + D, D)]
        y_a, y_b = fa(8 * K, NTT * D).rearrange("p (t n) -> p t n", t=NTT), \
            fa(28 * K, NTT * D).rearrange("p (t n) -> p t n", t=NTT)

        split = [[RA[:, (8 * (2 * s + w)) * K:(8 * (2 * s + w) + 8) * K] for w in range(2)] for s in range(3)]
        xT = [RA[:, 32 * K + w * KT * T:32 * K + (w + 1) * KT * T].rearrange("p (k t) -> p k t", k=KT)
              for w in range(2)]
        xgT = [[RA[:, (48 + 8 * par + 4 * w) * K:(52 + 8 * par + 4 * w) * K].rearrange("p (k t) -> p k t", k=KT)
                for w in range(2)] for par in range(2)]
        hT = [RA[:, (64 + 2 * w) * K:(66 + 2 * w) * K].rearrange("p (k t) -> p k t", k=4) for w in range(2)]

        s_const, s_mask, s_par, s_s0 = sem("const_in"), sem("mask_in"), sem("param_in"), sem("s0_in")
        s_x = [sem(f"x_in{i}") for i in range(NTT)]
        s_raw = [sem(f"raw_in{i}") for i in range(3)]
        s_hi, s_lo, s_tile = sem("hi_done"), sem("lo_done"), sem("tile_made")
        s_eva, s_evd = sem("evacuated_by_act"), sem("evacuated_by_dve")
        s_xt, s_xh, s_xl = sem("x_transposed"), sem("xT_hi"), sem("xT_lo")
        s_pt, s_pp = sem("param_transposed"), sem("param_ready")
        s_zero, s_fill = sem("zero_tile"), sem("slots_filled")
        s_abs, s_lnf, s_b = sem("abs_z"), sem("ln1p"), sem("b_ready")
        s_d, s_e, s_z, s_p, s_pc = sem("exponent"), sem("decay"), sem("decayed_qk"), sem("pairs"), sem("pairs_used")
        s_ps = sem("sample_pairs_used")
        s_qx, s_kx = sem("q_decayed"), sem("k_decayed")
        s_cb, s_cbt, s_cbo, s_cbs = sem("conv_tail"), sem("conv_tail_t"), sem("conv_tail_out"), sem("conv_state_stored")
        s_kt, s_ktc = sem("k_transposed"), sem("k_token_major")
        s_su, s_st, s_o, s_oc = sem("state_update"), sem("state_ready"), sem("o_made"), sem("o_copied")
        s_vm, s_sus, s_s0n, s_sto = sem("v_masked"), sem("sample_update"), sem("sample_state"), sem("sample_states_stored")
        s_stp = sem("prompt_state_stored")
        s_selt, s_sel = sem("groups_transposed"), sem("groups_t_ready")
        s_csq, s_cms, s_crt, s_crc, s_cbc = (sem("conv_squares"), sem("conv_mean_square"), sem("conv_root"),
                                             sem("conv_reciprocal"), sem("conv_scale_spread"))
        s_cf, s_ch, s_cl = sem("conv_row_f32"), sem("conv_row_hi"), sem("conv_row_lo")
        s_hg, s_sg = sem("o_gain_in"), sem("silu_g_scaled")
        s_qm = sem("q_masked")
        s_osq, s_red, s_ort, s_on, s_ot, s_oh_, s_ol = (sem("o_squares"), sem("o_mean_square"), sem("o_root"), sem("o_normed"),
                                                       sem("o_transposed"), sem("o_hi"), sem("o_lo"))
        s_s0d = sem("s0_decayed")
        s_xr, s_lnp, s_lnp2, s_wr = sem("residual_in"), sem("ln1_params_in"), sem("ln2_params_in"), sem("router_in")
        s_xr0 = sem("residual_zeroed")
        s_w, s_wc = sem("mix_out"), sem("mix_added")
        s_var, s_std, s_nm, s_nrm, s_xgn, s_x1, s_x1d = (sem("ln_var"), sem("ln_std"), sem("ln_shift"), sem("ln_normed"),
                                                  sem("ln_scaled"), sem("ln_out_by_pool"), sem("ln_out_by_dve"))
        s_1t, s_1c, s_lgt, s_lgs, s_lg = (sem("x1_transposed"), sem("x1T_copied"), sem("logits_expert_major"),
                                                 sem("logits_copied"), sem("logits_token_major"))
        s_rl, s_re = sem("logit_shifted"), sem("logit_exp")
        s_oh, s_rk, s_slot, s_sc = sem("choice"), sem("rank"), sem("slots"), sem("rows_scattered")
        s_dv, s_ac = sem("dve_chain"), sem("act_chain")
        m_raw = [sem(f"moe_raw_in{i}") for i in range(6)]
        m_xg = [sem(f"moe_x_in{i}") for i in range(2)]
        m_t, m_th, m_tl = sem("moe_x_transposed"), sem("moe_xT_hi"), sem("moe_xT_lo")
        m_hi, m_lo, m_use = sem("moe_hi"), sem("moe_lo"), sem("moe_chunk_used")
        m_sg, m_h, m_ht, m_hh, m_hl = sem("moe_silu"), sem("moe_h"), sem("moe_h_transposed"), sem("moe_hT_hi"), sem("moe_hT_lo")
        m_ya, m_yd = sem("moe_y_act"), sem("moe_y_dve")
        m_st = [sem(f"moe_y_stored{i}") for i in range(2)]
        s_ga = [sem(f"rows_gathered{i}") for i in range(NTT)]
        s_ax, s_fvar, s_fstd, s_fnm, s_fnr, s_fg = (sem("x1_times_alpha"), sem("final_var"), sem("final_std"), sem("final_shift"),
                                                    sem("final_normed"), sem("final_scaled"))
        s_yp, s_y1, s_out = sem("final_out_by_pool"), sem("final_out_by_dve"), sem("out_stored")

        block = ctx.enter_context(nc.Block())

        act_tiles = [n for n, (kind, _, _) in enumerate(TILES) if kind not in BY_DVE]
        dve_tiles = [n for n, (kind, _, _) in enumerate(TILES) if kind in BY_DVE]

        def wait_evacuated(eng, n):
            if n in act_tiles:
                eng.wait_ge(s_eva, act_tiles.index(n) + 1)
            else:
                eng.wait_ge(s_evd, dve_tiles.index(n) + 1)

        def tile_banks(n):
            return (bank[n % 4], None) if TILES[n][0] in TOKEN_MAJOR else (bank[n % 2], bank[2 + n % 2])

        def bank_before(n):
            both = TILES[n][0] in TOKEN_MAJOR and TILES[n - 2][0] in TOKEN_MAJOR
            return n - 4 if both else n - 2

        def tiles_of(o):
            return [n for n, t in enumerate(TILES) if t[1] == o]

        def halves(view, L, n):
            w = view[:, :, 0:n].rearrange("p h (n s l) -> p h n s l", s=2, l=L)
            return w[:, :, :, 0, :], w[:, :, :, 1, :], w[:, :, :, 0, L - 1:L]

        def conv_pieces(h, pb, ps):
            us = u[:, h, 2 + SEQ:UW].rearrange("p (b t) -> p b t", b=DB)
            return [(u[:, h, 2:2 + HT], pb[:, 0:HT]), (u[:, h, 2 + HT:2 + SEQ], ps[:, 0:SEQ - HT]),
                    (us[:, :, 2:2 + DS], ps[:, SEQ - HT:HT].rearrange("p (b t) -> p b t", b=DB))]

        def chunk_weights(s, w):
            return split[s][w].rearrange("p (k n) -> p k n", k=KT)

        def tok(tt):
            return slice(tt * P, min((tt + 1) * P, T))

        NP_LEVELS = (LEVELS + 1) * H

        OV_ORDER = (0, 1, 4, 5, 2, 3)
        mv1 = rt[:, 8:8 + 2 * NTT].rearrange("p (t s) -> p t s", s=2)
        eps_rms, eps_ln = rt[:, 20:21], rt[:, 21:22]
        shift = rt[:, 128:128 + NTT]
        stats = rt[:, 24:24 + 12 * NTT].rearrange("p (t s) -> p t s", t=NTT)
        NE = NTT * E
        ra = lambda i: rt[:, 88 + i * NE:88 + (i + 1) * NE]
        t3 = lambda v: v.rearrange("p (t e) -> p t e", t=NTT)
        t4 = lambda v: v.rearrange("p (x e) -> p x e", e=TOPG)
        r_l, r_p, r_o1, r_o2 = ra(0), ra(1), ra(2), ra(3)
        R0 = Z0 + KT * E
        rb = lambda i, n: fa(R0 + i, n)

        gw = rt[:, 408:418]
        choice = fa(R0 + 640, NE)

        def o_bank(tt):
            return bank[6] if tt == NTT - 1 else bank[tt]

        def w_bank(n):
            return bank[(7, 4, 5, 0)[n % 4]]

        ss, root = rt[:, 88:88 + 4 * NTT], rt[:, 108:108 + 4 * NTT]

        def raw_use(bi, j):
            return bi if j in (2, 3) else bi + 1

        def gate_count(bi):
            return 2 if isinstance(bi, int) and bi == 0 else 6 * bi + 0

        def up_count(bi):
            return 4 if isinstance(bi, int) and bi == 0 else 6 * bi + 4

        def down_count(bi):
            if isinstance(bi, int) and bi == E - 1:
                return 6 * E
            return 6 * (bi + 1) + 2

        def store_count(bi, par):
            return 8 * (bi - par)

        def count_of(bi, j):
            if isinstance(bi, int) and bi == 0:
                return {0: 1, 1: 2, 4: 3, 5: 5}[j]
            if isinstance(bi, int) and bi == 1 and j == 0:
                return 4
            if isinstance(bi, int) and bi == E:
                return 6 * E - 2 + j - 1
            return 6 * bi + j - 1

        def slot_free_count(bi, j):
            if isinstance(bi, int) and bi == 0:
                return 2 if j == 5 else None
            if isinstance(bi, int) and bi == 1 and j < 3:
                return (1, 4, 3)[j]
            if isinstance(bi, int) and bi == E and j == 3:
                return used_count(E - 1, 3)
            if j >= 3:
                return used_count(bi, j - 3)
            return used_count(bi - 1, j + 3)

        def used_count(bi, j):
            if isinstance(bi, int) and bi == 0:
                return {0: 1, 1: 2, 4: 3, 5: 4}[j]
            if isinstance(bi, int) and bi == E:
                return 6 * E - 2 + j - 1
            return 6 * bi + j - 1

        def split_slot(bi, j):
            return {0: 0, 1: 1, 4: 2, 5: 1}[j] if isinstance(bi, int) and bi == 0 else j % 3

        @block.sync
        def _(sp):
            sp.dma_start(const, a["const_f32"]).then_inc(s_const, 16)
            w_in = a["w_in"][0].rearrange("(k p) n -> p k n", p=P)
            w_out = a["w_out"][0].rearrange("(k p) n -> p k n", p=P)

            def load_w(c):
                src = w_in[:, :, ORDER[c][1] * CW:(ORDER[c][1] + 1) * CW] if c < NCH \
                    else w_out[:, :, (c - NCH) * CW:(c - NCH + 1) * CW]
                sp.dma_start(raw[c % 3].rearrange("p (k n) -> p k n", k=KT), src).then_inc(s_raw[c % 3], 16)

            for tt in range(4):
                sp.dma_start(xn[:, tt, :], a["x_prompt"][0, tt * P:(tt + 1) * P, :]).then_inc(s_x[tt], 16)
            sp.dma_start(xn[0:NS, 4, :], a["x_sample"].rearrange("b t n -> (b t) n")).then_inc(s_x[4], 16)
            load_w(0)
            pr = sq[:, 0, 0:P]
            sp.dma_start(fa(E0, LEVELS * P), a["const_mask"]).then_inc(s_mask, 16)
            sp.dma_start(pr[0:4, :], a["hgrn_norm_g"].rearrange("a (t p) -> (a t) p", p=P)).then_inc(s_par, 16)
            sp.dma_start(pr[4:16, :], a["conv_w"].rearrange("a j (t p) -> (a j t) p", p=P)).then_inc(s_par, 16)
            sp.dma_start(pr[16:20, :], a["conv_norm_g"].rearrange("a (t p) -> (a t) p", p=P)).then_inc(s_par, 16)
            sp.dma_start(pr[20:84, :], a["state_conv"].rearrange("a b j (t p) -> (a b j t) p", p=P)).then_inc(s_par, 16)
            for c in range(1, NCH + NWO):
                if c >= 3:
                    sp.wait_ge(s_lo, c - 2)
                load_w(c)
                if c == NCH:
                    sp.wait_ge(s_fill, 64)
                    sp.dma_start(s0, a["state_hgrn"][0].rearrange("b h k v -> k b h v")).then_inc(s_s0, 16)
            sp.wait_ge(s_cbo, 1)
            sp.dma_start(a["out_conv_prompt"][0, 0, :, :], cb_out[0:2, :]).then_inc(s_cbs, 16)
            sp.dma_start(a["out_conv_sample"][0].rearrange("b j n -> (b j) n"), cb_out[2:18, :]).then_inc(s_cbs, 16)
            sp.wait_ge(s_kt, H + 1)
            sp.dma_start(h_gain, a["hgrn_norm_g"].broadcast_to([P, 512])).then_inc(s_hg, 16)
            sp.wait_ge(s_st, NC)
            sp.dma_start(a["out_hgrn_prompt"][0, 0].rearrange("h k v -> k h v"), state[:, NC - 1, :, :]).then_inc(s_stp, 16)
            sp.wait_ge(s_stp, 16)
            sp.wait_ge(s_o, NTT)
            sp.wait_ge(s_xr0, 1)
            sp.dma_start(xr[:, 0:4, :], a["x_prompt"][0].rearrange("(t p) n -> p t n", p=P)).then_inc(s_xr, 16)
            sp.dma_start(xr[0:NS, 4, :], a["x_sample"].rearrange("b t n -> (b t) n")).then_inc(s_xr, 16)
            for i, name in enumerate(("ln1_g", "ln1_b")):
                sp.dma_start(ln[:, i, :], a[name].broadcast_to([P, D])).then_inc(s_lnp, 16)
            sp.wait_ge(s_cl, 4)
            sp.dma_start(wr, a["w_router"].rearrange("(k p) e -> p k e", p=P)).then_inc(s_wr, 16)
            sp.dma_start(rt[:, 448:464], a["router_bias"].unsqueeze(0).broadcast_to([P, E])).then_inc(s_wr, 16)
            sp.wait_ge(s_s0n, 2 * H)
            sp.dma_start(a["out_hgrn_sample"][0].rearrange("b h k v -> k b h v"), s0).then_inc(s_sto, 16)
            for i, name in ((2, "ln2_g"), (3, "ln2_b")):
                sp.dma_start(ln[:, i, :], a[name].broadcast_to([P, D])).then_inc(s_lnp2, 16)

            w_gu = [a["w_gate"][0], a["w_up"][0]]

            def gu_src(which, e, c):
                w = w_gu[which][e] if isinstance(e, int) else w_gu[which][bass.ds(e, 1)].squeeze(0)
                return w[c * 512:(c + 1) * 512, :].rearrange("(p t) n -> p (t n)", t=4)

            def d_src(e, c):
                w = a["w_down"][0][e] if isinstance(e, int) else a["w_down"][0][bass.ds(e, 1)].squeeze(0)
                return w[c * 256:(c + 1) * 256, :].rearrange("(p t) n -> p (t n)", t=2)

            def load(slot, src):
                sp.dma_start(raw[slot], src).then_inc(m_raw[slot], 16)

            def moe_loads(bi, e, ep):
                last = isinstance(bi, int) and bi == E
                for j in (2, 3) if last else range(6):
                    sp.wait_ge(m_lo, count_of(bi - 1, j))
                    load(j, gu_src(0, e, j) if j < 2 else d_src(ep, j - 2) if j < 4 else gu_src(1, e, j - 4))

            sp.wait_ge(s_sto, 16)
            load(4, gu_src(1, 0, 0))
            load(5, gu_src(1, 0, 1))
            load(3, d_src(0, 1))
            sp.wait_ge(s_lo, NCH + NWO - 2)
            load(0, gu_src(0, 0, 0))
            sp.wait_ge(s_lo, NCH + NWO - 1)
            load(1, gu_src(0, 0, 1))
            sp.wait_ge(s_lo, NCH + NWO)
            load(2, d_src(0, 0))
            sp.wait_ge(s_on, NTT)
            x_slot = xg_dram.rearrange("(b p) n -> b p n", p=P)

            def load_x(bi, par):
                src = x_slot[bi] if isinstance(bi, int) else x_slot[bass.ds(bi, 1)].squeeze(0)
                sp.dma_start(xg[par], src).then_inc(m_xg[par], 16)

            for j in range(2):
                sp.wait_ge(m_lo, count_of(0, j))
                load(j, gu_src(0, 1, j))
            sp.wait_ge(s_sc, 16 * 2 * NTT)
            load_x(0, 0)
            load_x(1, 1)
            for j in (4, 5):
                sp.wait_ge(m_lo, count_of(0, j))
                load(j, gu_src(1, 1, j - 4))
            sp.wait_ge(m_t, 1)
            load_x(2, 0)
            def load_step(bi, par):
                sp.wait_ge(m_t, bi)
                if not (isinstance(bi, int) and bi == E - 1):
                    load_x(bi + 1, 1 - par)
                moe_loads(bi, bi, bi - 1)

            with sp.Fori(0, (E - 4) // 2) as i:
                load_step(2 * i + 2, 0)
                load_step(2 * i + 3, 1)
            load_step(E - 2, 0)
            load_step(E - 1, 1)
            moe_loads(E, None, E - 1)
            sp.wait_ge(s_slot, 3)
            n_over = sp.value_load(itab[0:1, 0:1], min_val=0, max_val=NOV)
            with sp.If(0 < n_over):
                with sp.Fori(0, NOV // 2) as i:
                    for r in range(2):
                        v = 2 * i + r
                        with sp.If(v < n_over):
                            e = sp.value_load(itab[0:1, bass.ds(v + 1, 1)], min_val=0, max_val=E - 1)
                            sp.wait_ge(m_t, E + v)
                            load_x(E + v, r)
                            sp.wait_ge(m_lo, 6 * E + 6 * v)
                            for j in range(2):
                                load(j, gu_src(0, e, j))
                            for j in range(2):
                                load(4 + j, gu_src(1, e, j))
                            for j in range(2):
                                load(2 + j, d_src(e, j))
            for tt in range(NTT):
                if tt < NTT - 1:
                    sp.wait_ge(s_yp, tt + 1)
                else:
                    sp.wait_ge(s_y1, 1)
                if tt < 4:
                    sp.dma_start(a["out_prompt"][0, tt * P:(tt + 1) * P, :], xr[:, tt, :]).then_inc(s_out, 16)
                else:
                    sp.dma_start(a["out_sample"].rearrange("b t n -> (b t) n"), xr[0:NS, tt, :]).then_inc(s_out, 16)
            sp.wait_ge(s_out, 16 * NTT)
            sp.wait_ge(s_cbs, 32)
            sp.wait_ge(s_sto, 16)
            sp.wait_ge(s_stp, 16)

        @block.gpsimd
        def _(pool):
            nc.gpsimd.memset(fa(32 * K, D), 0.0).then_inc(s_zero, 1)
            pool.wait_ge(s_zero, 1)
            pool.wait_ge(s_xl, 2 * NTT)
            fill_src = fa(32 * K, D).unsqueeze(1).broadcast_to([P, NOV, D])
            fills = (xg_dram[0:NOV * P, :], xg_dram[NOV * P:2 * NOV * P, :], xg_dram[2 * NOV * P:NBLK * P, :],
                     yg_dram[E * P:NBLK * P, :])

            def fill(i):
                pool.wait_ge(s_lo, 2 * i + 2)
                pool.dma_start(fills[i].rearrange("(b p) n -> p b n", p=P), fill_src).then_inc(s_fill, 16)

            def exponents(l):
                L, n = 1 << l, T if l < SLEVELS else SEQ
                if l >= 2:
                    pool.wait_ge(s_p, H * l)
                bl, br, mid = halves(b, L, n)
                dl, dr, _ = halves(ex[l % 2], L, n)
                mb = mid.broadcast_to(list(bl.shape))
                nc.gpsimd.tensor_tensor(dr, br, mb, ALU.subtract)
                nc.gpsimd.tensor_tensor(dl, mb, bl, ALU.subtract).then_inc(s_d, 1)

            fill(0)
            fill(1)
            pool.wait_ge(s_b, H)
            exponents(0)
            exponents(1)
            fill(2)
            exponents(2)
            exponents(3)
            fill(3)
            for l in range(4, LEVELS):
                exponents(l)
            pool.wait_ge(s_p, NP_LEVELS)
            for (c0, c1, w) in ((0, SEQ, P), (SEQ, T, DS)):
                bv = b[:, :, c0:c1].rearrange("p h (c t) -> p h c t", t=w)
                dv = ex[0][:, :, c0:c1].rearrange("p h (c t) -> p h c t", t=w)
                last = nc.gpsimd.tensor_tensor(dv, bv[:, :, :, w - 1:w].broadcast_to(list(bv.shape)), bv, ALU.subtract)
            last.then_inc(s_d, 1)
            pool.wait_ge(s_qx, 1)
            pool.wait_ge(s_cms, 2)
            seq_cols = const[:, C_QM:C_QM + DB * NS].rearrange("p (b t) -> p b t", b=DB)
            for h in range(H):
                last = nc.gpsimd.tensor_tensor(q_msk[:, h], q[:, h, SEQ:T].unsqueeze(1).broadcast_to([P, DB, NS]), seq_cols, ALU.mult)
            last.then_inc(s_qm, 1)
            pool.wait_ge(s_hg, 16)
            for o in (NCH - 2, NCH - 1):
                half = slice((o % 2) * CW, (o % 2) * CW + CW)
                pool.wait_ge(s_eva, act_tiles.index(tiles_of(o)[-1]) + 1)
                nc.gpsimd.tensor_tensor(sg[:, 0:4, half], sg[:, 0:4, half],
                                        h_gain[:, half].unsqueeze(1).broadcast_to([P, 4, CW]), ALU.mult)
                nc.gpsimd.tensor_tensor(sg[0:NS, 4, half], sg[0:NS, 4, half], h_gain[0:NS, half], ALU.mult).then_inc(s_sg, 1)
            seq_mask = small[0:NS, SM_SEQ:SM_SEQ + DB].unsqueeze(2).broadcast_to([NS, DB, P])

            def mask_values(h):
                nc.gpsimd.tensor_tensor(v_msk[0:NS], v_tok[0:NS, 4, h * P:(h + 1) * P].unsqueeze(1).broadcast_to([NS, DB, P]),
                                        seq_mask, ALU.mult).then_inc(s_vm, 1)

            mask_values(0)
            pool.wait_ge(s_stp, 16)
            pool.wait_ge(s_o, NTT)
            nc.gpsimd.memset(xr[:, 4, :], 0.0).then_inc(s_xr0, 1)
            nc.gpsimd.tensor_tensor(s0.rearrange("p b h v -> p (b h) v"), s0.rearrange("p b h v -> p (b h) v"),
                                    s0_decay.unsqueeze(2).broadcast_to([P, DB * H, P]), ALU.mult).then_inc(s_s0d, 1)
            for h in range(1, H):
                pool.wait_ge(s_sus, 2 * h)
                mask_values(h)
            pool.wait_ge(s_lnp, 32)
            for tt in range(POOL_LN):
                pool.wait_ge(s_xgn, tt + 1)
                nc.gpsimd.tensor_tensor(xr[:, tt, :], xr[:, tt, :], ln[:, 1, :], ALU.add).then_inc(s_x1, 1)
            for j in range(2):
                pool.wait_ge(m_hi, j + 1)
                nc.gpsimd.tensor_tensor(split[j][1], raw[j], split[j][0].bitcast(F32), ALU.subtract).then_inc(m_lo, 1)
            for n in range(2):
                for tt in range(NTT):
                    rows = NS if tt == NTT - 1 else P
                    if n == 0 and tt == 0:
                        pool.wait_ge(s_slot, 1)
                        pool.wait_ge(s_x1, POOL_LN)
                        pool.wait_ge(s_x1d, NTT - POOL_LN)
                    pool.indirect_dma_start(
                        out=xg_dram, out_offset=bass.IndirectOffsetOnAxis(ap=slot_i[0:rows, 5 * n + tt:5 * n + tt + 1].bitcast(U32), axis=0),
                        in_=xr[0:rows, tt, :], in_offset=None).then_inc(s_sc, 16)
            pool.wait_ge(s_sc, 16 * 2 * NTT)
            for tt in range(NTT):
                last = nc.gpsimd.tensor_scalar(xr[:, tt, :], xr[:, tt, :], ALPHA, None, ALU.mult)
            last.then_inc(s_ax, 1)
            y_slot = yg_dram.rearrange("(b p) n -> b p n", p=P)

            def store(bi, par):
                pool.wait_ge(m_ya, bi + 1)
                pool.wait_ge(m_yd, bi + 1)
                dst = y_slot[bi] if isinstance(bi, int) else y_slot[bass.ds(bi, 1)].squeeze(0)
                pool.dma_start(dst, ysb[par]).then_inc(m_st[par], 16)

            with pool.Fori(0, E // 2) as i:
                for par in range(2):
                    store(2 * i + par, par)
            for par in range(2):
                pool.wait_ge(m_st[par], 16 * (E // 2))
            pool.wait_ge(s_slot, 3)
            n_over = pool.value_load(itab[0:1, 0:1], min_val=0, max_val=NOV)
            with pool.If(0 < n_over):
                with pool.Fori(0, NOV // 2) as i:
                    for par in range(2):
                        with pool.If(2 * i + par < n_over):
                            store(E + 2 * i + par, par)
                            pool.wait_ge(m_st[par], 16 * (E // 2) + 16 * (i + 1))
            for tt in range(NTT):
                rows = NS if tt == NTT - 1 else P
                for n, dst in enumerate((y_a, y_b)):
                    pool.indirect_dma_start(
                        out=dst[0:rows, tt, :], out_offset=None, in_=yg_dram,
                        in_offset=bass.IndirectOffsetOnAxis(ap=slot_i[0:rows, 5 * n + tt:5 * n + tt + 1].bitcast(U32), axis=0)).then_inc(s_ga[tt], 16)
            for tt in range(NTT - 1):
                pool.wait_ge(s_fg, tt + 1)
                nc.gpsimd.tensor_tensor(xr[:, tt, :], xr[:, tt, :], ln[:, 3, :], ALU.add).then_inc(s_yp, 1)
            for par in range(2):
                pool.wait_ge(m_st[par], 16 * (E // 2))

        @block.scalar
        def _(act):
            chain = [0]

            def link(ins):
                chain[0] += 1
                ins.then_inc(s_ac, 1)
                act.wait_ge(s_ac, chain[0])

            for m in range(2 * NTT):
                tt, hf = m // 2, m % 2
                n = P if tt < 4 else NS
                act.wait_ge(s_xt, m + 1)
                src = bank[m % 7][:, 0:4 * n].rearrange("p (k t) -> p k t", k=4)
                nc.scalar.activation(xT[0][:, 4 * hf:4 * hf + 4, tok(tt)], src, ACT.Copy).then_inc(s_xh, 1)
            act.wait_ge(s_pt, 1)
            nc.scalar.activation(params[:, 0:84], bank[7][:, 0:84], ACT.Copy).then_inc(s_pp, 1)

            def hi(o):
                act.wait_ge(s_raw[o % 3], 16 * (o // 3 + 1))
                if 2 <= o < NCH + 2:
                    act.wait_ge(s_tile, tiles_of(o - 2)[-1] + 1)
                elif o >= NCH + 2:
                    act.wait_ge(s_w, NTT * (o - 1 - NCH))
                nc.scalar.activation(split[o % 2][0], raw[o % 3], ACT.Copy).then_inc(s_hi, 1)

            def evacuate(o):
                for n in tiles_of(o):
                    kind, _, j = TILES[n]
                    if kind in BY_DVE:
                        continue
                    act.wait_ge(s_tile, n + 1)
                    pb, ps = tile_banks(n)
                    if kind in TOKEN_MAJOR:
                        rows = P if j < 4 else NS
                        dst, func = (v_tok, ACT.Copy) if kind == "v" else (sg, ACT.Silu)
                        nc.scalar.activation(dst[0:rows, j, (o % 2) * CW:(o % 2) * CW + CW], pb[0:rows, 0:CW],
                                             func).then_inc(s_eva, 1)
                        continue
                    h = 2 * (o % 2) + j
                    cols = [(pb[:, 0:HT], slice(0, HT)), (ps[:, 0:HT], slice(HT, T))]
                    if kind == "f":
                        for src, c in cols:
                            nc.scalar.activation(z[:, h, c], src, ACT.Copy)
                        for src, c in cols:
                            last = nc.scalar.activation(k[:, h, c], src, ACT.Sigmoid, scale=-1.0)
                        last.then_inc(s_eva, 1)
                    elif kind == "gc":
                        for dst, src in conv_pieces(h, pb, ps):
                            last = nc.scalar.activation(dst, src, ACT.Copy)
                        last.then_inc(s_eva, 1)
                    else:
                        for src, c in cols:
                            last = nc.scalar.activation(q[:, h, c], src, ACT.Silu)
                        last.then_inc(s_eva, 1)

            for o in range(NCH + 1):
                if o >= 2:
                    evacuate(o - 2)
                hi(o)
                if o == 4:
                    act.wait_ge(s_abs, 1)
                    link(nc.scalar.activation(ex[0][:, :, :], ex[0][:, :, :], ACT.Exp, scale=-1.0))
                    nc.scalar.activation(ex[0][:, :, :], ex[0][:, :, :], ACT.Ln, bias=1.0).then_inc(s_lnf, 1)
                l = o - FIRST_LEVEL_STEP
                if 0 <= l < LEVELS:
                    act.wait_ge(s_d, l + 1)
                    n = T if l < SLEVELS else SEQ
                    nc.scalar.activation(ex[l % 2][:, :, 0:n], ex[l % 2][:, :, 0:n], ACT.Exp).then_inc(s_e, 1)
                if o == 9:
                    act.wait_ge(s_selt, 1)
                    act.wait_ge(s_b, H)
                    nc.scalar.activation(const[0:8, C_RST:C_RST + 4 * P], bank[7][0:8, :], ACT.Copy).then_inc(s_sel, 1)
                if o == NCH - 1:
                    act.wait_ge(s_p, H * LEVELS)
                    nc.scalar.activation(ex[1][:, :, :], b[:, :, :], ACT.Exp).then_inc(s_e, 1)
                    act.wait_ge(s_d, LEVELS + 1)
                    nc.scalar.activation(ex[0][:, :, :], ex[0][:, :, :], ACT.Exp).then_inc(s_e, 1)
                    act.wait_ge(s_evd, len(dve_tiles))
                    nc.scalar.activation(sq[:, :, :], yc[:, :, :], ACT.Square).then_inc(s_csq, 1)
                    act.wait_ge(s_cbt, 1)
                    nc.scalar.activation(cb_out[0:18, :], bank[7][0:18, :], ACT.Copy).then_inc(s_cbo, 1)
                if o == NCH:
                    for g in range(2):
                        act.wait_ge(s_cms, g + 1)
                        nc.scalar.activation(r_conv[:, g * HT:(g + 1) * HT], bank[6 + g][0:8, 0:HT], ACT.Sqrt,
                                             bias=eps_rms[0:8, :], scale=1.0 / 64).then_inc(s_crt, 1)
            evacuate(NCH - 1)
            for j in range(4):
                act.wait_ge(s_cf, 2 * j + 2)
                nc.scalar.activation(xT[0][:, 4 + j, :], yc[:, j, :], ACT.Copy).then_inc(s_ch, 1)
            hi(NCH + 1)

            def o_squares(i):
                tt = i
                rows = P if tt < 4 else NS
                act.wait_ge(s_o, i + 1)
                if i >= 2:
                    act.wait_ge(s_red, i - 1)
                nc.scalar.activation(o_sq[i % 2][0:rows, :], o_bank(tt)[0:rows, :], ACT.Square).then_inc(s_osq, 1)

            def o_hi(i):
                tt = i
                rows = P if tt < 4 else NS
                act.wait_ge(s_ot, i + 1)
                nc.scalar.activation(xT[0][:, 0:4, tok(tt)], o_bank(tt)[:, 0:4 * rows].rearrange("p (h t) -> p h t", h=H),
                                     ACT.Copy).then_inc(s_oh_, 1)

            o_squares(0)
            for i in range(NTT):
                rows = P if i < 4 else NS
                if i + 1 < NTT:
                    o_squares(i + 1)
                act.wait_ge(s_red, i + 1)
                nc.scalar.activation(root[0:rows, 4 * i:4 * i + 4], ss[0:rows, 4 * i:4 * i + 4], ACT.Sqrt,
                                     bias=eps_rms[0:rows, :], scale=1.0 / P).then_inc(s_ort, 1)
                if i:
                    o_hi(i - 1)
            o_hi(NTT - 1)
            hi(NCH + 2)
            hi(NCH + 3)
            def normalise(tt):
                act.wait_ge(s_var, tt + 1)
                nc.scalar.activation(rt[:, tt:tt + 1], mv1[:, tt, 1:2], ACT.Sqrt, bias=eps_ln).then_inc(s_std, 1)
                act.wait_ge(s_nm, tt + 1)
                nc.scalar.activation(xr[:, tt, :], xr[:, tt, :], ACT.Identity, bias=shift[:, tt:tt + 1],
                                     scale=rt[:, tt:tt + 1]).then_inc(s_nrm, 1)

            def copy_x1T(tt):
                n = P if tt < 4 else NS
                for hf in range(2):
                    m = 2 * tt + hf
                    act.wait_ge(s_1t, m + 1)
                    nc.scalar.activation(x1T[tt // 2][:, 4 * hf:4 * hf + 4, (tt % 2) * P:(tt % 2) * P + n],
                                         bank[1 + m % 4][:, 0:4 * n].rearrange("p (k t) -> p k t", k=4), ACT.Copy).then_inc(s_1c, 1)

            for tt in range(NTT - 1):
                normalise(tt)
            copy_x1T(0)
            normalise(NTT - 1)
            for tt in range(1, NTT):
                copy_x1T(tt)
            for g in range(3):
                act.wait_ge(s_lgt, g + 1)
                n = 2 * P if g < 2 else NS
                last = nc.scalar.activation(lg[:, 2 * g * P:2 * g * P + n], bank[5 + g][0:E, 0:n], ACT.Copy)
            last.then_inc(s_lgs, 1)
            act.wait_ge(s_rl, 1)
            nc.scalar.activation(r_p, r_l, ACT.Exp).then_inc(s_re, 1)
            for j in (0, 1, 4):
                act.wait_ge(m_raw[j], 16)
                nc.scalar.activation(split[split_slot(0, j)][0], raw[j], ACT.Copy).then_inc(m_hi, 1)

            def mhi(bi, j, slot=None):
                act.wait_ge(m_raw[j], 16 * raw_use(bi, j))
                f = slot_free_count(bi, j)
                if f is not None:
                    act.wait_ge(m_use, f)
                nc.scalar.activation(split[split_slot(bi, j)][0], raw[j], ACT.Copy).then_inc(m_hi, 1)

            def x_hi(bi, par):
                for c in range(2):
                    act.wait_ge(m_t, bi + 1)
                    nc.scalar.activation(xgT[par][0][:, 4 * c:4 * c + 4, :], bank[c][:, :].rearrange("p (k t) -> p k t", k=4),
                                         ACT.Copy).then_inc(m_th, 1)

            def h_hi(bi):
                act.wait_ge(m_ht, bi + 1)
                nc.scalar.activation(hT[0][:, :, :], bank[4][:, :].rearrange("p (k t) -> p k t", k=4),
                                     ACT.Copy).then_inc(m_hh, 1)

            def silu(bi):
                act.wait_ge(m_use, gate_count(bi))
                if not (isinstance(bi, int) and bi == 0):
                    act.wait_ge(m_h, bi)
                nc.scalar.activation(silu_g, bank[2][:, :], ACT.Silu).then_inc(m_sg, 1)

            def y_half(bi, par):
                act.wait_ge(m_use, down_count(bi))
                if not (isinstance(bi, int) and bi < 2):
                    act.wait_ge(m_st[par], store_count(bi, par))
                nc.scalar.activation(ysb[par][:, 0:512], bank[5][:, :], ACT.Copy).then_inc(m_ya, 1)

            def step(bi, par):
                first, last = isinstance(bi, int) and bi == 0, isinstance(bi, int) and bi == E - 1
                if not first:
                    mhi(bi, 2)
                    h_hi(bi - 1)
                    mhi(bi, 3)
                if first:
                    mhi(1, 0)
                else:
                    mhi(bi, 4)
                silu(bi)
                mhi(bi, 5)
                if not last and not first:
                    mhi(bi + 1, 0)
                if not first:
                    y_half(bi - 1, 1 - par)
                if not last:
                    x_hi(bi + 1, 1 - par)
                    mhi(bi + 1, 1)

            x_hi(0, 0)
            step(0, 0)
            step(1, 1)
            step(2, 0)
            with act.Fori(0, (E - 4) // 2) as i:
                step(2 * i + 3, 1)
                step(2 * i + 4, 0)
            step(E - 1, 1)
            mhi(E, 2)
            h_hi(E - 1)
            mhi(E, 3)
            y_half(E - 1, 1)
            act.wait_ge(s_slot, 3)
            n_over = act.value_load(itab[0:1, 0:1], min_val=0, max_val=NOV)
            with act.If(0 < n_over):
                with act.Fori(0, NOV // 2) as i:
                    for par in range(2):
                        v = 2 * i + par
                        with act.If(v < n_over):
                            x_hi(E + v, par)
                            for s, j in enumerate(OV_ORDER):
                                if s == 4:
                                    h_hi(E + v)
                                act.wait_ge(m_raw[j], 16 * (E + v + 1))
                                act.wait_ge(m_use, 6 * E + 6 * v if s < 3 else 6 * E + 6 * v + s - 2)
                                nc.scalar.activation(split[s % 3][0], raw[j], ACT.Copy).then_inc(m_hi, 1)
                                if s == 3:
                                    act.wait_ge(m_use, 6 * E + 6 * v + 2)
                                    act.wait_ge(m_h, E + v)
                                    nc.scalar.activation(silu_g, bank[2][:, :], ACT.Silu).then_inc(m_sg, 1)
                            act.wait_ge(m_use, 6 * E + 6 * v + 6)
                            act.wait_ge(m_st[par], 16 * (E // 2) + 16 * i)
                            nc.scalar.activation(ysb[par][:, 0:512], bank[5][:, :], ACT.Copy).then_inc(m_ya, 1)
            for tt in range(NTT):
                act.wait_ge(s_fvar, tt + 1)
                nc.scalar.activation(rt[:, tt:tt + 1], mv1[:, tt, 1:2], ACT.Sqrt, bias=eps_ln).then_inc(s_fstd, 1)
                act.wait_ge(s_fnm, tt + 1)
                nc.scalar.activation(xr[:, tt, :], xr[:, tt, :], ACT.Identity, bias=shift[:, tt:tt + 1],
                                     scale=rt[:, tt:tt + 1]).then_inc(s_fnr, 1)

        @block.vector
        def _(dve):
            tt_, ts_, stt = nc.vector.tensor_tensor, nc.vector.tensor_scalar, nc.vector.scalar_tensor_tensor
            chain = [0]

            def link(ins):
                chain[0] += 1
                ins.then_inc(s_dv, 1)
                dve.wait_ge(s_dv, chain[0])

            f = lambda r: r.bitcast(F32)
            nc.vector.memset(eps_rms, RMS_EPS)
            link(nc.vector.memset(eps_ln, LN_EPS))
            for m in range(2 * NTT):
                tt, hf = m // 2, m % 2
                n = P if tt < 4 else NS
                dve.wait_ge(s_xh, m + 1)
                src = bank[m % 7][:, 0:4 * n].rearrange("p (k t) -> p k t", k=4)
                tt_(xT[1][:, 4 * hf:4 * hf + 4, tok(tt)], src, f(xT[0][:, 4 * hf:4 * hf + 4, tok(tt)]),
                    ALU.subtract).then_inc(s_xl, 1)

            dve.wait_ge(s_const, 16)

            def lo(o):
                dve.wait_ge(s_hi, o + 1)
                tt_(split[o % 2][1], raw[o % 3], f(split[o % 2][0]), ALU.subtract).then_inc(s_lo, 1)

            par_g = lambda base, j: params[:, base + j:base + j + 1]

            def evacuate(o):
                for n in tiles_of(o):
                    kind, _, j = TILES[n]
                    if kind not in BY_DVE:
                        continue
                    dve.wait_ge(s_tile, n + 1)
                    pb, ps = tile_banks(n)
                    h = 2 * (o % 2) + j
                    if kind == "cx":
                        if o == 8 and j == 0:
                            dve.wait_ge(s_eva, act_tiles.index(tiles_of(7)[1]) + 1)
                            dve.wait_ge(s_pp, 1)
                        us = u[:, h, 2 + SEQ:UW].rearrange("p (b t) -> p b t", b=DB)
                        link(nc.vector.memset(u[:, h, 0:2], 0.0))
                        for dst, src in conv_pieces(h, pb, ps):
                            last = tt_(dst, dst, src, ALU.mult)
                        last.then_inc(s_evd, 1)
                        link(nc.vector.tensor_copy(us[:, :, 0:2],
                                                   params[:, 20:84].rearrange("p (b j t) -> p b j t", b=DB, j=2)[:, :, :, h]))
                        dve.wait_ge(s_evd, dve_tiles.index(n) + 1)
                        yp, ys = yc[:, h, 0:SEQ], yc[:, h, SEQ:T].rearrange("p (b t) -> p b t", b=DB)
                        ts_(yp, u[:, h, 0:SEQ], par_g(4, h), None, ALU.mult)
                        link(ts_(ys, us[:, :, 0:DS], par_g(4, h), None, ALU.mult))
                        for jj in (1, 2):
                            stt(yp, u[:, h, jj:jj + SEQ], par_g(4 + 4 * jj, h), yp, ALU.mult, ALU.add)
                            link(stt(ys, us[:, :, jj:jj + DS], par_g(4 + 4 * jj, h), ys, ALU.mult, ALU.add))
                        nc.vector.tensor_copy(cb[:, h, 0:2], u[:, h, SEQ:SEQ + 2])
                        nc.vector.tensor_copy(cb[:, h, 2:18].rearrange("p (b t) -> p b t", b=DB),
                                              us[:, :, DS:DS + 2]).then_inc(s_cb, 1)
                    else:
                        tt_(yc[:, h, 0:HT], yc[:, h, 0:HT], pb[:, 0:HT], ALU.mult)
                        tt_(yc[:, h, HT:T], yc[:, h, HT:T], ps[:, 0:HT], ALU.mult).then_inc(s_evd, 1)

            def decayed(l):
                L, n = 1 << l, T if l < SLEVELS else SEQ
                dve.wait_ge(s_e, l + 1)
                dl, dr, _ = halves(ex[l % 2], L, n)
                _, qr, _ = halves(q, L, n)
                kl, _, _ = halves(k, L, n)
                tt_(dr, dr, qr, ALU.mult)
                tt_(dl, dl, kl, ALU.mult).then_inc(s_z, 1)

            def take_pairs(li):
                for h in range(H):
                    p = li * H + h
                    dve.wait_ge(s_p, p + 1)
                    src = bank[4 + p % 3][:, :].rearrange("p (c t) -> p c t", c=NC)
                    if li == 0:
                        tt_(att[:, h, :, :], src, ident.unsqueeze(1).broadcast_to([P, NC, P]), ALU.mult).then_inc(s_pc, 1)
                    else:
                        m = masks[:, (li - 1) * P:li * P].unsqueeze(1).broadcast_to([P, NC, P])
                        nc.vector.copy_predicated(att[:, h, :, :], m, src).then_inc(s_pc, 1)
                if li <= SLEVELS:
                    src = bank[7][0:NS, 0:H * NS].rearrange("p (h t) -> p h t", h=H)
                    if li == 0:
                        tt_(att_s[0:NS], src, ident[0:NS, 0:NS].unsqueeze(1).broadcast_to([NS, H, NS]), ALU.mult).then_inc(s_ps, 1)
                    else:
                        m = masks[0:NS, (li - 1) * P:(li - 1) * P + NS].unsqueeze(1).broadcast_to([NS, H, NS])
                        nc.vector.copy_predicated(att_s[0:NS], m, src).then_inc(s_ps, 1)
                    dve.wait_ge(s_ps, li + 1)
                dve.wait_ge(s_pc, H * (li + 1))

            for o_ in range(NCH + 1):
                if o_ >= 2:
                    evacuate(o_ - 2)
                l = o_ - FIRST_LEVEL_STEP
                if 0 <= l - 1 <= LEVELS:
                    take_pairs(l - 1)
                lo(o_)
                if o_ == 0:
                    dve.wait_ge(s_mask, 16)
                    link(nc.vector.tensor_copy(masks[:, :], fa(E0, LEVELS * P)))
                if o_ == 3:
                    dve.wait_ge(s_eva, 4)
                    stt(ex[0][:, :, :], z[:, :, :], -1.0, z[:, :, :], ALU.mult, ALU.max).then_inc(s_abs, 1)
                if o_ == 4:
                    dve.wait_ge(s_lnf, 1)
                    link(stt(z[:, :, :], z[:, :, :], 0.0, ex[0][:, :, :], ALU.min, ALU.subtract))
                    for h in range(H):
                        nc.vector.tensor_tensor_scan(b[:, h, :], reset, z[:, h, :], 0.0, ALU.mult, ALU.add).then_inc(s_b, 1)
                    dve.wait_ge(s_b, H)
                if 0 <= l - 1 < LEVELS:
                    if l == 1:
                        dve.wait_ge(s_eva, 8)
                    decayed(l - 1)
                if o_ == NCH - 1:
                    dve.wait_ge(s_e, LEVELS + 1)
                    tt_(q[:, :, :], q[:, :, :], ex[1][:, :, :], ALU.mult).then_inc(s_qx, 1)
                    nc.vector.tensor_copy(p_decay, ex[1][:, :, P - 1:SEQ:P])
                    link(nc.vector.tensor_copy(s0_decay.rearrange("p (b h) -> p h b", h=H), ex[1][:, :, SEQ + DS - 1:T:DS]))
                    dve.wait_ge(s_e, LEVELS + 2)
                    tt_(k[:, :, :], k[:, :, :], ex[0][:, :, :], ALU.mult).then_inc(s_kx, 1)
                    for h in range(H):
                        dve.wait_ge(s_kt, h + 1)
                        nc.vector.tensor_copy(k_tok[:, h, :, :], bank[4 + h % 2][:, :].rearrange("p (c k) -> p c k", c=NC)).then_inc(s_ktc, 1)
                    dve.wait_ge(s_kt, H + 1)
                    nc.vector.tensor_copy(k_tok_s[0:NS], bank[4][0:NS, :].rearrange("p (h k) -> p h k", h=H)).then_inc(s_ktc, 1)
            dve.wait_ge(s_crt, 2)
            nc.vector.reciprocal(r_conv, r_conv).then_inc(s_crc, 1)
            for m in range(8):
                j, cols = m // 2, slice((m % 2) * HT, (m % 2 + 1) * HT)
                dve.wait_ge(s_cbc, m + 1)
                stt(yc[:, j, cols], yc[:, j, cols], params[:, 16 + j:17 + j], bank[6 + m % 2][:, 0:HT], ALU.mult,
                    ALU.mult).then_inc(s_cf, 1)
            for c in range(NC):
                dve.wait_ge(s_su, c + 1)
                pb = bank[4 + c % 2]
                if c == 0:
                    nc.vector.tensor_copy(state[:, 0, :, :], pb[:, :].rearrange("p (h v) -> p h v", h=H)).then_inc(s_st, 1)
                else:
                    dve.wait_ge(s_st, c)
                    for h in range(H):
                        last = stt(state[:, c, h, :], state[:, c - 1, h, :], p_decay[:, h, c:c + 1], pb[:, h * P:(h + 1) * P],
                                   ALU.mult, ALU.add)
                    last.then_inc(s_st, 1)
                dve.wait_ge(s_ch, c + 1)
                tt_(xT[1][:, 4 + c, :], yc[:, c, :], f(xT[0][:, 4 + c, :]), ALU.subtract).then_inc(s_cl, 1)

            def o_lo(i):
                tt = i
                rows = P if tt < 4 else NS
                dve.wait_ge(s_oh_, i + 1)
                tt_(xT[1][:, 0:4, tok(tt)], o_bank(tt)[:, 0:4 * rows].rearrange("p (h t) -> p h t", h=H),
                    f(xT[0][:, 0:4, tok(tt)]), ALU.subtract).then_inc(s_ol, 1)

            dve.wait_ge(s_sg, 2)
            for i, tt in enumerate(range(NTT)):
                rows = P if tt < 4 else NS
                place = o_n[i % 2][0:rows, :]
                rr = root[0:rows, 4 * i:4 * i + 4]
                dve.wait_ge(s_osq, i + 1)
                nc.vector.tensor_reduce(ss[0:rows, 4 * i:4 * i + 4], o_sq[i % 2][0:rows, :].rearrange("p (h v) -> p h v", h=H),
                                        AX, ALU.add).then_inc(s_red, 1)
                if i >= 2:
                    dve.wait_ge(s_ot, i - 1)
                tt_(place, o_bank(tt)[0:rows, :], sg[0:rows, tt, :], ALU.mult).then_inc(s_dv, 1)
                chain[0] += 1
                if i:
                    o_lo(i - 1)
                dve.wait_ge(s_ort, i + 1)
                link(nc.vector.reciprocal(rr, rr))
                p3 = place.rearrange("p (h v) -> p h v", h=H)
                tt_(p3, p3, rr.unsqueeze(2).broadcast_to([rows, H, P]), ALU.mult).then_inc(s_on, 1)
            o_lo(NTT - 1)
            lo(NCH + 1)
            dve.wait_ge(s_xr, 32)

            def shift_scale(tt, std_sem=s_std, out_sem=s_nm):
                dve.wait_ge(std_sem, tt + 1)
                link(nc.vector.reciprocal(rt[:, tt:tt + 1], rt[:, tt:tt + 1]))
                stt(shift[:, tt:tt + 1], mv1[:, tt, 0:1], -1.0, rt[:, tt:tt + 1], ALU.mult, ALU.mult).then_inc(out_sem, 1)

            def ln_gain(tt):
                dve.wait_ge(s_nrm, tt + 1)
                tt_(xr[:, tt, :], xr[:, tt, :], ln[:, 0, :], ALU.mult).then_inc(s_xgn, 1)
                if tt >= POOL_LN:
                    dve.wait_ge(s_xgn, tt + 1)
                    tt_(xr[:, tt, :], xr[:, tt, :], ln[:, 1, :], ALU.add).then_inc(s_x1d, 1)

            for c in range(NWO):
                for tt in range(NTT):
                    n = c * NTT + tt
                    rows = P if tt < 4 else NS
                    dve.wait_ge(s_w, n + 1)
                    dst = xr[0:rows, tt, c * CW:(c + 1) * CW]
                    stt(dst, dst, ALPHA, w_bank(n)[0:rows, 0:CW], ALU.mult, ALU.add).then_inc(s_wc, 1)
                    if c % 2:
                        dve.wait_ge(s_wc, n + 1)
                        g = c // 2
                        nc.vector.bn_stats(stats[:, tt, 6 * g:6 * g + 6], xr[:, tt, 512 * g:512 * g + 512]).then_inc(s_dv, 1)
                        chain[0] += 1
                    if c == NWO - 1:
                        dve.wait_ge(s_dv, chain[0])
                        nc.vector.bn_aggr(mv1[:, tt, :], stats[:, tt, :]).then_inc(s_var, 1)
                        if tt >= 1:
                            shift_scale(tt - 1)
                        if tt == 2:
                            dve.wait_ge(s_lnp, 32)
                        if tt >= 2:
                            ln_gain(tt - 2)
                if c < 2:
                    lo(NCH + 2 + c)
                if c == 0:
                    dve.wait_ge(s_s0d, 1)
                if c < NWO - 1:
                    for h, g in ((c, 0), (c, 1)) if c < 2 else ((2, 0), (2, 1), (3, 0), (3, 1)):
                        dve.wait_ge(s_sus, 2 * h + g + 1)
                        sl = s0[:, 4 * g:4 * g + 4, h, :]
                        tt_(sl, sl, bank[1 + g][:, :].rearrange("p (b v) -> p b v", b=4), ALU.add).then_inc(s_s0n, 1)
            shift_scale(NTT - 1)
            ln_gain(NTT - 2)
            ln_gain(NTT - 1)

            bias_b = rt[:, 448:464].unsqueeze(1).broadcast_to([P, NTT, E])
            mx, s5 = rb(0, NTT), rb(8, NTT)
            pair, gs, gm, g1 = rb(16, 6 * 20), rb(136, 20), rb(156, NTT), rb(164, 20)
            pm, tmp, m1, m2 = rb(184, NE), rb(264, NE), rb(344, NTT), rb(352, NTT)
            rank, nb, ob, on_, big = rb(360, NE), rb(456, E), rb(472, E), rb(488, E), rb(504, NE)
            before = rb(720, NE + E)
            cnt = before[:, NE:NE + E]
            slot_f, tf = rb(584, 2 * NTT), rb(600, 16)
            bc = lambda v, n: v.unsqueeze(2).broadcast_to([P, v.shape[1], n])
            dve.wait_ge(s_wr, 32)
            nc.vector.memset(r_l[:, 4 * E:NE], 0.0).then_inc(s_dv, 1)
            chain[0] += 1
            dve.wait_ge(s_lg, 1)
            dve.wait_ge(s_dv, chain[0])
            tt_(t3(r_l)[:, 0:4], bank[3][:, 0:4 * E].rearrange("p (t e) -> p t e", e=E), bias_b[:, 0:4], ALU.add)
            link(tt_(r_l[0:NS, 4 * E:NE], bank[3][0:NS, 4 * E:NE], rt[0:NS, 448:464], ALU.add))
            link(nc.vector.tensor_reduce(mx, t3(r_l), AX, ALU.max))
            tt_(t3(r_l), t3(r_l), bc(mx, E), ALU.subtract).then_inc(s_rl, 1)
            dve.wait_ge(s_re, 1)
            link(nc.vector.tensor_reduce(s5, t3(r_p), AX, ALU.add))
            link(nc.vector.reciprocal(s5, s5))
            link(tt_(t3(r_p), t3(r_p), bc(s5, E), ALU.mult))
            pv, p4 = pair.rearrange("p (g s) -> p g s", s=6), t4(r_p)
            n6 = 0
            for i in range(TOPG):
                for j in range(i + 1, TOPG):
                    last = tt_(pv[:, :, n6:n6 + 1], p4[:, :, i:i + 1], p4[:, :, j:j + 1], ALU.add)
                    n6 += 1
            link(last)
            g3 = lambda v: v.rearrange("p (t g) -> p t g", t=NTT)
            link(nc.vector.tensor_reduce(gs, pv, AX, ALU.max))
            link(nc.vector.tensor_reduce(gm, g3(gs), AX, ALU.max))

            def first_max(out, vals, mxv, order, n):
                link(tt_(out, vals, bc(mxv, n), ALU.is_equal))
                link(tt_(out, out, order.unsqueeze(1).broadcast_to([P, NTT, n]), ALU.mult))
                link(nc.vector.tensor_reduce(tf[:, 0:NTT], out, AX, ALU.max))
                link(tt_(out, out, bc(tf[:, 0:NTT], n), ALU.is_equal))

            first_max(g3(g1), g3(gs), gm, small[:, SM_G4:SM_G4 + TOPG], TOPG)
            gmask = g1.unsqueeze(2).broadcast_to([P, NTT * TOPG, TOPG])
            eo = small[:, SM_E16:SM_E16 + E]
            tt_(t4(tmp), p4, gmask, ALU.mult)
            link(ts_(t4(pm), gmask, 1.0, None, ALU.subtract))
            link(tt_(pm, pm, tmp, ALU.add))
            link(nc.vector.tensor_reduce(m1, t3(pm), AX, ALU.max))
            first_max(t3(r_o1), t3(pm), m1, eo, E)
            link(stt(pm, r_o1, -4.0, pm, ALU.mult, ALU.add))
            link(nc.vector.tensor_reduce(m2, t3(pm), AX, ALU.max))
            first_max(t3(r_o2), t3(pm), m2, eo, E)
            link(tt_(tf[:, 8:8 + NTT], m1, m2, ALU.add))
            link(nc.vector.reciprocal(tf[:, 8:8 + NTT], tf[:, 8:8 + NTT]))
            tt_(gw[:, 0:NTT], m1, tf[:, 8:8 + NTT], ALU.mult)
            link(tt_(gw[:, NTT:2 * NTT], m2, tf[:, 8:8 + NTT], ALU.mult))
            val = small[:, SM_VAL:SM_VAL + NTT].unsqueeze(2).broadcast_to([P, NTT, E])
            link(tt_(tmp, r_o1, r_o2, ALU.add))
            tt_(t3(choice), t3(tmp), val, ALU.mult).then_inc(s_oh, 1)
            nc.vector.memset(before[:, 0:E], 0.0)
            dve.wait_ge(s_rk, 1)
            link(nc.vector.tensor_copy(before[:, E:2 * E], bank[4][:, NE:NE + E]))
            for j in range(2, NTT + 1):
                link(tt_(before[:, j * E:(j + 1) * E], before[:, (j - 1) * E:j * E], bank[4][:, NE + (j - 1) * E:NE + j * E],
                         ALU.add))
            link(tt_(rank, bank[4][:, 0:NE], before[:, 0:NE], ALU.add))
            link(ts_(nb, cnt, float(P), None, ALU.is_gt))
            for j in range(2, NTT):
                link(stt(nb, cnt, float(P * j), nb, ALU.is_gt, ALU.add))
            link(nc.vector.tensor_tensor_scan(ob, ones[:, 0:E], nb, 0.0, ALU.mult, ALU.add))
            link(tt_(on_, ob, nb, ALU.subtract))
            link(ts_(on_, on_, float(P), float(E * P - P), ALU.mult, ALU.add))
            link(tt_(on_, on_, small[:, SM_E128:SM_E128 + E], ALU.subtract))
            link(ts_(big, rank, float(P), None, ALU.is_ge))
            link(tt_(t3(big), t3(big), on_.unsqueeze(1).broadcast_to([P, NTT, E]), ALU.mult))
            link(tt_(rank, rank, big, ALU.add))
            link(tt_(t3(rank), t3(rank), small[:, SM_E128:SM_E128 + E].unsqueeze(1).broadcast_to([P, NTT, E]), ALU.add))
            for n, oh in enumerate((r_o1, r_o2)):
                link(tt_(tmp, rank, oh, ALU.mult))
                link(nc.vector.tensor_reduce(slot_f[:, n * NTT:(n + 1) * NTT], t3(tmp), AX, ALU.add))
            nc.vector.tensor_copy(slot_i[:, :], slot_f).then_inc(s_slot, 1)
            dve.wait_ge(m_lo, 2)
            dve.wait_ge(m_hi, 3)
            tt_(split[2][1], raw[4], f(split[2][0]), ALU.subtract).then_inc(m_lo, 1)
            link(nc.vector.tensor_copy(tf[:, 0:1], ob[:, E - 1:E]))
            for v in range(NOV):
                link(ts_(tmp[:, 0:E], ob, float(v), None, ALU.is_le))
                link(nc.vector.tensor_reduce(tf[:, 1 + v:2 + v], tmp[:, 0:E], AX, ALU.add))
            link(ts_(tf[:, 1:1 + NOV], tf[:, 1:1 + NOV], float(E - 1), None, ALU.min))
            nc.vector.tensor_copy(itab[:, 0:1 + NOV], tf[:, 0:1 + NOV]).then_inc(s_slot, 2)
            dve.wait_ge(s_slot, 3)

            def mlo(bi, j):
                dve.wait_ge(m_hi, count_of(bi, j))
                sl = split[split_slot(bi, j)]
                tt_(sl[1], raw[j], f(sl[0]), ALU.subtract).then_inc(m_lo, 1)

            def x_lo(bi, par):
                for c in range(2):
                    dve.wait_ge(m_th, 2 * bi + c + 1)
                    tt_(xgT[par][1][:, 4 * c:4 * c + 4, :], bank[c][:, :].rearrange("p (k t) -> p k t", k=4),
                        f(xgT[par][0][:, 4 * c:4 * c + 4, :]), ALU.subtract).then_inc(m_tl, 1)

            def h_lo(bi):
                dve.wait_ge(m_hh, bi + 1)
                tt_(hT[1][:, :, :], bank[4][:, :].rearrange("p (k t) -> p k t", k=4), f(hT[0][:, :, :]),
                    ALU.subtract).then_inc(m_hl, 1)

            def y_half(bi, par):
                dve.wait_ge(m_use, down_count(bi))
                if not (isinstance(bi, int) and bi < 2):
                    dve.wait_ge(m_st[par], store_count(bi, par))
                nc.vector.tensor_copy(ysb[par][:, 512:D], bank[6][:, :]).then_inc(m_yd, 1)

            def hidden(bi):
                dve.wait_ge(m_use, up_count(bi))
                dve.wait_ge(m_sg, bi + 1)
                if not (isinstance(bi, int) and bi == 0):
                    dve.wait_ge(m_ht, bi)
                tt_(hbuf, silu_g, bank[3][:, :], ALU.mult).then_inc(m_h, 1)

            def step(bi, par):
                first, last = isinstance(bi, int) and bi == 0, isinstance(bi, int) and bi == E - 1
                if not first:
                    mlo(bi, 2)
                    h_lo(bi - 1)
                    mlo(bi, 3)
                if first:
                    mlo(1, 0)
                else:
                    mlo(bi, 4)
                mlo(bi, 5)
                if not last and not first:
                    mlo(bi + 1, 0)
                if not first:
                    y_half(bi - 1, 1 - par)
                if not last:
                    x_lo(bi + 1, 1 - par)
                    mlo(bi + 1, 1)
                hidden(bi)

            x_lo(0, 0)
            step(0, 0)
            step(1, 1)
            step(2, 0)
            with dve.Fori(0, (E - 4) // 2) as i:
                step(2 * i + 3, 1)
                step(2 * i + 4, 0)
            step(E - 1, 1)
            mlo(E, 2)
            h_lo(E - 1)
            mlo(E, 3)
            y_half(E - 1, 1)
            dve.wait_ge(s_slot, 3)
            n_over = dve.value_load(itab[0:1, 0:1], min_val=0, max_val=NOV)
            with dve.If(0 < n_over):
                with dve.Fori(0, NOV // 2) as i:
                    for par in range(2):
                        v = 2 * i + par
                        with dve.If(v < n_over):
                            x_lo(E + v, par)
                            for s, j in enumerate(OV_ORDER):
                                if s == 4:
                                    h_lo(E + v)
                                dve.wait_ge(m_hi, 6 * E + 6 * v + s + 1)
                                tt_(split[s % 3][1], raw[j], f(split[s % 3][0]), ALU.subtract).then_inc(m_lo, 1)
                                if s == 3:
                                    dve.wait_ge(m_ht, E + v)
                                    dve.wait_ge(m_use, 6 * E + 6 * v + 4)
                                    dve.wait_ge(m_sg, E + v + 1)
                                    tt_(hbuf, silu_g, bank[3][:, :], ALU.mult).then_inc(m_h, 1)
                            dve.wait_ge(m_use, 6 * E + 6 * v + 6)
                            dve.wait_ge(m_st[par], 16 * (E // 2) + 16 * i)
                            nc.vector.tensor_copy(ysb[par][:, 512:D], bank[6][:, :]).then_inc(m_yd, 1)
            dve.wait_ge(s_ax, 1)
            dve.wait_ge(s_lnp2, 32)

            def final_gain(tt):
                dve.wait_ge(s_fnr, tt + 1)
                ins = tt_(xr[:, tt, :], xr[:, tt, :], ln[:, 2, :], ALU.mult)
                if tt < NTT - 1:
                    ins.then_inc(s_fg, 1)
                else:
                    link(ins)
                    tt_(xr[:, tt, :], xr[:, tt, :], ln[:, 3, :], ALU.add).then_inc(s_y1, 1)

            for tt in range(NTT):
                rows = P if tt < 4 else NS
                dve.wait_ge(s_ga[tt], 32)
                for n, y in enumerate((y_a, y_b)):
                    g = gw[0:rows, n * NTT + tt:n * NTT + tt + 1]
                    link(stt(xr[0:rows, tt, :], y[0:rows, tt, :], g, xr[0:rows, tt, :], ALU.mult, ALU.add))
                for g in range(2):
                    nc.vector.bn_stats(stats[:, tt, 6 * g:6 * g + 6], xr[:, tt, 512 * g:512 * g + 512]).then_inc(s_dv, 1)
                chain[0] += 2
                dve.wait_ge(s_dv, chain[0])
                nc.vector.bn_aggr(mv1[:, tt, :], stats[:, tt, :]).then_inc(s_fvar, 1)
                if tt:
                    final_gain(tt - 1)
                shift_scale(tt, s_fstd, s_fnm)
            final_gain(NTT - 1)

        @block.tensor
        def _(pe):
            mm, tr = nc.tensor.matmul, nc.tensor.transpose
            pe.wait_ge(s_const, 16)
            for m in range(2 * NTT):
                tt, hf = m // 2, m % 2
                rows = P if tt < 4 else NS
                pe.wait_ge(s_x[tt], 16)
                if m >= 7:
                    pe.wait_ge(s_xl, m - 6)
                for j in range(4):
                    kt = 4 * hf + j
                    last = tr(bank[m % 7][:, j * rows:(j + 1) * rows], xn[0:rows, tt, kt * P:(kt + 1) * P],
                              ident[0:rows, 0:rows])
                last.then_inc(s_xt, 1)
            pe.wait_ge(s_par, 64)
            tr(bank[7][:, 0:84], sq[0:84, 0, 0:P], ident[0:84, 0:84]).then_inc(s_pt, 1)
            pe.wait_ge(s_xl, 2 * NTT)
            pe.wait_ge(s_pp, 1)

            def project(o):
                pe.wait_ge(s_lo, o + 1)
                wh, wl = chunk_weights(o % 2, 0), chunk_weights(o % 2, 1)
                for n in tiles_of(o):
                    kind, _, j = TILES[n]
                    if n >= 2:
                        wait_evacuated(pe, bank_before(n))
                    pb, ps = tile_banks(n)
                    if kind in TOKEN_MAJOR:
                        rows = P if j < 4 else NS
                        for kt in range(KT):
                            for i, (x_, w_) in enumerate(((0, wh), (0, wl), (1, wh))):
                                last = mm(pb[0:rows, 0:CW], xT[x_][:, kt, tok(j)], w_[:, kt, :],
                                          start=(kt == 0 and i == 0), stop=(kt == KT - 1 and i == 2))
                    else:
                        for kt in range(KT):
                            for i, (w_, x_) in enumerate(((wh, 0), (wh, 1), (wl, 0))):
                                first, end = kt == 0 and i == 0, kt == KT - 1 and i == 2
                                lhs = w_[:, kt, j * P:(j + 1) * P]
                                mm(pb[:, 0:HT], lhs, xT[x_][:, kt, 0:HT], start=first, stop=end)
                                last = mm(ps[:, 0:HT], lhs, xT[x_][:, kt, HT:T], start=first, stop=end)
                    last.then_inc(s_tile, 1)
                    if o == NCH - 1 and j:
                        spread(2 * j - 2)
                        spread(2 * j - 1)

            def spread(m):
                if m == 0:
                    pe.wait_ge(s_crc, 1)
                if m >= 2:
                    pe.wait_ge(s_cf, m - 1)
                mm(bank[6 + m % 2][:, 0:HT], groups_t[:, m // 2, :], r_conv[:, (m % 2) * HT:(m % 2 + 1) * HT],
                   start=True, stop=True).then_inc(s_cbc, 1)

            def pairs(li):
                if li == 0:
                    pe.wait_ge(s_eva, 8)
                else:
                    pe.wait_ge(s_z, li)
                lf, rf = (k, q) if li == 0 else (ex[(li - 1) % 2], ex[(li - 1) % 2])
                if li <= SLEVELS:
                    if li:
                        pe.wait_ge(s_ps, li)
                    for h in range(H):
                        last = mm(bank[7][0:NS, h * NS:(h + 1) * NS], lf[:, h, SEQ:T], rf[:, h, SEQ:T], start=True, stop=True)
                for h in range(H):
                    p = li * H + h
                    if p >= 3:
                        pe.wait_ge(s_pc, p - 2)
                    for c in range(NC):
                        cols = slice(c * P, (c + 1) * P)
                        last = mm(bank[4 + p % 3][:, cols], lf[:, h, cols], rf[:, h, cols], start=True, stop=True)
                    last.then_inc(s_p, 1)

            for o_ in range(NCH):
                project(o_)
                li = o_ - FIRST_LEVEL_STEP + 1
                if 0 <= li <= LEVELS:
                    pairs(li)

                if o_ == 7:
                    pe.wait_ge(s_ps, SLEVELS + 1)
                    for j in range(4):
                        last = tr(bank[7][0:8, j * P:(j + 1) * P], groups[:, j, :], ident)
                    last.then_inc(s_selt, 1)
                if o_ == 11:
                    pe.wait_ge(s_cb, 4)
                    pe.wait_ge(s_sel, 1)
                    for j in range(4):
                        last = tr(bank[7][0:18, j * P:(j + 1) * P], cb[:, j, :], ident)
                    last.then_inc(s_cbt, 1)
                if o_ == 12:
                    pe.wait_ge(s_kx, 1)
                    for m in range(H + 1):
                        if m >= 2:
                            pe.wait_ge(s_ktc, m - 1)
                        if m < H:
                            for c in range(NC):
                                last = tr(bank[4 + m % 2][:, c * P:(c + 1) * P], k[:, m, c * P:(c + 1) * P], ident)
                        else:
                            for h in range(H):
                                last = tr(bank[4][0:NS, h * P:(h + 1) * P], k[:, h, SEQ:T], ident)
                        last.then_inc(s_kt, 1)
                    pe.wait_ge(s_csq, 1)
                    pe.wait_ge(s_cbo, 1)
                    pe.wait_ge(s_pc, NP_LEVELS)
                    for g in range(2):
                        for j in range(4):
                            last = mm(bank[6 + g][0:8, 0:HT], groups[:, j, :], sq[:, j, g * HT:(g + 1) * HT],
                                      start=(j == 0), stop=(j == 3))
                        last.then_inc(s_cms, 1)
            wait_evacuated(pe, len(TILES) - 1)
            pe.wait_ge(s_ktc, H + 1)
            pe.wait_ge(s_qx, 1)

            def update(c):
                if c >= 2:
                    pe.wait_ge(s_st, c - 1)
                for h in range(H):
                    last = mm(bank[4 + c % 2][:, h * P:(h + 1) * P], k_tok[:, h, c, :], v_tok[:, c, h * P:(h + 1) * P],
                              start=True, stop=True)
                last.then_inc(s_su, 1)

            def prompt_o(c):
                cols = slice(c * P, (c + 1) * P)
                if c:
                    pe.wait_ge(s_st, c)
                for h in range(H):
                    vh = slice(h * P, (h + 1) * P)
                    last = mm(bank[c][:, vh], att[:, h, c, :], v_tok[:, c, vh], start=True, stop=(c == 0))
                    if c:
                        last = mm(bank[c][:, vh], q[:, h, cols], state[:, c - 1, h, :], start=False, stop=True)
                last.then_inc(s_o, 1)

            update(0)
            update(1)
            prompt_o(0)
            prompt_o(1)
            update(2)
            update(3)
            prompt_o(2)
            prompt_o(3)
            pe.wait_ge(s_cf, 8)
            pe.wait_ge(s_s0, 16)
            pe.wait_ge(s_qm, 1)

            def turn_o(i):
                rows = P if i < 4 else NS
                pe.wait_ge(s_on, i + 1)
                for h in range(H):
                    last = tr(o_bank(i)[:, h * rows:(h + 1) * rows], o_n[i % 2][0:rows, h * P:(h + 1) * P],
                              ident[0:rows, 0:rows])
                last.then_inc(s_ot, 1)

            for h in range(H):
                vh = slice(h * P, (h + 1) * P)
                mm(bank[6][0:NS, vh], att_s[0:NS, h, :], v_tok[0:NS, 4, vh], start=True, stop=False)
                for bi in range(DB):
                    last = mm(bank[6][0:NS, vh], q_msk[:, h, bi, :], s0[:, bi, h, :], start=False, stop=(bi == DB - 1))
                if h == H - 1:
                    last.then_inc(s_o, 1)
                turn_o(h)
            pe.wait_ge(s_cl, 4)
            pe.wait_ge(s_st, NC)
            for c in range(NWO):
                pe.wait_ge(s_lo, NCH + c + 1)
                wh, wl = chunk_weights((NCH + c) % 2, 0), chunk_weights((NCH + c) % 2, 1)
                for tt in range(NTT):
                    n = c * NTT + tt
                    rows = P if tt < 4 else NS
                    if c == 0:
                        pe.wait_ge(s_ol, tt + 1)
                    if n >= 4:
                        pe.wait_ge(s_wc, n - 3)
                    for kt in range(KT):
                        for i, (x_, w_) in enumerate(((0, wh), (0, wl), (1, wh))):
                            last = mm(w_bank(n)[0:rows, 0:CW], xT[x_][:, kt, tok(tt)], w_[:, kt, :],
                                      start=(kt == 0 and i == 0), stop=(kt == KT - 1 and i == 2))
                    last.then_inc(s_w, 1)
                    if n == 0:
                        turn_o(NTT - 1)
                if c < NWO - 1:
                    for h, g in ((c, 0), (c, 1)) if c < 2 else ((2, 0), (2, 1), (3, 0), (3, 1)):
                        pe.wait_ge(s_vm, h + 1)
                        if h:
                            pe.wait_ge(s_s0n, 2 * h + g - 1)
                        mm(bank[1 + g][:, :], k_tok_s[0:NS, h, :], v_msk[0:NS, 4 * g:4 * g + 4, :],
                           start=True, stop=True).then_inc(s_sus, 1)
            def logits(g):
                t0, t1 = 2 * g * P, min((2 * g + 2) * P, T)
                pe.wait_ge(s_1c, min(4 * g + 4, 2 * NTT))
                pb = bank[5 + g][0:E, 0:t1 - t0]
                for kt in range(KT):
                    last = mm(pb, wr[:, kt, :], x1T[g][:, kt, :], start=(kt == 0), stop=(kt == KT - 1))
                last.then_inc(s_lgt, 1)

            pe.wait_ge(s_s0n, 2 * H)
            pe.wait_ge(s_wr, 32)
            for tt in range(NTT):
                if tt < POOL_LN:
                    pe.wait_ge(s_x1, tt + 1)
                else:
                    pe.wait_ge(s_x1d, tt - POOL_LN + 1)
                rows = P if tt < 4 else NS
                for hf in range(2):
                    m = 2 * tt + hf
                    if m == 2:
                        pe.wait_ge(s_wc, NWO * NTT)
                    if m >= 4:
                        pe.wait_ge(s_1c, m - 3)
                    for j in range(4):
                        kt = 4 * hf + j
                        last = tr(bank[1 + m % 4][:, j * rows:(j + 1) * rows], xr[0:rows, tt, kt * P:(kt + 1) * P],
                                  ident[0:rows, 0:rows])
                    last.then_inc(s_1t, 1)
                if tt in (2, 4):
                    logits(tt // 2 - 1)
            logits(2)
            pe.wait_ge(s_lgs, 1)
            for tt in range(NTT):
                rows = P if tt < 4 else NS
                last = tr(bank[3][0:rows, tt * E:(tt + 1) * E], lg[:, tok(tt)], ident[0:E, 0:E])
            last.then_inc(s_lg, 1)
            pe.wait_ge(s_oh, 1)
            mm(bank[4][:, 0:NE], tri, choice, start=True, stop=True)
            mm(bank[4][:, NE:2 * NE], ones, choice, start=True, stop=True).then_inc(s_rk, 1)

            def x_turn(bi, par):
                pe.wait_ge(m_xg[par], 8 * (bi - par) + 16)
                if not (isinstance(bi, int) and bi == 0):
                    pe.wait_ge(m_tl, 2 * bi)
                for c in range(2):
                    for t in range(4):
                        last = tr(bank[c][:, t * P:(t + 1) * P], xg[par][:, c * 512 + t:(c + 1) * 512:4], ident)
                last.then_inc(m_t, 1)

            def gate_up(out, par, slot, c, wait):
                pe.wait_ge(m_lo, wait)
                w = [split[slot][i].rearrange("p (t n) -> p t n", t=4) for i in range(2)]
                for t in range(4):
                    kt = 4 * c + t
                    for i, (x_, w_) in enumerate(((0, 0), (0, 1), (1, 0))):
                        last = mm(out[:, :], xgT[par][x_][:, kt, :], w[w_][:, t, :],
                                  start=(kt == 0 and i == 0), stop=(kt == KT - 1 and i == 2))
                last.then_inc(m_use, 1)

            def down(slot, c, wait):
                pe.wait_ge(m_lo, wait)
                w = [split[slot][i].rearrange("p (t n) -> p t n", t=2) for i in range(2)]
                for t in range(2):
                    kt = 2 * c + t
                    for i, (x_, w_) in enumerate(((0, 0), (0, 1), (1, 0))):
                        for g in range(2):
                            last = mm(bank[5 + g][:, :], hT[x_][:, kt, :], w[w_][:, t, 512 * g:512 * g + 512],
                                      start=(kt == 0 and i == 0), stop=(kt == 3 and i == 2))
                last.then_inc(m_use, 1)

            def h_turn(bi):
                pe.wait_ge(m_h, bi + 1)
                if not (isinstance(bi, int) and bi == 0):
                    pe.wait_ge(m_hl, bi)
                for kt in range(4):
                    c, t = kt // 2, kt % 2
                    last = tr(bank[4][:, kt * P:(kt + 1) * P], hbuf[:, c * 256 + t:(c + 1) * 256:2], ident)
                last.then_inc(m_ht, 1)

            def down_ready(bi):
                pe.wait_ge(m_hl, bi + 1)
                if not (isinstance(bi, int) and bi == 0):
                    pe.wait_ge(m_ya, bi)
                    pe.wait_ge(m_yd, bi)

            def step(bi, par):
                first, last = isinstance(bi, int) and bi == 0, isinstance(bi, int) and bi == E - 1
                pe.wait_ge(m_tl, 2 * bi + 2)
                if not first:
                    pe.wait_ge(m_sg, bi)
                gate_up(bank[2], par, 0, 0, count_of(bi, 0))
                if not first:
                    h_turn(bi - 1)
                gate_up(bank[2], par, 1, 1, count_of(bi, 1))
                if not first:
                    down_ready(bi - 1)
                    down(2, 0, count_of(bi, 2))
                    down(0, 1, count_of(bi, 3))
                if not last:
                    x_turn(bi + 1, 1 - par)
                gate_up(bank[3], par, split_slot(bi, 4), 0, count_of(bi, 4))
                gate_up(bank[3], par, split_slot(bi, 5), 1, count_of(bi, 5))

            x_turn(0, 0)
            step(0, 0)
            step(1, 1)
            step(2, 0)
            with pe.Fori(0, (E - 4) // 2) as i:
                step(2 * i + 3, 1)
                step(2 * i + 4, 0)
            step(E - 1, 1)
            h_turn(E - 1)
            down_ready(E - 1)
            down(2, 0, count_of(E, 2))
            down(0, 1, count_of(E, 3))
            pe.wait_ge(s_slot, 3)
            n_over = pe.value_load(itab[0:1, 0:1], min_val=0, max_val=NOV)
            with pe.If(0 < n_over):
                with pe.Fori(0, NOV // 2) as i:
                    for par in range(2):
                        v = 2 * i + par
                        with pe.If(v < n_over):
                            base = 6 * E + 6 * v
                            x_turn(E + v, par)
                            pe.wait_ge(m_tl, 2 * (E + v) + 2)
                            pe.wait_ge(m_sg, E + v)
                            gate_up(bank[2], par, 0, 0, base + 1)
                            gate_up(bank[2], par, 1, 1, base + 2)
                            gate_up(bank[3], par, 2, 0, base + 3)
                            gate_up(bank[3], par, 0, 1, base + 4)
                            h_turn(E + v)
                            down_ready(E + v)
                            down(1, 0, base + 5)
                            down(2, 1, base + 6)


_INS = ["x_prompt", "x_sample", "state_hgrn", "state_conv", "w_in", "w_out", "hgrn_norm_g", "conv_w", "conv_norm_g",
        "ln1_g", "ln1_b", "ln2_g", "ln2_b", "w_router", "router_bias", "w_gate", "w_up", "w_down"]
_OUTS = [("out_prompt", (1, SEQ, D)), ("out_sample", (DB, DS, D)), ("out_hgrn_prompt", (1, 1, H, P, P)),
         ("out_conv_prompt", (1, 1, 2, 512)), ("out_hgrn_sample", (1, DB, H, P, P)), ("out_conv_sample", (1, DB, 2, 512))]


def kernel(**inputs):
    import concourse.bacc as bacc
    from concourse.bass_utils import run_bass_kernel_spmd

    nc = bacc.Bacc("TRN2", target_bir_lowering=False, num_devices=1)
    const_f32, const_mask = constants()
    arrays = {name: np.ascontiguousarray(inputs[name]) for name in _INS}
    arrays["const_f32"], arrays["const_mask"] = const_f32, const_mask
    aps = {name: nc.dram_tensor(name, x.shape, mybir.dt.from_np(x.dtype), kind="ExternalInput").ap()
           for name, x in arrays.items()}
    for name, shape in _OUTS:
        aps[name] = nc.dram_tensor(name, shape, F32, kind="ExternalOutput").ap()
    build(nc, aps)
    r = run_bass_kernel_spmd(nc, [arrays], core_ids=[0])
    return tuple(r.results[0][name] for name, _ in _OUTS)
```

```python
from contextlib import ExitStack

import numpy as np

import concourse.bass as bass
from concourse import mybir

F32 = mybir.dt.float32
F32R = mybir.dt.float32r
U8 = mybir.dt.uint8
I32 = mybir.dt.int32
U32 = mybir.dt.uint32
ALU = mybir.AluOpType
ACT = mybir.ActivationFunctionType
AX = mybir.AxisListType.X

P = 128
D = 1024
KT = D // P
SEQ, DB, DS = 512, 8, 4
NS = DB * DS
T = SEQ + NS
HT = T // 2
NTT = (T + P - 1) // P
H = 4
NC = SEQ // P
LEVELS = 7
SLEVELS = 2
CW = 256
N_IN = 3584
NCH = N_IN // CW
NWO = D // CW
UW = 2 + SEQ + DB * (2 + DS)
E, TOPG, FF = 16, 4, 512
NRAW = 8
RING = 4
NOV = 8
NBLK = E + NOV
ALPHA = float(2 ** 0.25)
LN_EPS, RMS_EPS = 1e-5, 1e-6

ORDER = [("f", 2), ("f", 3), ("q", 0), ("q", 1), ("v", 4), ("v", 5), ("gc", 10), ("gc", 11),
         ("cx", 12), ("cx", 13), ("gb", 8), ("gb", 9), ("g", 6), ("g", 7)]


TOKEN_MAJOR = ("v", "g")


def out_tiles():
    out = []
    for o, (kind, _) in enumerate(ORDER):
        out += [(kind, o, j) for j in range(NTT if kind in TOKEN_MAJOR else CW // P)]
    return out


TILES = out_tiles()
POOL_LN = 3
BY_DVE = ("cx", "gb")
FIRST_LEVEL_STEP = 5

C_ID, C_TRI, C_ONE, C_SEL, C_RST, C_SM = 0, 128, 256, 384, 416, 416 + T
C_QM = C_SM + 90
C_IO = C_QM + DB * NS
C_N = C_IO + P
SM_E16, SM_G4, SM_VAL, SM_SEQ, SM_TOK, SM_BLK = 0, 16, 20, 25, 33, 38


def constants():
    p = np.arange(P)
    c = np.zeros((P, C_N), np.float32)
    c[:, C_ID:C_ID + P] = np.eye(P)
    c[:, C_TRI:C_TRI + P] = p[:, None] < p[None, :]
    for j in range(4):
        c[:, C_SEL + 8 * j:C_SEL + 8 * j + 8] = 2 * j + p[:, None] // 64 == np.arange(8)[None, :]
    c[:, C_ONE:C_ONE + P] = 1.0
    t = np.arange(T)
    c[:, C_RST:C_RST + T] = np.where(t < SEQ, t % P != 0, (t - SEQ) % DS != 0)
    s = c[:, C_SM:]
    s[:, SM_E16:SM_E16 + E] = E - np.arange(E)
    s[:, SM_BLK:SM_BLK + NBLK + 1] = P * np.arange(NBLK + 1)
    s[:, SM_TOK:SM_TOK + NTT] = np.arange(NTT)[None, :] * P + p[:, None]
    c[:, C_IO:C_IO + P] = np.arange(P)[None, :]
    s[:, SM_G4:SM_G4 + TOPG] = TOPG - np.arange(TOPG)
    s[:, SM_VAL:SM_VAL + NTT] = (np.arange(NTT)[None, :] * P + p[:, None]) < T
    s[:, SM_SEQ:SM_SEQ + DB] = (p[:, None] // DS) == np.arange(DB)[None, :]
    c[:, C_QM:C_QM + DB * NS] = (np.arange(NS)[None, :] // DS == np.arange(DB)[:, None]).reshape(1, -1)
    m = np.zeros((P, LEVELS, P), np.float32)
    for l in range(LEVELS):
        L = 1 << l
        m[:, l, :] = ((p[:, None] // (2 * L) == p[None, :] // (2 * L)) & (p[:, None] % (2 * L) < L)
                      & (p[None, :] % (2 * L) >= L))
    return c, m.reshape(P, LEVELS * P)


def build(nc, a):
    ctx = ExitStack()

    def sem(name):
        return ctx.enter_context(nc.semaphore(name))

    with ctx:
        x1_dram = nc.dram_tensor("x1_by_token", (T, D), F32, kind="Internal").ap()
        yg_dram = nc.dram_tensor("y_by_slot", (NBLK * P, D), F32, kind="Internal").ap()

        FW = 35472
        FA = ctx.enter_context(nc.sbuf_tensor("FA", [P, FW], F32))
        RA = ctx.enter_context(nc.sbuf_tensor("RA", [P, 68 * 256], F32R))
        masks = ctx.enter_context(nc.sbuf_tensor("masks", [P, LEVELS * P], U8))
        itab = ctx.enter_context(nc.sbuf_tensor("itab", [P, 16], I32))
        ids = ctx.enter_context(nc.sbuf_tensor("ids", [P, NBLK], I32))
        slot_i = ctx.enter_context(nc.sbuf_tensor("slot_i", [P, 2 * NTT], I32))
        bank = [ctx.enter_context(nc.psum_tensor(f"bank{i}", [P, 512], F32)) for i in range(8)]

        def fa(off, n):
            return FA[:, off:off + n]

        const = fa(0, C_N)
        ident, tri = const[:, C_ID:C_ID + P], const[:, C_TRI:C_TRI + P]
        ones = const[:, C_ONE:C_ONE + P]
        groups = const[:, C_SEL:C_SEL + 32].rearrange("p (j g) -> p j g", j=4)
        reset = const[:, C_RST:C_RST + T]
        groups_t = const[0:8, C_RST:C_RST + 4 * P].rearrange("p (j c) -> p j c", j=4)
        small = const[:, C_SM:C_SM + 90]
        o_small = C_N
        params = fa(o_small, 88)
        p_decay = fa(o_small + 88, H * NC).rearrange("p (h c) -> p h c", h=H)
        s0_decay = fa(o_small + 88 + H * NC, DB * H)
        rt = fa(o_small + 136, 464)
        assert o_small + 600 <= 2048
        K = 256
        raw = [fa(8 * K + 2048 * i, 2048) for i in range(6)]
        raw += [fa(68 * K, 2048), fa(68 * K + 2 * H * T, 2048)]
        s0 = fa(32 * K, 4096).rearrange("p (b h v) -> p b h v", b=DB, h=H)
        A0 = 48 * K
        xn = fa(A0, NTT * D).rearrange("p (t n) -> p t n", t=NTT)
        v_tok = fa(A0, NTT * 512).rearrange("p (t n) -> p t n", t=NTT)
        sg = fa(A0 + NTT * 512, NTT * 512).rearrange("p (t n) -> p t n", t=NTT)
        Q0 = 68 * K
        heads = lambda off: fa(off, H * T).rearrange("p (h t) -> p h t", h=H)
        q, k, b = heads(Q0), heads(Q0 + H * T), heads(Q0 + 2 * H * T)
        Z0 = Q0 + 3 * H * T
        z = heads(Z0)
        yc = heads(Z0)
        E0 = Z0 + H * T
        ex = [heads(E0), heads(E0 + H * T)]
        AT0 = E0 + 2 * H * T
        att = fa(AT0, H * NC * P).rearrange("p (h c t) -> p h c t", h=H, c=NC)
        att_s = fa(AT0 + H * NC * P, H * NS).rearrange("p (h t) -> p h t", h=H)
        U0 = AT0 + H * NC * P + H * NS
        u = fa(U0, 4 * UW).rearrange("p (j t) -> p j t", j=4)
        sq = heads(U0)
        SQ0 = U0 + 4 * UW
        cb = fa(SQ0, 4 * 18).rearrange("p (j t) -> p j t", j=4)
        cb_out = fa(SQ0 + 72, 512)
        assert SQ0 + 72 + 512 <= FW, (SQ0 + 584, FW)
        k_tok = fa(E0 + H * T, H * NC * P).rearrange("p (h c k) -> p h c k", h=H, c=NC)
        state = fa(E0, NC * H * P).rearrange("p (c h v) -> p c h v", c=NC, h=H)
        k_tok_s = fa(Q0 + H * T, 512).rearrange("p (h k) -> p h k", h=H)
        v_msk = fa(Q0 + H * T + 512, DB * P).rearrange("p (b v) -> p b v", b=DB)
        h_gain = fa(Q0 + H * T + 1536, 512)
        B0 = Q0 + 2 * H * T
        o_sq = [fa(B0, 512), fa(B0 + 512, 512)]
        o_n = [fa(B0 + 1024, 512), fa(B0 + 1536, 512)]
        q_msk = fa(U0, H * DB * NS).rearrange("p (h b t) -> p h b t", h=H, b=DB)
        r_conv = fa(B0 + 1024, T)[0:8, :]
        xr = fa(E0, NTT * D).rearrange("p (t n) -> p t n", t=NTT)
        ln = fa(Q0, 4 * D).rearrange("p (i n) -> p i n", i=4)
        x1T = [fa(U0, 2 * D).rearrange("p (k t) -> p k t", k=KT),
               fa(B0, 2 * D).rearrange("p (k t) -> p k t", k=KT),
               fa(Z0 + 1024, KT * NS).rearrange("p (k t) -> p k t", k=KT)]
        row_hot = fa(B0, 2 * NTT * P).rearrange("p (s r) -> p s r", s=2 * NTT)
        from_blk = fa(B0 + 2 * NTT * P, 2 * NTT * (NBLK + 1)).rearrange("p (s b) -> p s b", s=2 * NTT)
        in_blk = fa(B0 + 1536, 2 * NTT * NBLK).rearrange("p (s b) -> p s b", s=2 * NTT)
        lg = fa(Z0 + 1024 + KT * NS, T)[0:E, :]
        xg = [fa(56 * K, D), fa(60 * K, D)]
        wr = fa(Z0, KT * E).rearrange("p (k e) -> p k e", k=KT)
        silu_g, hbuf = fa(64 * K, 512), fa(66 * K, 512)
        ysb = [fa(U0, D), fa(U0 + D, D)]
        y_a, y_b = fa(8 * K, NTT * D).rearrange("p (t n) -> p t n", t=NTT), \
            fa(28 * K, NTT * D).rearrange("p (t n) -> p t n", t=NTT)

        split = [[RA[:, (8 * (2 * s + w)) * K:(8 * (2 * s + w) + 8) * K] for w in range(2)] for s in range(3)]
        xT = [RA[:, 32 * K + w * KT * T:32 * K + (w + 1) * KT * T].rearrange("p (k t) -> p k t", k=KT)
              for w in range(2)]
        xgT = [[RA[:, (48 + 8 * par + 4 * w) * K:(52 + 8 * par + 4 * w) * K].rearrange("p (k t) -> p k t", k=KT)
                for w in range(2)] for par in range(2)]
        hT = [RA[:, (64 + 2 * w) * K:(66 + 2 * w) * K].rearrange("p (k t) -> p k t", k=4) for w in range(2)]

        s_const, s_mask, s_par, s_s0 = sem("const_in"), sem("mask_in"), sem("param_in"), sem("s0_in")
        s_x = [sem(f"x_in{i}") for i in range(NTT)]
        s_raw = [sem(f"raw_in{i}") for i in range(3)]
        s_hi, s_lo, s_tile = sem("hi_done"), sem("lo_done"), sem("tile_made")
        s_eva, s_evd = sem("evacuated_by_act"), sem("evacuated_by_dve")
        s_xt, s_xh, s_xl = sem("x_transposed"), sem("xT_hi"), sem("xT_lo")
        s_pt, s_pp = sem("param_transposed"), sem("param_ready")
        s_zero, s_fill = sem("zero_tile"), sem("slots_filled")
        s_abs, s_lnf, s_b = sem("abs_z"), sem("ln1p"), sem("b_ready")
        s_d, s_e, s_z, s_p, s_pc = sem("exponent"), sem("decay"), sem("decayed_qk"), sem("pairs"), sem("pairs_used")
        s_ps = sem("sample_pairs_used")
        s_qx, s_kx = sem("q_decayed"), sem("k_decayed")
        s_cb, s_cbt, s_cbo, s_cbs = sem("conv_tail"), sem("conv_tail_t"), sem("conv_tail_out"), sem("conv_state_stored")
        s_kt, s_ktc = sem("k_transposed"), sem("k_token_major")
        s_su, s_st, s_o, s_oc = sem("state_update"), sem("state_ready"), sem("o_made"), sem("o_copied")
        s_vm, s_sus, s_s0n, s_sto = sem("v_masked"), sem("sample_update"), sem("sample_state"), sem("sample_states_stored")
        s_stp = sem("prompt_state_stored")
        s_selt, s_sel = sem("groups_transposed"), sem("groups_t_ready")
        s_csq, s_cms, s_crt, s_crc, s_cbc = (sem("conv_squares"), sem("conv_mean_square"), sem("conv_root"),
                                             sem("conv_reciprocal"), sem("conv_scale_spread"))
        s_cf, s_ch, s_cl = sem("conv_row_f32"), sem("conv_row_hi"), sem("conv_row_lo")
        s_hg, s_sg = sem("o_gain_in"), sem("silu_g_scaled")
        s_qm = sem("q_masked")
        s_osq, s_red, s_ort, s_on, s_ot, s_oh_, s_ol = (sem("o_squares"), sem("o_mean_square"), sem("o_root"), sem("o_normed"),
                                                       sem("o_transposed"), sem("o_hi"), sem("o_lo"))
        s_s0d = sem("s0_decayed")
        s_xr, s_lnp, s_lnp2, s_wr = sem("residual_in"), sem("ln1_params_in"), sem("ln2_params_in"), sem("router_in")
        s_xr0 = sem("residual_zeroed")
        s_w, s_wc = sem("mix_out"), sem("mix_added")
        s_var, s_std, s_nm, s_nrm, s_xgn, s_x1, s_x1d = (sem("ln_var"), sem("ln_std"), sem("ln_shift"), sem("ln_normed"),
                                                  sem("ln_scaled"), sem("ln_out_by_pool"), sem("ln_out_by_dve"))
        s_1t, s_1c, s_lgt, s_lgs, s_lg = (sem("x1_transposed"), sem("x1T_copied"), sem("logits_expert_major"),
                                                 sem("logits_copied"), sem("logits_token_major"))
        s_rl, s_re = sem("logit_shifted"), sem("logit_exp")
        s_oh, s_rk, s_slot = sem("choice"), sem("rank"), sem("slots")
        s_hot, s_tab, s_ids, s_x1s = sem("slot_indicators"), sem("token_table"), sem("token_ids"), sem("x1_stored")
        s_dv, s_ac = sem("dve_chain"), sem("act_chain")
        m_raw = [sem(f"moe_raw_in{i}") for i in range(NRAW)]
        m_xg = [sem(f"moe_x_in{i}") for i in range(2)]
        m_t, m_th, m_tl = sem("moe_x_transposed"), sem("moe_xT_hi"), sem("moe_xT_lo")
        m_hi, m_lo, m_use = sem("moe_hi"), sem("moe_lo"), sem("moe_chunk_used")
        m_sg, m_h, m_ht, m_hh, m_hl = sem("moe_silu"), sem("moe_h"), sem("moe_h_transposed"), sem("moe_hT_hi"), sem("moe_hT_lo")
        m_ya, m_yd = sem("moe_y_act"), sem("moe_y_dve")
        m_st = [sem(f"moe_y_stored{i}") for i in range(2)]
        s_ga = [sem(f"rows_gathered{i}") for i in range(NTT)]
        s_ax, s_fvar, s_fstd, s_fnm, s_fnr, s_fg = (sem("x1_times_alpha"), sem("final_var"), sem("final_std"), sem("final_shift"),
                                                    sem("final_normed"), sem("final_scaled"))
        s_yp, s_y1, s_out = sem("final_out_by_pool"), sem("final_out_by_dve"), sem("out_stored")

        block = ctx.enter_context(nc.Block())

        act_tiles = [n for n, (kind, _, _) in enumerate(TILES) if kind not in BY_DVE]
        dve_tiles = [n for n, (kind, _, _) in enumerate(TILES) if kind in BY_DVE]

        def wait_evacuated(eng, n):
            if n in act_tiles:
                eng.wait_ge(s_eva, act_tiles.index(n) + 1)
            else:
                eng.wait_ge(s_evd, dve_tiles.index(n) + 1)

        def tile_banks(n):
            return (bank[n % 4], None) if TILES[n][0] in TOKEN_MAJOR else (bank[n % 2], bank[2 + n % 2])

        def bank_before(n):
            both = TILES[n][0] in TOKEN_MAJOR and TILES[n - 2][0] in TOKEN_MAJOR
            return n - 4 if both else n - 2

        def tiles_of(o):
            return [n for n, t in enumerate(TILES) if t[1] == o]

        def halves(view, L, n):
            w = view[:, :, 0:n].rearrange("p h (n s l) -> p h n s l", s=2, l=L)
            return w[:, :, :, 0, :], w[:, :, :, 1, :], w[:, :, :, 0, L - 1:L]

        def conv_pieces(h, pb, ps):
            us = u[:, h, 2 + SEQ:UW].rearrange("p (b t) -> p b t", b=DB)
            return [(u[:, h, 2:2 + HT], pb[:, 0:HT]), (u[:, h, 2 + HT:2 + SEQ], ps[:, 0:SEQ - HT]),
                    (us[:, :, 2:2 + DS], ps[:, SEQ - HT:HT].rearrange("p (b t) -> p b t", b=DB))]

        def chunk_weights(s, w):
            return split[s][w].rearrange("p (k n) -> p k n", k=KT)

        def tok(tt):
            return slice(tt * P, min((tt + 1) * P, T))

        NP_LEVELS = (LEVELS + 1) * H

        OV_ORDER = (0, 1, 4, 5, 2, 3)
        mv1 = rt[:, 8:8 + 2 * NTT].rearrange("p (t s) -> p t s", s=2)
        eps_rms, eps_ln = rt[:, 20:21], rt[:, 21:22]
        shift = rt[:, 128:128 + NTT]
        stats = rt[:, 24:24 + 12 * NTT].rearrange("p (t s) -> p t s", t=NTT)
        NE = NTT * E
        ra = lambda i: rt[:, 88 + i * NE:88 + (i + 1) * NE]
        t3 = lambda v: v.rearrange("p (t e) -> p t e", t=NTT)
        t4 = lambda v: v.rearrange("p (x e) -> p x e", e=TOPG)
        r_l, r_p, r_o1, r_o2 = ra(0), ra(1), ra(2), ra(3)
        R0 = Z0 + KT * E
        rb = lambda i, n: fa(R0 + i, n)

        gw = rt[:, 408:418]
        choice = fa(R0 + 640, NE)

        def o_bank(tt):
            return bank[6] if tt == NTT - 1 else bank[tt]

        def w_bank(n):
            return bank[(7, 4, 5, 0)[n % 4]]

        ss, root = rt[:, 88:88 + 4 * NTT], rt[:, 108:108 + 4 * NTT]

        def raw_place(n, i=0):
            return n % NRAW, 16 * (n // NRAW + 1) + 16 * (6 * RING // NRAW) * i

        def gate_count(bi):
            return 2 if isinstance(bi, int) and bi == 0 else 6 * bi + 0

        def up_count(bi):
            return 4 if isinstance(bi, int) and bi == 0 else 6 * bi + 4

        def down_count(bi):
            if isinstance(bi, int) and bi == E - 1:
                return 6 * E
            return 6 * (bi + 1) + 2

        def store_count(bi, par):
            return 8 * (bi - par)

        def count_of(bi, j):
            if isinstance(bi, int) and bi == 0:
                return {0: 1, 1: 2, 4: 3, 5: 5}[j]
            if isinstance(bi, int) and bi == 1 and j == 0:
                return 4
            if isinstance(bi, int) and bi == E:
                return 6 * E - 2 + j - 1
            return 6 * bi + j - 1

        def slot_free_count(bi, j):
            if isinstance(bi, int) and bi == 0:
                return 2 if j == 5 else None
            if isinstance(bi, int) and bi == 1 and j < 3:
                return (1, 4, 3)[j]
            if isinstance(bi, int) and bi == E:
                return used_count(E - 1, j + 1)
            if j >= 3:
                return used_count(bi, j - 3)
            return used_count(bi - 1, j + 3)

        def used_count(bi, j):
            if isinstance(bi, int) and bi == 0:
                return {0: 1, 1: 2, 4: 3, 5: 4}[j]
            if isinstance(bi, int) and bi == E:
                return 6 * E - 2 + j - 1
            return 6 * bi + j - 1

        def split_slot(bi, j):
            if isinstance(bi, int) and bi == 0:
                return {0: 0, 1: 1, 4: 2, 5: 1}[j]
            if isinstance(bi, int) and bi == E:
                return j - 2
            return j % 3

        @block.sync
        def _(sp):
            sp.dma_start(const, a["const_f32"]).then_inc(s_const, 16)
            w_in = a["w_in"][0].rearrange("(k p) n -> p k n", p=P)
            w_out = a["w_out"][0].rearrange("(k p) n -> p k n", p=P)

            def load_w(c):
                src = w_in[:, :, ORDER[c][1] * CW:(ORDER[c][1] + 1) * CW] if c < NCH \
                    else w_out[:, :, (c - NCH) * CW:(c - NCH + 1) * CW]
                sp.dma_start(raw[c % 3].rearrange("p (k n) -> p k n", k=KT), src).then_inc(s_raw[c % 3], 16)

            for tt in range(4):
                sp.dma_start(xn[:, tt, :], a["x_prompt"][0, tt * P:(tt + 1) * P, :]).then_inc(s_x[tt], 16)
            sp.dma_start(xn[0:NS, 4, :], a["x_sample"].rearrange("b t n -> (b t) n")).then_inc(s_x[4], 16)
            load_w(0)
            pr = sq[:, 0, 0:P]
            sp.dma_start(fa(E0, LEVELS * P), a["const_mask"]).then_inc(s_mask, 16)
            sp.dma_start(pr[0:4, :], a["hgrn_norm_g"].rearrange("a (t p) -> (a t) p", p=P)).then_inc(s_par, 16)
            sp.dma_start(pr[4:16, :], a["conv_w"].rearrange("a j (t p) -> (a j t) p", p=P)).then_inc(s_par, 16)
            sp.dma_start(pr[16:20, :], a["conv_norm_g"].rearrange("a (t p) -> (a t) p", p=P)).then_inc(s_par, 16)
            sp.dma_start(pr[20:84, :], a["state_conv"].rearrange("a b j (t p) -> (a b j t) p", p=P)).then_inc(s_par, 16)
            for c in range(1, NCH + NWO):
                if c >= 3:
                    sp.wait_ge(s_lo, c - 2)
                load_w(c)
                if c == NCH:
                    sp.wait_ge(s_fill, 16)
                    sp.dma_start(s0, a["state_hgrn"][0].rearrange("b h k v -> k b h v")).then_inc(s_s0, 16)
            sp.wait_ge(s_cbo, 1)
            sp.dma_start(a["out_conv_prompt"][0, 0, :, :], cb_out[0:2, :]).then_inc(s_cbs, 16)
            sp.dma_start(a["out_conv_sample"][0].rearrange("b j n -> (b j) n"), cb_out[2:18, :]).then_inc(s_cbs, 16)
            sp.wait_ge(s_kt, H + 1)
            sp.dma_start(h_gain, a["hgrn_norm_g"].broadcast_to([P, 512])).then_inc(s_hg, 16)
            sp.wait_ge(s_st, NC)
            sp.dma_start(a["out_hgrn_prompt"][0, 0].rearrange("h k v -> k h v"), state[:, NC - 1, :, :]).then_inc(s_stp, 16)
            sp.wait_ge(s_stp, 16)
            sp.wait_ge(s_o, NTT)
            sp.wait_ge(s_xr0, 1)
            sp.dma_start(xr[:, 0:4, :], a["x_prompt"][0].rearrange("(t p) n -> p t n", p=P)).then_inc(s_xr, 16)
            sp.dma_start(xr[0:NS, 4, :], a["x_sample"].rearrange("b t n -> (b t) n")).then_inc(s_xr, 16)
            for i, name in enumerate(("ln1_g", "ln1_b")):
                sp.dma_start(ln[:, i, :], a[name].broadcast_to([P, D])).then_inc(s_lnp, 16)
            sp.wait_ge(s_cl, 4)
            sp.dma_start(wr, a["w_router"].rearrange("(k p) e -> p k e", p=P)).then_inc(s_wr, 16)
            sp.dma_start(rt[:, 448:464], a["router_bias"].unsqueeze(0).broadcast_to([P, E])).then_inc(s_wr, 16)
            sp.wait_ge(s_s0n, 2 * H)
            sp.dma_start(a["out_hgrn_sample"][0].rearrange("b h k v -> k b h v"), s0).then_inc(s_sto, 16)
            for i, name in ((2, "ln2_g"), (3, "ln2_b")):
                sp.dma_start(ln[:, i, :], a[name].broadcast_to([P, D])).then_inc(s_lnp2, 16)

            w_gu = [a["w_gate"][0], a["w_up"][0]]

            def gu_src(which, e, c):
                w = w_gu[which][e] if isinstance(e, int) else w_gu[which][bass.ds(e, 1)].squeeze(0)
                return w[c * 512:(c + 1) * 512, :].rearrange("(p t) n -> p (t n)", t=4)

            def d_src(e, c):
                w = a["w_down"][0][e] if isinstance(e, int) else a["w_down"][0][bass.ds(e, 1)].squeeze(0)
                return w[c * 256:(c + 1) * 256, :].rearrange("(p t) n -> p (t n)", t=2)

            def load(n, src):
                slot, _ = raw_place(n)
                sp.dma_start(raw[slot], src).then_inc(m_raw[slot], 16)

            def source(j, e, ep):
                return gu_src(0, e, j) if j < 2 else d_src(ep, j - 2) if j < 4 else gu_src(1, e, j - 4)

            def moe_loads(bi, s, chunks=range(6)):
                for j in chunks:
                    sp.wait_ge(m_lo, count_of(bi, j) - NRAW)
                    load(count_of(s, j) - 1, source(j, bi, bi - 1))

            sp.wait_ge(s_sto, 16)
            load(4, source(5, 0, None))
            load(5, source(1, 1, 0))
            load(3, source(0, 1, 0))
            sp.wait_ge(s_lo, NCH + NWO - 2)
            load(0, source(0, 0, None))
            sp.wait_ge(s_lo, NCH + NWO - 1)
            load(1, source(1, 0, None))
            sp.wait_ge(s_lo, NCH + NWO)
            load(2, source(4, 0, None))
            sp.wait_ge(s_on, NTT)
            for tt in range(NTT):
                if tt < POOL_LN:
                    sp.wait_ge(s_x1, tt + 1)
                else:
                    sp.wait_ge(s_x1d, tt - POOL_LN + 1)
                rows = P if tt < 4 else NS
                sp.dma_start(x1_dram[tt * P:tt * P + rows, :], xr[0:rows, tt, :]).then_inc(s_x1s, 16)
            load(6, source(2, 1, 0))
            moe_loads(1, 1, (4, 5))
            moe_loads(2, 2, (0,))
            sp.wait_ge(m_t, 1)
            load(7, source(3, 1, 0))
            moe_loads(2, 2, range(1, 6))
            with sp.Fori(0, (E - 4) // RING) as i:
                for s in range(3, 3 + RING):
                    moe_loads(RING * i + s, s)
            moe_loads(E - 1, E - 1)
            moe_loads(E, E, (2, 3))
            sp.wait_ge(s_slot, 3)
            n_over = sp.value_load(itab[0:1, 0:1], min_val=0, max_val=NOV)
            with sp.If(0 < n_over):
                with sp.Fori(0, NOV // RING) as i:
                    for r in range(RING):
                        v = RING * i + r
                        with sp.If(v < n_over):
                            e = sp.value_load(itab[0:1, bass.ds(v + 1, 1)], min_val=0, max_val=E - 1)
                            for o, j in enumerate(OV_ORDER):
                                sp.wait_ge(m_lo, 6 * E + 6 * v + o + 1 - NRAW)
                                load(6 * E + 6 * r + o, source(j, e, e))
            for tt in range(NTT):
                if tt < NTT - 1:
                    sp.wait_ge(s_yp, tt + 1)
                else:
                    sp.wait_ge(s_y1, 1)
                if tt < 4:
                    sp.dma_start(a["out_prompt"][0, tt * P:(tt + 1) * P, :], xr[:, tt, :]).then_inc(s_out, 16)
                else:
                    sp.dma_start(a["out_sample"].rearrange("b t n -> (b t) n"), xr[0:NS, tt, :]).then_inc(s_out, 16)
            sp.wait_ge(s_out, 16 * NTT)
            sp.wait_ge(s_cbs, 32)
            sp.wait_ge(s_sto, 16)
            sp.wait_ge(s_stp, 16)

        @block.gpsimd
        def _(pool):
            nc.gpsimd.memset(fa(32 * K, D), 0.0).then_inc(s_zero, 1)
            pool.wait_ge(s_zero, 1)
            pool.wait_ge(s_xl, 2 * NTT)
            fill_src = fa(32 * K, D).unsqueeze(1).broadcast_to([P, NOV, D])
            pool.wait_ge(s_lo, 2)
            pool.dma_start(yg_dram[E * P:NBLK * P, :].rearrange("(b p) n -> p b n", p=P), fill_src).then_inc(s_fill, 16)

            def exponents(l):
                L, n = 1 << l, T if l < SLEVELS else SEQ
                if l >= 2:
                    pool.wait_ge(s_p, H * l)
                bl, br, mid = halves(b, L, n)
                dl, dr, _ = halves(ex[l % 2], L, n)
                mb = mid.broadcast_to(list(bl.shape))
                nc.gpsimd.tensor_tensor(dr, br, mb, ALU.subtract)
                nc.gpsimd.tensor_tensor(dl, mb, bl, ALU.subtract).then_inc(s_d, 1)

            pool.wait_ge(s_b, H)
            for l in range(LEVELS):
                exponents(l)
            pool.wait_ge(s_p, NP_LEVELS)
            for (c0, c1, w) in ((0, SEQ, P), (SEQ, T, DS)):
                bv = b[:, :, c0:c1].rearrange("p h (c t) -> p h c t", t=w)
                dv = ex[0][:, :, c0:c1].rearrange("p h (c t) -> p h c t", t=w)
                last = nc.gpsimd.tensor_tensor(dv, bv[:, :, :, w - 1:w].broadcast_to(list(bv.shape)), bv, ALU.subtract)
            last.then_inc(s_d, 1)
            pool.wait_ge(s_qx, 1)
            pool.wait_ge(s_cms, 2)
            seq_cols = const[:, C_QM:C_QM + DB * NS].rearrange("p (b t) -> p b t", b=DB)
            for h in range(H):
                last = nc.gpsimd.tensor_tensor(q_msk[:, h], q[:, h, SEQ:T].unsqueeze(1).broadcast_to([P, DB, NS]), seq_cols, ALU.mult)
            last.then_inc(s_qm, 1)
            pool.wait_ge(s_hg, 16)
            for o in (NCH - 2, NCH - 1):
                half = slice((o % 2) * CW, (o % 2) * CW + CW)
                pool.wait_ge(s_eva, act_tiles.index(tiles_of(o)[-1]) + 1)
                nc.gpsimd.tensor_tensor(sg[:, 0:4, half], sg[:, 0:4, half],
                                        h_gain[:, half].unsqueeze(1).broadcast_to([P, 4, CW]), ALU.mult)
                nc.gpsimd.tensor_tensor(sg[0:NS, 4, half], sg[0:NS, 4, half], h_gain[0:NS, half], ALU.mult).then_inc(s_sg, 1)
            seq_mask = small[0:NS, SM_SEQ:SM_SEQ + DB].unsqueeze(2).broadcast_to([NS, DB, P])

            def mask_values(h):
                nc.gpsimd.tensor_tensor(v_msk[0:NS], v_tok[0:NS, 4, h * P:(h + 1) * P].unsqueeze(1).broadcast_to([NS, DB, P]),
                                        seq_mask, ALU.mult).then_inc(s_vm, 1)

            mask_values(0)
            pool.wait_ge(s_stp, 16)
            pool.wait_ge(s_o, NTT)
            nc.gpsimd.memset(xr[:, 4, :], 0.0).then_inc(s_xr0, 1)
            nc.gpsimd.tensor_tensor(s0.rearrange("p b h v -> p (b h) v"), s0.rearrange("p b h v -> p (b h) v"),
                                    s0_decay.unsqueeze(2).broadcast_to([P, DB * H, P]), ALU.mult).then_inc(s_s0d, 1)
            for h in range(1, H):
                pool.wait_ge(s_sus, 2 * h)
                mask_values(h)
            pool.wait_ge(s_lnp, 32)
            for tt in range(POOL_LN):
                pool.wait_ge(s_xgn, tt + 1)
                nc.gpsimd.tensor_tensor(xr[:, tt, :], xr[:, tt, :], ln[:, 1, :], ALU.add).then_inc(s_x1, 1)
            for n, j in enumerate((0, 1, 4)):
                pool.wait_ge(m_hi, n + 1)
                sl = split[split_slot(0, j)]
                nc.gpsimd.tensor_tensor(sl[1], raw[n], sl[0].bitcast(F32), ALU.subtract).then_inc(m_lo, 1)
            def gather(bi, par):
                pool.indirect_dma_start(
                    out=xg[par], out_offset=None, in_=x1_dram,
                    in_offset=bass.IndirectOffsetOnAxis(ap=ids[:, bi:bi + 1].bitcast(U32), axis=0)).then_inc(m_xg[par], 16)

            pool.wait_ge(s_x1s, 16 * NTT)
            pool.wait_ge(s_ids, 1)
            gather(0, 0)
            gather(1, 1)
            pool.wait_ge(m_t, 1)
            gather(2, 0)

            def times_alpha(tiles):
                for tt in tiles:
                    nc.gpsimd.tensor_scalar(xr[:, tt, :], xr[:, tt, :], ALPHA, None, ALU.mult).then_inc(s_ax, 1)

            y_slot = yg_dram.rearrange("(b p) n -> b p n", p=P)

            def store(bi, par):
                pool.wait_ge(m_ya, bi + 1)
                pool.wait_ge(m_yd, bi + 1)
                pool.dma_start(y_slot[bi], ysb[par]).then_inc(m_st[par], 16)

            def step(bi, par):
                pool.wait_ge(m_t, bi)
                if bi < E - 1:
                    gather(bi + 1, 1 - par)
                store(bi - 2, par)

            for bi in range(2, E):
                if bi - 2 < NTT:
                    times_alpha((bi - 2,))
                step(bi, bi % 2)
            store(E - 2, 0)
            store(E - 1, 1)
            for par in range(2):
                pool.wait_ge(m_st[par], 16 * (E // 2))
            pool.wait_ge(s_slot, 3)
            n_over = pool.value_load(itab[0:1, 0:1], min_val=0, max_val=NOV)
            with pool.If(0 < n_over):
                for v in range(NOV):
                    with pool.If(v < n_over):
                        pool.wait_ge(m_t, E + v)
                        gather(E + v, v % 2)
                        store(E + v, v % 2)
                        pool.wait_ge(m_st[v % 2], 16 * (E // 2) + 16 * (v // 2 + 1))
            for tt in range(NTT):
                rows = NS if tt == NTT - 1 else P
                for n, dst in enumerate((y_a, y_b)):
                    pool.indirect_dma_start(
                        out=dst[0:rows, tt, :], out_offset=None, in_=yg_dram,
                        in_offset=bass.IndirectOffsetOnAxis(ap=slot_i[0:rows, 5 * n + tt:5 * n + tt + 1].bitcast(U32), axis=0)).then_inc(s_ga[tt], 16)
            for tt in range(NTT - 1):
                pool.wait_ge(s_fg, tt + 1)
                nc.gpsimd.tensor_tensor(xr[:, tt, :], xr[:, tt, :], ln[:, 3, :], ALU.add).then_inc(s_yp, 1)
            for par in range(2):
                pool.wait_ge(m_st[par], 16 * (E // 2))

        @block.scalar
        def _(act):
            chain = [0]

            def link(ins):
                chain[0] += 1
                ins.then_inc(s_ac, 1)
                act.wait_ge(s_ac, chain[0])

            for m in range(2 * NTT):
                tt, hf = m // 2, m % 2
                n = P if tt < 4 else NS
                act.wait_ge(s_xt, m + 1)
                src = bank[m % 7][:, 0:4 * n].rearrange("p (k t) -> p k t", k=4)
                nc.scalar.activation(xT[0][:, 4 * hf:4 * hf + 4, tok(tt)], src, ACT.Copy).then_inc(s_xh, 1)
            act.wait_ge(s_pt, 1)
            nc.scalar.activation(params[:, 0:84], bank[7][:, 0:84], ACT.Copy).then_inc(s_pp, 1)

            def hi(o):
                act.wait_ge(s_raw[o % 3], 16 * (o // 3 + 1))
                if 2 <= o < NCH + 2:
                    act.wait_ge(s_tile, tiles_of(o - 2)[-1] + 1)
                elif o >= NCH + 2:
                    act.wait_ge(s_w, NTT * (o - 1 - NCH))
                nc.scalar.activation(split[o % 2][0], raw[o % 3], ACT.Copy).then_inc(s_hi, 1)

            def evacuate(o):
                for n in tiles_of(o):
                    kind, _, j = TILES[n]
                    if kind in BY_DVE:
                        continue
                    act.wait_ge(s_tile, n + 1)
                    pb, ps = tile_banks(n)
                    if kind in TOKEN_MAJOR:
                        rows = P if j < 4 else NS
                        dst, func = (v_tok, ACT.Copy) if kind == "v" else (sg, ACT.Silu)
                        nc.scalar.activation(dst[0:rows, j, (o % 2) * CW:(o % 2) * CW + CW], pb[0:rows, 0:CW],
                                             func).then_inc(s_eva, 1)
                        continue
                    h = 2 * (o % 2) + j
                    cols = [(pb[:, 0:HT], slice(0, HT)), (ps[:, 0:HT], slice(HT, T))]
                    if kind == "f":
                        for src, c in cols:
                            nc.scalar.activation(z[:, h, c], src, ACT.Copy)
                        for src, c in cols:
                            last = nc.scalar.activation(k[:, h, c], src, ACT.Sigmoid, scale=-1.0)
                        last.then_inc(s_eva, 1)
                    elif kind == "gc":
                        for dst, src in conv_pieces(h, pb, ps):
                            last = nc.scalar.activation(dst, src, ACT.Copy)
                        last.then_inc(s_eva, 1)
                    else:
                        for src, c in cols:
                            last = nc.scalar.activation(q[:, h, c], src, ACT.Silu)
                        last.then_inc(s_eva, 1)

            for o in range(NCH + 1):
                if o >= 2:
                    evacuate(o - 2)
                hi(o)
                if o == 4:
                    act.wait_ge(s_abs, 1)
                    link(nc.scalar.activation(ex[0][:, :, :], ex[0][:, :, :], ACT.Exp, scale=-1.0))
                    nc.scalar.activation(ex[0][:, :, :], ex[0][:, :, :], ACT.Ln, bias=1.0).then_inc(s_lnf, 1)
                l = o - FIRST_LEVEL_STEP
                if 0 <= l < LEVELS:
                    act.wait_ge(s_d, l + 1)
                    n = T if l < SLEVELS else SEQ
                    nc.scalar.activation(ex[l % 2][:, :, 0:n], ex[l % 2][:, :, 0:n], ACT.Exp).then_inc(s_e, 1)
                if o == 9:
                    act.wait_ge(s_selt, 1)
                    act.wait_ge(s_b, H)
                    nc.scalar.activation(const[0:8, C_RST:C_RST + 4 * P], bank[7][0:8, :], ACT.Copy).then_inc(s_sel, 1)
                if o == NCH - 1:
                    act.wait_ge(s_p, H * LEVELS)
                    nc.scalar.activation(ex[1][:, :, :], b[:, :, :], ACT.Exp).then_inc(s_e, 1)
                    act.wait_ge(s_d, LEVELS + 1)
                    nc.scalar.activation(ex[0][:, :, :], ex[0][:, :, :], ACT.Exp).then_inc(s_e, 1)
                    act.wait_ge(s_evd, len(dve_tiles))
                    nc.scalar.activation(sq[:, :, :], yc[:, :, :], ACT.Square).then_inc(s_csq, 1)
                    act.wait_ge(s_cbt, 1)
                    nc.scalar.activation(cb_out[0:18, :], bank[7][0:18, :], ACT.Copy).then_inc(s_cbo, 1)
                if o == NCH:
                    for g in range(2):
                        act.wait_ge(s_cms, g + 1)
                        nc.scalar.activation(r_conv[:, g * HT:(g + 1) * HT], bank[6 + g][0:8, 0:HT], ACT.Sqrt,
                                             bias=eps_rms[0:8, :], scale=1.0 / 64).then_inc(s_crt, 1)
            evacuate(NCH - 1)
            for j in range(4):
                act.wait_ge(s_cf, 2 * j + 2)
                nc.scalar.activation(xT[0][:, 4 + j, :], yc[:, j, :], ACT.Copy).then_inc(s_ch, 1)
            hi(NCH + 1)

            def o_squares(i):
                tt = i
                rows = P if tt < 4 else NS
                act.wait_ge(s_o, i + 1)
                if i >= 2:
                    act.wait_ge(s_red, i - 1)
                nc.scalar.activation(o_sq[i % 2][0:rows, :], o_bank(tt)[0:rows, :], ACT.Square).then_inc(s_osq, 1)

            def o_hi(i):
                tt = i
                rows = P if tt < 4 else NS
                act.wait_ge(s_ot, i + 1)
                nc.scalar.activation(xT[0][:, 0:4, tok(tt)], o_bank(tt)[:, 0:4 * rows].rearrange("p (h t) -> p h t", h=H),
                                     ACT.Copy).then_inc(s_oh_, 1)

            o_squares(0)
            for i in range(NTT):
                rows = P if i < 4 else NS
                if i + 1 < NTT:
                    o_squares(i + 1)
                act.wait_ge(s_red, i + 1)
                nc.scalar.activation(root[0:rows, 4 * i:4 * i + 4], ss[0:rows, 4 * i:4 * i + 4], ACT.Sqrt,
                                     bias=eps_rms[0:rows, :], scale=1.0 / P).then_inc(s_ort, 1)
                if i:
                    o_hi(i - 1)
            o_hi(NTT - 1)
            hi(NCH + 2)
            hi(NCH + 3)
            def normalise(tt):
                act.wait_ge(s_var, tt + 1)
                nc.scalar.activation(rt[:, tt:tt + 1], mv1[:, tt, 1:2], ACT.Sqrt, bias=eps_ln).then_inc(s_std, 1)
                act.wait_ge(s_nm, tt + 1)
                nc.scalar.activation(xr[:, tt, :], xr[:, tt, :], ACT.Identity, bias=shift[:, tt:tt + 1],
                                     scale=rt[:, tt:tt + 1]).then_inc(s_nrm, 1)

            def copy_x1T(tt):
                n = P if tt < 4 else NS
                for hf in range(2):
                    m = 2 * tt + hf
                    act.wait_ge(s_1t, m + 1)
                    nc.scalar.activation(x1T[tt // 2][:, 4 * hf:4 * hf + 4, (tt % 2) * P:(tt % 2) * P + n],
                                         bank[1 + m % 4][:, 0:4 * n].rearrange("p (k t) -> p k t", k=4), ACT.Copy).then_inc(s_1c, 1)

            for tt in range(NTT - 1):
                normalise(tt)
            copy_x1T(0)
            normalise(NTT - 1)
            for tt in range(1, NTT):
                copy_x1T(tt)
            for g in range(3):
                act.wait_ge(s_lgt, g + 1)
                n = 2 * P if g < 2 else NS
                last = nc.scalar.activation(lg[:, 2 * g * P:2 * g * P + n], bank[5 + g][0:E, 0:n], ACT.Copy)
            last.then_inc(s_lgs, 1)
            act.wait_ge(s_rl, 1)
            nc.scalar.activation(r_p, r_l, ACT.Exp).then_inc(s_re, 1)
            for n, j in enumerate((0, 1, 4)):
                act.wait_ge(m_raw[n], 16)
                nc.scalar.activation(split[split_slot(0, j)][0], raw[n], ACT.Copy).then_inc(m_hi, 1)

            def mhi(bi, j, s=None, i=0):
                place, loaded = raw_place(count_of(bi if s is None else s, j) - 1, i)
                act.wait_ge(m_raw[place], loaded)
                f = slot_free_count(bi, j)
                if f is not None:
                    act.wait_ge(m_use, f)
                nc.scalar.activation(split[split_slot(bi, j)][0], raw[place], ACT.Copy).then_inc(m_hi, 1)

            def x_hi(bi, par):
                for c in range(2):
                    act.wait_ge(m_t, bi + 1)
                    nc.scalar.activation(xgT[par][0][:, 4 * c:4 * c + 4, :], bank[c][:, :].rearrange("p (k t) -> p k t", k=4),
                                         ACT.Copy).then_inc(m_th, 1)

            def h_hi(bi):
                act.wait_ge(m_ht, bi + 1)
                nc.scalar.activation(hT[0][:, :, :], bank[4][:, :].rearrange("p (k t) -> p k t", k=4),
                                     ACT.Copy).then_inc(m_hh, 1)

            def silu(bi):
                act.wait_ge(m_use, gate_count(bi))
                if not (isinstance(bi, int) and bi == 0):
                    act.wait_ge(m_h, bi)
                nc.scalar.activation(silu_g, bank[2][:, :], ACT.Silu).then_inc(m_sg, 1)

            def y_half(bi, par):
                act.wait_ge(m_use, down_count(bi))
                if not (isinstance(bi, int) and bi < 2):
                    act.wait_ge(m_st[par], store_count(bi, par))
                nc.scalar.activation(ysb[par][:, 0:512], bank[5][:, :], ACT.Copy).then_inc(m_ya, 1)

            def step(bi, par, s=None, i=0):
                first, last = isinstance(bi, int) and bi == 0, isinstance(bi, int) and bi == E - 1
                after = None if s is None else s + 1
                if not first:
                    mhi(bi, 2, s, i)
                    h_hi(bi - 1)
                    mhi(bi, 3, s, i)
                if first:
                    mhi(1, 0)
                else:
                    mhi(bi, 4, s, i)
                silu(bi)
                mhi(bi, 5, s, i)
                if not last and not first:
                    mhi(bi + 1, 0, after, i)
                if last:
                    mhi(E, 2)
                if not first:
                    y_half(bi - 1, 1 - par)
                if not last:
                    x_hi(bi + 1, 1 - par)
                    mhi(bi + 1, 1, after, i)

            x_hi(0, 0)
            step(0, 0)
            step(1, 1)
            step(2, 0)
            with act.Fori(0, (E - 4) // RING) as i:
                for s in range(3, 3 + RING):
                    step(RING * i + s, s % 2, s, i)
            step(E - 1, 1)
            mhi(E, 3)
            h_hi(E - 1)
            y_half(E - 1, 1)
            act.wait_ge(s_slot, 3)
            n_over = act.value_load(itab[0:1, 0:1], min_val=0, max_val=NOV)
            with act.If(0 < n_over):
                with act.Fori(0, NOV // RING) as i:
                    for r in range(RING):
                        v, par = RING * i + r, r % 2
                        with act.If(v < n_over):
                            x_hi(E + v, par)
                            for s in range(6):
                                if s == 4:
                                    h_hi(E + v)
                                place, loaded = raw_place(6 * E + 6 * r + s, i)
                                act.wait_ge(m_raw[place], loaded)
                                act.wait_ge(m_use, 6 * E + 6 * v if s < 3 else 6 * E + 6 * v + s - 2)
                                nc.scalar.activation(split[s % 3][0], raw[place], ACT.Copy).then_inc(m_hi, 1)
                                if s == 3:
                                    act.wait_ge(m_use, 6 * E + 6 * v + 2)
                                    act.wait_ge(m_h, E + v)
                                    nc.scalar.activation(silu_g, bank[2][:, :], ACT.Silu).then_inc(m_sg, 1)
                            act.wait_ge(m_use, 6 * E + 6 * v + 6)
                            act.wait_ge(m_st[par], 16 * (E // 2 + r // 2) + 8 * RING * i)
                            nc.scalar.activation(ysb[par][:, 0:512], bank[5][:, :], ACT.Copy).then_inc(m_ya, 1)
            for tt in range(NTT):
                act.wait_ge(s_fvar, tt + 1)
                nc.scalar.activation(rt[:, tt:tt + 1], mv1[:, tt, 1:2], ACT.Sqrt, bias=eps_ln).then_inc(s_fstd, 1)
                act.wait_ge(s_fnm, tt + 1)
                nc.scalar.activation(xr[:, tt, :], xr[:, tt, :], ACT.Identity, bias=shift[:, tt:tt + 1],
                                     scale=rt[:, tt:tt + 1]).then_inc(s_fnr, 1)

        @block.vector
        def _(dve):
            tt_, ts_, stt = nc.vector.tensor_tensor, nc.vector.tensor_scalar, nc.vector.scalar_tensor_tensor
            chain = [0]

            def link(ins):
                chain[0] += 1
                ins.then_inc(s_dv, 1)
                dve.wait_ge(s_dv, chain[0])

            f = lambda r: r.bitcast(F32)
            nc.vector.memset(eps_rms, RMS_EPS)
            link(nc.vector.memset(eps_ln, LN_EPS))
            for m in range(2 * NTT):
                tt, hf = m // 2, m % 2
                n = P if tt < 4 else NS
                dve.wait_ge(s_xh, m + 1)
                src = bank[m % 7][:, 0:4 * n].rearrange("p (k t) -> p k t", k=4)
                tt_(xT[1][:, 4 * hf:4 * hf + 4, tok(tt)], src, f(xT[0][:, 4 * hf:4 * hf + 4, tok(tt)]),
                    ALU.subtract).then_inc(s_xl, 1)

            dve.wait_ge(s_const, 16)

            def lo(o):
                dve.wait_ge(s_hi, o + 1)
                tt_(split[o % 2][1], raw[o % 3], f(split[o % 2][0]), ALU.subtract).then_inc(s_lo, 1)

            par_g = lambda base, j: params[:, base + j:base + j + 1]

            def evacuate(o):
                for n in tiles_of(o):
                    kind, _, j = TILES[n]
                    if kind not in BY_DVE:
                        continue
                    dve.wait_ge(s_tile, n + 1)
                    pb, ps = tile_banks(n)
                    h = 2 * (o % 2) + j
                    if kind == "cx":
                        if o == 8 and j == 0:
                            dve.wait_ge(s_eva, act_tiles.index(tiles_of(7)[1]) + 1)
                            dve.wait_ge(s_pp, 1)
                        us = u[:, h, 2 + SEQ:UW].rearrange("p (b t) -> p b t", b=DB)
                        link(nc.vector.memset(u[:, h, 0:2], 0.0))
                        for dst, src in conv_pieces(h, pb, ps):
                            last = tt_(dst, dst, src, ALU.mult)
                        last.then_inc(s_evd, 1)
                        link(nc.vector.tensor_copy(us[:, :, 0:2],
                                                   params[:, 20:84].rearrange("p (b j t) -> p b j t", b=DB, j=2)[:, :, :, h]))
                        dve.wait_ge(s_evd, dve_tiles.index(n) + 1)
                        yp, ys = yc[:, h, 0:SEQ], yc[:, h, SEQ:T].rearrange("p (b t) -> p b t", b=DB)
                        ts_(yp, u[:, h, 0:SEQ], par_g(4, h), None, ALU.mult)
                        link(ts_(ys, us[:, :, 0:DS], par_g(4, h), None, ALU.mult))
                        for jj in (1, 2):
                            stt(yp, u[:, h, jj:jj + SEQ], par_g(4 + 4 * jj, h), yp, ALU.mult, ALU.add)
                            link(stt(ys, us[:, :, jj:jj + DS], par_g(4 + 4 * jj, h), ys, ALU.mult, ALU.add))
                        nc.vector.tensor_copy(cb[:, h, 0:2], u[:, h, SEQ:SEQ + 2])
                        nc.vector.tensor_copy(cb[:, h, 2:18].rearrange("p (b t) -> p b t", b=DB),
                                              us[:, :, DS:DS + 2]).then_inc(s_cb, 1)
                    else:
                        tt_(yc[:, h, 0:HT], yc[:, h, 0:HT], pb[:, 0:HT], ALU.mult)
                        tt_(yc[:, h, HT:T], yc[:, h, HT:T], ps[:, 0:HT], ALU.mult).then_inc(s_evd, 1)

            def decayed(l):
                L, n = 1 << l, T if l < SLEVELS else SEQ
                dve.wait_ge(s_e, l + 1)
                dl, dr, _ = halves(ex[l % 2], L, n)
                _, qr, _ = halves(q, L, n)
                kl, _, _ = halves(k, L, n)
                tt_(dr, dr, qr, ALU.mult)
                tt_(dl, dl, kl, ALU.mult).then_inc(s_z, 1)

            def take_pairs(li):
                for h in range(H):
                    p = li * H + h
                    dve.wait_ge(s_p, p + 1)
                    src = bank[4 + p % 3][:, :].rearrange("p (c t) -> p c t", c=NC)
                    if li == 0:
                        tt_(att[:, h, :, :], src, ident.unsqueeze(1).broadcast_to([P, NC, P]), ALU.mult).then_inc(s_pc, 1)
                    else:
                        m = masks[:, (li - 1) * P:li * P].unsqueeze(1).broadcast_to([P, NC, P])
                        nc.vector.copy_predicated(att[:, h, :, :], m, src).then_inc(s_pc, 1)
                if li <= SLEVELS:
                    src = bank[7][0:NS, 0:H * NS].rearrange("p (h t) -> p h t", h=H)
                    if li == 0:
                        tt_(att_s[0:NS], src, ident[0:NS, 0:NS].unsqueeze(1).broadcast_to([NS, H, NS]), ALU.mult).then_inc(s_ps, 1)
                    else:
                        m = masks[0:NS, (li - 1) * P:(li - 1) * P + NS].unsqueeze(1).broadcast_to([NS, H, NS])
                        nc.vector.copy_predicated(att_s[0:NS], m, src).then_inc(s_ps, 1)
                    dve.wait_ge(s_ps, li + 1)
                dve.wait_ge(s_pc, H * (li + 1))

            for o_ in range(NCH + 1):
                if o_ >= 2:
                    evacuate(o_ - 2)
                l = o_ - FIRST_LEVEL_STEP
                if 0 <= l - 1 <= LEVELS:
                    take_pairs(l - 1)
                lo(o_)
                if o_ == 0:
                    dve.wait_ge(s_mask, 16)
                    link(nc.vector.tensor_copy(masks[:, :], fa(E0, LEVELS * P)))
                if o_ == 3:
                    dve.wait_ge(s_eva, 4)
                    stt(ex[0][:, :, :], z[:, :, :], -1.0, z[:, :, :], ALU.mult, ALU.max).then_inc(s_abs, 1)
                if o_ == 4:
                    dve.wait_ge(s_lnf, 1)
                    link(stt(z[:, :, :], z[:, :, :], 0.0, ex[0][:, :, :], ALU.min, ALU.subtract))
                    for h in range(H):
                        nc.vector.tensor_tensor_scan(b[:, h, :], reset, z[:, h, :], 0.0, ALU.mult, ALU.add).then_inc(s_b, 1)
                    dve.wait_ge(s_b, H)
                if 0 <= l - 1 < LEVELS:
                    if l == 1:
                        dve.wait_ge(s_eva, 8)
                    decayed(l - 1)
                if o_ == NCH - 1:
                    dve.wait_ge(s_e, LEVELS + 1)
                    tt_(q[:, :, :], q[:, :, :], ex[1][:, :, :], ALU.mult).then_inc(s_qx, 1)
                    nc.vector.tensor_copy(p_decay, ex[1][:, :, P - 1:SEQ:P])
                    link(nc.vector.tensor_copy(s0_decay.rearrange("p (b h) -> p h b", h=H), ex[1][:, :, SEQ + DS - 1:T:DS]))
                    dve.wait_ge(s_e, LEVELS + 2)
                    tt_(k[:, :, :], k[:, :, :], ex[0][:, :, :], ALU.mult).then_inc(s_kx, 1)
                    for h in range(H):
                        dve.wait_ge(s_kt, h + 1)
                        nc.vector.tensor_copy(k_tok[:, h, :, :], bank[4 + h % 2][:, :].rearrange("p (c k) -> p c k", c=NC)).then_inc(s_ktc, 1)
                    dve.wait_ge(s_kt, H + 1)
                    nc.vector.tensor_copy(k_tok_s[0:NS], bank[4][0:NS, :].rearrange("p (h k) -> p h k", h=H)).then_inc(s_ktc, 1)
            dve.wait_ge(s_crt, 2)
            nc.vector.reciprocal(r_conv, r_conv).then_inc(s_crc, 1)
            for m in range(8):
                j, cols = m // 2, slice((m % 2) * HT, (m % 2 + 1) * HT)
                dve.wait_ge(s_cbc, m + 1)
                stt(yc[:, j, cols], yc[:, j, cols], params[:, 16 + j:17 + j], bank[6 + m % 2][:, 0:HT], ALU.mult,
                    ALU.mult).then_inc(s_cf, 1)
            for c in range(NC):
                dve.wait_ge(s_su, c + 1)
                pb = bank[4 + c % 2]
                if c == 0:
                    nc.vector.tensor_copy(state[:, 0, :, :], pb[:, :].rearrange("p (h v) -> p h v", h=H)).then_inc(s_st, 1)
                else:
                    dve.wait_ge(s_st, c)
                    for h in range(H):
                        last = stt(state[:, c, h, :], state[:, c - 1, h, :], p_decay[:, h, c:c + 1], pb[:, h * P:(h + 1) * P],
                                   ALU.mult, ALU.add)
                    last.then_inc(s_st, 1)
                dve.wait_ge(s_ch, c + 1)
                tt_(xT[1][:, 4 + c, :], yc[:, c, :], f(xT[0][:, 4 + c, :]), ALU.subtract).then_inc(s_cl, 1)

            def o_lo(i):
                tt = i
                rows = P if tt < 4 else NS
                dve.wait_ge(s_oh_, i + 1)
                tt_(xT[1][:, 0:4, tok(tt)], o_bank(tt)[:, 0:4 * rows].rearrange("p (h t) -> p h t", h=H),
                    f(xT[0][:, 0:4, tok(tt)]), ALU.subtract).then_inc(s_ol, 1)

            dve.wait_ge(s_sg, 2)
            for i, tt in enumerate(range(NTT)):
                rows = P if tt < 4 else NS
                place = o_n[i % 2][0:rows, :]
                rr = root[0:rows, 4 * i:4 * i + 4]
                dve.wait_ge(s_osq, i + 1)
                nc.vector.tensor_reduce(ss[0:rows, 4 * i:4 * i + 4], o_sq[i % 2][0:rows, :].rearrange("p (h v) -> p h v", h=H),
                                        AX, ALU.add).then_inc(s_red, 1)
                if i >= 2:
                    dve.wait_ge(s_ot, i - 1)
                tt_(place, o_bank(tt)[0:rows, :], sg[0:rows, tt, :], ALU.mult).then_inc(s_dv, 1)
                chain[0] += 1
                if i:
                    o_lo(i - 1)
                dve.wait_ge(s_ort, i + 1)
                link(nc.vector.reciprocal(rr, rr))
                p3 = place.rearrange("p (h v) -> p h v", h=H)
                tt_(p3, p3, rr.unsqueeze(2).broadcast_to([rows, H, P]), ALU.mult).then_inc(s_on, 1)
            o_lo(NTT - 1)
            lo(NCH + 1)
            dve.wait_ge(s_xr, 32)

            def shift_scale(tt, std_sem=s_std, out_sem=s_nm):
                dve.wait_ge(std_sem, tt + 1)
                link(nc.vector.reciprocal(rt[:, tt:tt + 1], rt[:, tt:tt + 1]))
                stt(shift[:, tt:tt + 1], mv1[:, tt, 0:1], -1.0, rt[:, tt:tt + 1], ALU.mult, ALU.mult).then_inc(out_sem, 1)

            def ln_gain(tt):
                dve.wait_ge(s_nrm, tt + 1)
                tt_(xr[:, tt, :], xr[:, tt, :], ln[:, 0, :], ALU.mult).then_inc(s_xgn, 1)
                if tt >= POOL_LN:
                    dve.wait_ge(s_xgn, tt + 1)
                    tt_(xr[:, tt, :], xr[:, tt, :], ln[:, 1, :], ALU.add).then_inc(s_x1d, 1)

            for c in range(NWO):
                for tt in range(NTT):
                    n = c * NTT + tt
                    rows = P if tt < 4 else NS
                    dve.wait_ge(s_w, n + 1)
                    dst = xr[0:rows, tt, c * CW:(c + 1) * CW]
                    stt(dst, dst, ALPHA, w_bank(n)[0:rows, 0:CW], ALU.mult, ALU.add).then_inc(s_wc, 1)
                    if c % 2:
                        dve.wait_ge(s_wc, n + 1)
                        g = c // 2
                        nc.vector.bn_stats(stats[:, tt, 6 * g:6 * g + 6], xr[:, tt, 512 * g:512 * g + 512]).then_inc(s_dv, 1)
                        chain[0] += 1
                    if c == NWO - 1:
                        dve.wait_ge(s_dv, chain[0])
                        nc.vector.bn_aggr(mv1[:, tt, :], stats[:, tt, :]).then_inc(s_var, 1)
                        if tt >= 1:
                            shift_scale(tt - 1)
                        if tt == 2:
                            dve.wait_ge(s_lnp, 32)
                        if tt >= 2:
                            ln_gain(tt - 2)
                if c < 2:
                    lo(NCH + 2 + c)
                if c == 0:
                    dve.wait_ge(s_s0d, 1)
                if c < NWO - 1:
                    for h, g in ((c, 0), (c, 1)) if c < 2 else ((2, 0), (2, 1), (3, 0), (3, 1)):
                        dve.wait_ge(s_sus, 2 * h + g + 1)
                        sl = s0[:, 4 * g:4 * g + 4, h, :]
                        tt_(sl, sl, bank[1 + g][:, :].rearrange("p (b v) -> p b v", b=4), ALU.add).then_inc(s_s0n, 1)
            shift_scale(NTT - 1)
            ln_gain(NTT - 2)
            ln_gain(NTT - 1)

            bias_b = rt[:, 448:464].unsqueeze(1).broadcast_to([P, NTT, E])
            mx, s5 = rb(0, NTT), rb(8, NTT)
            pair, gs, gm, g1 = rb(16, 6 * 20), rb(136, 20), rb(156, NTT), rb(164, 20)
            pm, tmp, m1, m2 = rb(184, NE), rb(264, NE), rb(344, NTT), rb(352, NTT)
            rank, nb, ob, on_, big = rb(360, NE), rb(456, E), rb(472, E), rb(488, E), rb(504, NE)
            before = rb(720, NE + E)
            cnt = before[:, NE:NE + E]
            slot_f, tf, row = rb(584, 2 * NTT), rb(600, 16), rb(616, 2 * NTT)
            bc = lambda v, n: v.unsqueeze(2).broadcast_to([P, v.shape[1], n])
            dve.wait_ge(s_wr, 32)
            nc.vector.memset(r_l[:, 4 * E:NE], 0.0).then_inc(s_dv, 1)
            chain[0] += 1
            dve.wait_ge(s_lg, 1)
            dve.wait_ge(s_dv, chain[0])
            tt_(t3(r_l)[:, 0:4], bank[3][:, 0:4 * E].rearrange("p (t e) -> p t e", e=E), bias_b[:, 0:4], ALU.add)
            link(tt_(r_l[0:NS, 4 * E:NE], bank[3][0:NS, 4 * E:NE], rt[0:NS, 448:464], ALU.add))
            link(nc.vector.tensor_reduce(mx, t3(r_l), AX, ALU.max))
            tt_(t3(r_l), t3(r_l), bc(mx, E), ALU.subtract).then_inc(s_rl, 1)
            dve.wait_ge(s_re, 1)
            link(nc.vector.tensor_reduce(s5, t3(r_p), AX, ALU.add))
            link(nc.vector.reciprocal(s5, s5))
            link(tt_(t3(r_p), t3(r_p), bc(s5, E), ALU.mult))
            pv, p4 = pair.rearrange("p (g s) -> p g s", s=6), t4(r_p)
            n6 = 0
            for i in range(TOPG):
                for j in range(i + 1, TOPG):
                    last = tt_(pv[:, :, n6:n6 + 1], p4[:, :, i:i + 1], p4[:, :, j:j + 1], ALU.add)
                    n6 += 1
            link(last)
            g3 = lambda v: v.rearrange("p (t g) -> p t g", t=NTT)
            link(nc.vector.tensor_reduce(gs, pv, AX, ALU.max))
            link(nc.vector.tensor_reduce(gm, g3(gs), AX, ALU.max))

            def first_max(out, vals, mxv, order, n):
                link(tt_(out, vals, bc(mxv, n), ALU.is_equal))
                link(tt_(out, out, order.unsqueeze(1).broadcast_to([P, NTT, n]), ALU.mult))
                link(nc.vector.tensor_reduce(tf[:, 0:NTT], out, AX, ALU.max))
                link(tt_(out, out, bc(tf[:, 0:NTT], n), ALU.is_equal))

            first_max(g3(g1), g3(gs), gm, small[:, SM_G4:SM_G4 + TOPG], TOPG)
            gmask = g1.unsqueeze(2).broadcast_to([P, NTT * TOPG, TOPG])
            eo = small[:, SM_E16:SM_E16 + E]
            tt_(t4(tmp), p4, gmask, ALU.mult)
            link(ts_(t4(pm), gmask, 1.0, None, ALU.subtract))
            link(tt_(pm, pm, tmp, ALU.add))
            link(nc.vector.tensor_reduce(m1, t3(pm), AX, ALU.max))
            first_max(t3(r_o1), t3(pm), m1, eo, E)
            link(stt(pm, r_o1, -4.0, pm, ALU.mult, ALU.add))
            link(nc.vector.tensor_reduce(m2, t3(pm), AX, ALU.max))
            first_max(t3(r_o2), t3(pm), m2, eo, E)
            link(tt_(tf[:, 8:8 + NTT], m1, m2, ALU.add))
            link(nc.vector.reciprocal(tf[:, 8:8 + NTT], tf[:, 8:8 + NTT]))
            tt_(gw[:, 0:NTT], m1, tf[:, 8:8 + NTT], ALU.mult)
            link(tt_(gw[:, NTT:2 * NTT], m2, tf[:, 8:8 + NTT], ALU.mult))
            val = small[:, SM_VAL:SM_VAL + NTT].unsqueeze(2).broadcast_to([P, NTT, E])
            link(tt_(tmp, r_o1, r_o2, ALU.add))
            tt_(t3(choice), t3(tmp), val, ALU.mult).then_inc(s_oh, 1)
            nc.vector.memset(before[:, 0:E], 0.0)
            dve.wait_ge(s_rk, 1)
            link(nc.vector.tensor_copy(before[:, E:2 * E], bank[4][:, NE:NE + E]))
            for j in range(2, NTT + 1):
                link(tt_(before[:, j * E:(j + 1) * E], before[:, (j - 1) * E:j * E], bank[4][:, NE + (j - 1) * E:NE + j * E],
                         ALU.add))
            link(tt_(rank, bank[4][:, 0:NE], before[:, 0:NE], ALU.add))
            link(ts_(nb, cnt, float(P), None, ALU.is_gt))
            for j in range(2, NTT):
                link(stt(nb, cnt, float(P * j), nb, ALU.is_gt, ALU.add))
            link(nc.vector.tensor_tensor_scan(ob, ones[:, 0:E], nb, 0.0, ALU.mult, ALU.add))
            link(tt_(on_, ob, nb, ALU.subtract))
            link(ts_(on_, on_, float(P), float(E * P - P), ALU.mult, ALU.add))
            link(tt_(on_, on_, small[:, SM_BLK:SM_BLK + E], ALU.subtract))
            link(ts_(big, rank, float(P), None, ALU.is_ge))
            link(tt_(t3(big), t3(big), on_.unsqueeze(1).broadcast_to([P, NTT, E]), ALU.mult))
            link(tt_(rank, rank, big, ALU.add))
            link(tt_(t3(rank), t3(rank), small[:, SM_BLK:SM_BLK + E].unsqueeze(1).broadcast_to([P, NTT, E]), ALU.add))
            for n, oh in enumerate((r_o1, r_o2)):
                link(tt_(tmp, rank, oh, ALU.mult))
                link(nc.vector.tensor_reduce(slot_f[:, n * NTT:(n + 1) * NTT], t3(tmp), AX, ALU.add))
            n_sl = 2 * NTT
            first_slot = small[:, SM_BLK:SM_BLK + NBLK + 1].unsqueeze(1).broadcast_to([P, n_sl, NBLK + 1])
            link(tt_(from_blk, slot_f.unsqueeze(2).broadcast_to([P, n_sl, NBLK + 1]), first_slot, ALU.is_ge))
            tt_(in_blk, from_blk[:, :, 0:NBLK], from_blk[:, :, 1:NBLK + 1], ALU.subtract).then_inc(s_dv, 1)
            chain[0] += 1
            link(nc.vector.tensor_reduce(row, from_blk[:, :, 1:NBLK + 1], AX, ALU.add))
            link(stt(row, row, -float(P), slot_f, ALU.mult, ALU.add))
            tok_ids = small[:, SM_TOK:SM_TOK + NTT].unsqueeze(2).broadcast_to([P, NTT, NBLK])
            for n in range(2):
                tt_(in_blk[:, n * NTT:(n + 1) * NTT], in_blk[:, n * NTT:(n + 1) * NTT], tok_ids, ALU.mult)
                sl = slice(n * NTT, (n + 1) * NTT)
                tt_(row_hot[:, sl], const[:, C_IO:C_IO + P].unsqueeze(1).broadcast_to([P, NTT, P]),
                    row[:, sl].unsqueeze(2).broadcast_to([P, NTT, P]), ALU.is_equal).then_inc(s_hot, 1)
            nc.vector.tensor_copy(slot_i[:, :], slot_f).then_inc(s_slot, 1)
            dve.wait_ge(s_tab, 1)
            nc.vector.tensor_copy(ids[:, :], bank[5][:, 0:NBLK]).then_inc(s_ids, 1)
            link(nc.vector.tensor_copy(tf[:, 0:1], ob[:, E - 1:E]))
            for v in range(NOV):
                link(ts_(tmp[:, 0:E], ob, float(v), None, ALU.is_le))
                link(nc.vector.tensor_reduce(tf[:, 1 + v:2 + v], tmp[:, 0:E], AX, ALU.add))
            link(ts_(tf[:, 1:1 + NOV], tf[:, 1:1 + NOV], float(E - 1), None, ALU.min))
            nc.vector.tensor_copy(itab[:, 0:1 + NOV], tf[:, 0:1 + NOV]).then_inc(s_slot, 2)
            dve.wait_ge(s_slot, 3)

            def mlo(bi, j, s=None, i=0):
                place, _ = raw_place(count_of(bi if s is None else s, j) - 1, i)
                dve.wait_ge(m_hi, count_of(bi, j))
                sl = split[split_slot(bi, j)]
                tt_(sl[1], raw[place], f(sl[0]), ALU.subtract).then_inc(m_lo, 1)

            def x_lo(bi, par):
                for c in range(2):
                    dve.wait_ge(m_th, 2 * bi + c + 1)
                    tt_(xgT[par][1][:, 4 * c:4 * c + 4, :], bank[c][:, :].rearrange("p (k t) -> p k t", k=4),
                        f(xgT[par][0][:, 4 * c:4 * c + 4, :]), ALU.subtract).then_inc(m_tl, 1)

            def h_lo(bi):
                dve.wait_ge(m_hh, bi + 1)
                tt_(hT[1][:, :, :], bank[4][:, :].rearrange("p (k t) -> p k t", k=4), f(hT[0][:, :, :]),
                    ALU.subtract).then_inc(m_hl, 1)

            def y_half(bi, par):
                dve.wait_ge(m_use, down_count(bi))
                if not (isinstance(bi, int) and bi < 2):
                    dve.wait_ge(m_st[par], store_count(bi, par))
                nc.vector.tensor_copy(ysb[par][:, 512:D], bank[6][:, :]).then_inc(m_yd, 1)

            def hidden(bi):
                dve.wait_ge(m_use, up_count(bi))
                dve.wait_ge(m_sg, bi + 1)
                if not (isinstance(bi, int) and bi == 0):
                    dve.wait_ge(m_ht, bi)
                tt_(hbuf, silu_g, bank[3][:, :], ALU.mult).then_inc(m_h, 1)

            def step(bi, par, s=None, i=0):
                first, last = isinstance(bi, int) and bi == 0, isinstance(bi, int) and bi == E - 1
                after = None if s is None else s + 1
                if not first:
                    mlo(bi, 2, s, i)
                    h_lo(bi - 1)
                    mlo(bi, 3, s, i)
                if first:
                    mlo(1, 0)
                else:
                    mlo(bi, 4, s, i)
                mlo(bi, 5, s, i)
                if not last and not first:
                    mlo(bi + 1, 0, after, i)
                if last:
                    mlo(E, 2)
                if not first:
                    y_half(bi - 1, 1 - par)
                if not last:
                    x_lo(bi + 1, 1 - par)
                    mlo(bi + 1, 1, after, i)
                hidden(bi)

            x_lo(0, 0)
            dve.wait_ge(m_lo, 3)
            step(0, 0)
            step(1, 1)
            step(2, 0)
            with dve.Fori(0, (E - 4) // RING) as i:
                for s in range(3, 3 + RING):
                    step(RING * i + s, s % 2, s, i)
            step(E - 1, 1)
            mlo(E, 3)
            h_lo(E - 1)
            y_half(E - 1, 1)
            dve.wait_ge(s_slot, 3)
            n_over = dve.value_load(itab[0:1, 0:1], min_val=0, max_val=NOV)
            with dve.If(0 < n_over):
                with dve.Fori(0, NOV // RING) as i:
                    for r in range(RING):
                        v, par = RING * i + r, r % 2
                        with dve.If(v < n_over):
                            x_lo(E + v, par)
                            for s in range(6):
                                if s == 4:
                                    h_lo(E + v)
                                dve.wait_ge(m_hi, 6 * E + 6 * v + s + 1)
                                tt_(split[s % 3][1], raw[raw_place(6 * E + 6 * r + s)[0]], f(split[s % 3][0]), ALU.subtract).then_inc(m_lo, 1)
                                if s == 3:
                                    dve.wait_ge(m_ht, E + v)
                                    dve.wait_ge(m_use, 6 * E + 6 * v + 4)
                                    dve.wait_ge(m_sg, E + v + 1)
                                    tt_(hbuf, silu_g, bank[3][:, :], ALU.mult).then_inc(m_h, 1)
                            dve.wait_ge(m_use, 6 * E + 6 * v + 6)
                            dve.wait_ge(m_st[par], 16 * (E // 2 + r // 2) + 8 * RING * i)
                            nc.vector.tensor_copy(ysb[par][:, 512:D], bank[6][:, :]).then_inc(m_yd, 1)
            dve.wait_ge(s_ax, NTT)
            dve.wait_ge(s_lnp2, 32)

            def final_gain(tt):
                dve.wait_ge(s_fnr, tt + 1)
                ins = tt_(xr[:, tt, :], xr[:, tt, :], ln[:, 2, :], ALU.mult)
                if tt < NTT - 1:
                    ins.then_inc(s_fg, 1)
                else:
                    link(ins)
                    tt_(xr[:, tt, :], xr[:, tt, :], ln[:, 3, :], ALU.add).then_inc(s_y1, 1)

            for tt in range(NTT):
                rows = P if tt < 4 else NS
                dve.wait_ge(s_ga[tt], 32)
                for n, y in enumerate((y_a, y_b)):
                    g = gw[0:rows, n * NTT + tt:n * NTT + tt + 1]
                    link(stt(xr[0:rows, tt, :], y[0:rows, tt, :], g, xr[0:rows, tt, :], ALU.mult, ALU.add))
                for g in range(2):
                    nc.vector.bn_stats(stats[:, tt, 6 * g:6 * g + 6], xr[:, tt, 512 * g:512 * g + 512]).then_inc(s_dv, 1)
                chain[0] += 2
                dve.wait_ge(s_dv, chain[0])
                nc.vector.bn_aggr(mv1[:, tt, :], stats[:, tt, :]).then_inc(s_fvar, 1)
                if tt:
                    final_gain(tt - 1)
                shift_scale(tt, s_fstd, s_fnm)
            final_gain(NTT - 1)

        @block.tensor
        def _(pe):
            mm, tr = nc.tensor.matmul, nc.tensor.transpose
            pe.wait_ge(s_const, 16)
            for m in range(2 * NTT):
                tt, hf = m // 2, m % 2
                rows = P if tt < 4 else NS
                pe.wait_ge(s_x[tt], 16)
                if m >= 7:
                    pe.wait_ge(s_xl, m - 6)
                for j in range(4):
                    kt = 4 * hf + j
                    last = tr(bank[m % 7][:, j * rows:(j + 1) * rows], xn[0:rows, tt, kt * P:(kt + 1) * P],
                              ident[0:rows, 0:rows])
                last.then_inc(s_xt, 1)
            pe.wait_ge(s_par, 64)
            tr(bank[7][:, 0:84], sq[0:84, 0, 0:P], ident[0:84, 0:84]).then_inc(s_pt, 1)
            pe.wait_ge(s_xl, 2 * NTT)
            pe.wait_ge(s_pp, 1)

            def project(o):
                pe.wait_ge(s_lo, o + 1)
                wh, wl = chunk_weights(o % 2, 0), chunk_weights(o % 2, 1)
                for n in tiles_of(o):
                    kind, _, j = TILES[n]
                    if n >= 2:
                        wait_evacuated(pe, bank_before(n))
                    pb, ps = tile_banks(n)
                    if kind in TOKEN_MAJOR:
                        rows = P if j < 4 else NS
                        for kt in range(KT):
                            for i, (x_, w_) in enumerate(((0, wh), (0, wl), (1, wh))):
                                last = mm(pb[0:rows, 0:CW], xT[x_][:, kt, tok(j)], w_[:, kt, :],
                                          start=(kt == 0 and i == 0), stop=(kt == KT - 1 and i == 2))
                    else:
                        for kt in range(KT):
                            for i, (w_, x_) in enumerate(((wh, 0), (wh, 1), (wl, 0))):
                                first, end = kt == 0 and i == 0, kt == KT - 1 and i == 2
                                lhs = w_[:, kt, j * P:(j + 1) * P]
                                mm(pb[:, 0:HT], lhs, xT[x_][:, kt, 0:HT], start=first, stop=end)
                                last = mm(ps[:, 0:HT], lhs, xT[x_][:, kt, HT:T], start=first, stop=end)
                    last.then_inc(s_tile, 1)
                    if o == NCH - 1 and j:
                        spread(2 * j - 2)
                        spread(2 * j - 1)

            def spread(m):
                if m == 0:
                    pe.wait_ge(s_crc, 1)
                if m >= 2:
                    pe.wait_ge(s_cf, m - 1)
                mm(bank[6 + m % 2][:, 0:HT], groups_t[:, m // 2, :], r_conv[:, (m % 2) * HT:(m % 2 + 1) * HT],
                   start=True, stop=True).then_inc(s_cbc, 1)

            def pairs(li):
                if li == 0:
                    pe.wait_ge(s_eva, 8)
                else:
                    pe.wait_ge(s_z, li)
                lf, rf = (k, q) if li == 0 else (ex[(li - 1) % 2], ex[(li - 1) % 2])
                if li <= SLEVELS:
                    if li:
                        pe.wait_ge(s_ps, li)
                    for h in range(H):
                        last = mm(bank[7][0:NS, h * NS:(h + 1) * NS], lf[:, h, SEQ:T], rf[:, h, SEQ:T], start=True, stop=True)
                for h in range(H):
                    p = li * H + h
                    if p >= 3:
                        pe.wait_ge(s_pc, p - 2)
                    for c in range(NC):
                        cols = slice(c * P, (c + 1) * P)
                        last = mm(bank[4 + p % 3][:, cols], lf[:, h, cols], rf[:, h, cols], start=True, stop=True)
                    last.then_inc(s_p, 1)

            for o_ in range(NCH):
                project(o_)
                li = o_ - FIRST_LEVEL_STEP + 1
                if 0 <= li <= LEVELS:
                    pairs(li)

                if o_ == 7:
                    pe.wait_ge(s_ps, SLEVELS + 1)
                    for j in range(4):
                        last = tr(bank[7][0:8, j * P:(j + 1) * P], groups[:, j, :], ident)
                    last.then_inc(s_selt, 1)
                if o_ == 11:
                    pe.wait_ge(s_cb, 4)
                    pe.wait_ge(s_sel, 1)
                    for j in range(4):
                        last = tr(bank[7][0:18, j * P:(j + 1) * P], cb[:, j, :], ident)
                    last.then_inc(s_cbt, 1)
                if o_ == 12:
                    pe.wait_ge(s_kx, 1)
                    for m in range(H + 1):
                        if m >= 2:
                            pe.wait_ge(s_ktc, m - 1)
                        if m < H:
                            for c in range(NC):
                                last = tr(bank[4 + m % 2][:, c * P:(c + 1) * P], k[:, m, c * P:(c + 1) * P], ident)
                        else:
                            for h in range(H):
                                last = tr(bank[4][0:NS, h * P:(h + 1) * P], k[:, h, SEQ:T], ident)
                        last.then_inc(s_kt, 1)
                    pe.wait_ge(s_csq, 1)
                    pe.wait_ge(s_cbo, 1)
                    pe.wait_ge(s_pc, NP_LEVELS)
                    for g in range(2):
                        for j in range(4):
                            last = mm(bank[6 + g][0:8, 0:HT], groups[:, j, :], sq[:, j, g * HT:(g + 1) * HT],
                                      start=(j == 0), stop=(j == 3))
                        last.then_inc(s_cms, 1)
            wait_evacuated(pe, len(TILES) - 1)
            pe.wait_ge(s_ktc, H + 1)
            pe.wait_ge(s_qx, 1)

            def update(c):
                if c >= 2:
                    pe.wait_ge(s_st, c - 1)
                for h in range(H):
                    last = mm(bank[4 + c % 2][:, h * P:(h + 1) * P], k_tok[:, h, c, :], v_tok[:, c, h * P:(h + 1) * P],
                              start=True, stop=True)
                last.then_inc(s_su, 1)

            def prompt_o(c):
                cols = slice(c * P, (c + 1) * P)
                if c:
                    pe.wait_ge(s_st, c)
                for h in range(H):
                    vh = slice(h * P, (h + 1) * P)
                    last = mm(bank[c][:, vh], att[:, h, c, :], v_tok[:, c, vh], start=True, stop=(c == 0))
                    if c:
                        last = mm(bank[c][:, vh], q[:, h, cols], state[:, c - 1, h, :], start=False, stop=True)
                last.then_inc(s_o, 1)

            update(0)
            update(1)
            prompt_o(0)
            prompt_o(1)
            update(2)
            update(3)
            prompt_o(2)
            prompt_o(3)
            pe.wait_ge(s_cf, 8)
            pe.wait_ge(s_s0, 16)
            pe.wait_ge(s_qm, 1)

            def turn_o(i):
                rows = P if i < 4 else NS
                pe.wait_ge(s_on, i + 1)
                for h in range(H):
                    last = tr(o_bank(i)[:, h * rows:(h + 1) * rows], o_n[i % 2][0:rows, h * P:(h + 1) * P],
                              ident[0:rows, 0:rows])
                last.then_inc(s_ot, 1)

            for h in range(H):
                vh = slice(h * P, (h + 1) * P)
                mm(bank[6][0:NS, vh], att_s[0:NS, h, :], v_tok[0:NS, 4, vh], start=True, stop=False)
                for bi in range(DB):
                    last = mm(bank[6][0:NS, vh], q_msk[:, h, bi, :], s0[:, bi, h, :], start=False, stop=(bi == DB - 1))
                if h == H - 1:
                    last.then_inc(s_o, 1)
                turn_o(h)
            pe.wait_ge(s_cl, 4)
            pe.wait_ge(s_st, NC)
            for c in range(NWO):
                pe.wait_ge(s_lo, NCH + c + 1)
                wh, wl = chunk_weights((NCH + c) % 2, 0), chunk_weights((NCH + c) % 2, 1)
                for tt in range(NTT):
                    n = c * NTT + tt
                    rows = P if tt < 4 else NS
                    if c == 0:
                        pe.wait_ge(s_ol, tt + 1)
                    if n >= 4:
                        pe.wait_ge(s_wc, n - 3)
                    for kt in range(KT):
                        for i, (x_, w_) in enumerate(((0, wh), (0, wl), (1, wh))):
                            last = mm(w_bank(n)[0:rows, 0:CW], xT[x_][:, kt, tok(tt)], w_[:, kt, :],
                                      start=(kt == 0 and i == 0), stop=(kt == KT - 1 and i == 2))
                    last.then_inc(s_w, 1)
                    if n == 0:
                        turn_o(NTT - 1)
                if c < NWO - 1:
                    for h, g in ((c, 0), (c, 1)) if c < 2 else ((2, 0), (2, 1), (3, 0), (3, 1)):
                        pe.wait_ge(s_vm, h + 1)
                        if h:
                            pe.wait_ge(s_s0n, 2 * h + g - 1)
                        mm(bank[1 + g][:, :], k_tok_s[0:NS, h, :], v_msk[0:NS, 4 * g:4 * g + 4, :],
                           start=True, stop=True).then_inc(s_sus, 1)
            def logits(g):
                t0, t1 = 2 * g * P, min((2 * g + 2) * P, T)
                pe.wait_ge(s_1c, min(4 * g + 4, 2 * NTT))
                pb = bank[5 + g][0:E, 0:t1 - t0]
                for kt in range(KT):
                    last = mm(pb, wr[:, kt, :], x1T[g][:, kt, :], start=(kt == 0), stop=(kt == KT - 1))
                last.then_inc(s_lgt, 1)

            pe.wait_ge(s_s0n, 2 * H)
            pe.wait_ge(s_wr, 32)
            for tt in range(NTT):
                if tt < POOL_LN:
                    pe.wait_ge(s_x1, tt + 1)
                else:
                    pe.wait_ge(s_x1d, tt - POOL_LN + 1)
                rows = P if tt < 4 else NS
                for hf in range(2):
                    m = 2 * tt + hf
                    if m == 2:
                        pe.wait_ge(s_wc, NWO * NTT)
                    if m >= 4:
                        pe.wait_ge(s_1c, m - 3)
                    for j in range(4):
                        kt = 4 * hf + j
                        last = tr(bank[1 + m % 4][:, j * rows:(j + 1) * rows], xr[0:rows, tt, kt * P:(kt + 1) * P],
                                  ident[0:rows, 0:rows])
                    last.then_inc(s_1t, 1)
                if tt in (2, 4):
                    logits(tt // 2 - 1)
            logits(2)
            pe.wait_ge(s_lgs, 1)
            for tt in range(NTT):
                rows = P if tt < 4 else NS
                last = tr(bank[3][0:rows, tt * E:(tt + 1) * E], lg[:, tok(tt)], ident[0:E, 0:E])
            last.then_inc(s_lg, 1)
            pe.wait_ge(s_oh, 1)
            mm(bank[4][:, 0:NE], tri, choice, start=True, stop=True)
            mm(bank[4][:, NE:2 * NE], ones, choice, start=True, stop=True).then_inc(s_rk, 1)

            for n in range(2):
                pe.wait_ge(s_hot, n + 1)
                for tt in range(NTT):
                    rows, i = P if tt < 4 else NS, n * NTT + tt
                    last = mm(bank[5][:, 0:NBLK], row_hot[0:rows, i, :], in_blk[0:rows, i, :], start=(i == 0),
                              stop=(i == 2 * NTT - 1))
            last.then_inc(s_tab, 1)

            def x_turn(bi, par):
                pe.wait_ge(m_xg[par], 8 * (bi - par) + 16)
                if not (isinstance(bi, int) and bi == 0):
                    pe.wait_ge(m_tl, 2 * bi)
                for c in range(2):
                    for t in range(4):
                        last = tr(bank[c][:, t * P:(t + 1) * P], xg[par][:, c * 512 + t:(c + 1) * 512:4], ident)
                last.then_inc(m_t, 1)

            def gate_up(out, par, slot, c, wait):
                pe.wait_ge(m_lo, wait)
                w = [split[slot][i].rearrange("p (t n) -> p t n", t=4) for i in range(2)]
                for t in range(4):
                    kt = 4 * c + t
                    for i, (x_, w_) in enumerate(((0, 0), (0, 1), (1, 0))):
                        last = mm(out[:, :], xgT[par][x_][:, kt, :], w[w_][:, t, :],
                                  start=(kt == 0 and i == 0), stop=(kt == KT - 1 and i == 2))
                last.then_inc(m_use, 1)

            def down(slot, c, wait):
                pe.wait_ge(m_lo, wait)
                w = [split[slot][i].rearrange("p (t n) -> p t n", t=2) for i in range(2)]
                for t in range(2):
                    kt = 2 * c + t
                    for i, (x_, w_) in enumerate(((0, 0), (0, 1), (1, 0))):
                        for g in range(2):
                            last = mm(bank[5 + g][:, :], hT[x_][:, kt, :], w[w_][:, t, 512 * g:512 * g + 512],
                                      start=(kt == 0 and i == 0), stop=(kt == 3 and i == 2))
                last.then_inc(m_use, 1)

            def h_turn(bi):
                pe.wait_ge(m_h, bi + 1)
                if not (isinstance(bi, int) and bi == 0):
                    pe.wait_ge(m_hl, bi)
                for kt in range(4):
                    c, t = kt // 2, kt % 2
                    last = tr(bank[4][:, kt * P:(kt + 1) * P], hbuf[:, c * 256 + t:(c + 1) * 256:2], ident)
                last.then_inc(m_ht, 1)

            def down_ready(bi):
                pe.wait_ge(m_hl, bi + 1)
                if not (isinstance(bi, int) and bi == 0):
                    pe.wait_ge(m_ya, bi)
                    pe.wait_ge(m_yd, bi)

            def step(bi, par):
                first, last = isinstance(bi, int) and bi == 0, isinstance(bi, int) and bi == E - 1
                pe.wait_ge(m_tl, 2 * bi + 2)
                if not first:
                    pe.wait_ge(m_sg, bi)
                gate_up(bank[2], par, 0, 0, count_of(bi, 0))
                if not first:
                    h_turn(bi - 1)
                gate_up(bank[2], par, 1, 1, count_of(bi, 1))
                if not first:
                    down_ready(bi - 1)
                    down(2, 0, count_of(bi, 2))
                    down(0, 1, count_of(bi, 3))
                if not last:
                    x_turn(bi + 1, 1 - par)
                gate_up(bank[3], par, split_slot(bi, 4), 0, count_of(bi, 4))
                gate_up(bank[3], par, split_slot(bi, 5), 1, count_of(bi, 5))

            x_turn(0, 0)
            step(0, 0)
            step(1, 1)
            step(2, 0)
            with pe.Fori(0, (E - 4) // 2) as i:
                step(2 * i + 3, 1)
                step(2 * i + 4, 0)
            step(E - 1, 1)
            h_turn(E - 1)
            down_ready(E - 1)
            down(split_slot(E, 2), 0, count_of(E, 2))
            down(split_slot(E, 3), 1, count_of(E, 3))
            pe.wait_ge(s_slot, 3)
            n_over = pe.value_load(itab[0:1, 0:1], min_val=0, max_val=NOV)
            with pe.If(0 < n_over):
                with pe.Fori(0, NOV // 2) as i:
                    for par in range(2):
                        v = 2 * i + par
                        with pe.If(v < n_over):
                            base = 6 * E + 6 * v
                            x_turn(E + v, par)
                            pe.wait_ge(m_tl, 2 * (E + v) + 2)
                            pe.wait_ge(m_sg, E + v)
                            gate_up(bank[2], par, 0, 0, base + 1)
                            gate_up(bank[2], par, 1, 1, base + 2)
                            gate_up(bank[3], par, 2, 0, base + 3)
                            gate_up(bank[3], par, 0, 1, base + 4)
                            h_turn(E + v)
                            down_ready(E + v)
                            down(1, 0, base + 5)
                            down(2, 1, base + 6)


_INS = ["x_prompt", "x_sample", "state_hgrn", "state_conv", "w_in", "w_out", "hgrn_norm_g", "conv_w", "conv_norm_g",
        "ln1_g", "ln1_b", "ln2_g", "ln2_b", "w_router", "router_bias", "w_gate", "w_up", "w_down"]
_OUTS = [("out_prompt", (1, SEQ, D)), ("out_sample", (DB, DS, D)), ("out_hgrn_prompt", (1, 1, H, P, P)),
         ("out_conv_prompt", (1, 1, 2, 512)), ("out_hgrn_sample", (1, DB, H, P, P)), ("out_conv_sample", (1, DB, 2, 512))]


def kernel(**inputs):
    import concourse.bacc as bacc
    from concourse.bass_utils import run_bass_kernel_spmd

    nc = bacc.Bacc("TRN2", target_bir_lowering=False, num_devices=1)
    const_f32, const_mask = constants()
    arrays = {name: np.ascontiguousarray(inputs[name]) for name in _INS}
    arrays["const_f32"], arrays["const_mask"] = const_f32, const_mask
    aps = {name: nc.dram_tensor(name, x.shape, mybir.dt.from_np(x.dtype), kind="ExternalInput").ap()
           for name, x in arrays.items()}
    for name, shape in _OUTS:
        aps[name] = nc.dram_tensor(name, shape, F32, kind="ExternalOutput").ap()
    build(nc, aps)
    r = run_bass_kernel_spmd(nc, [arrays], core_ids=[0])
    return tuple(r.results[0][name] for name, _ in _OUTS)
```
